# Optimizing a Trainium2 kernel written in Bass

```python
import numpy as np
import jax
import jax.numpy as jnp
from jax import lax

D_MODEL = 1024
BATCH = 1
SEQ = 512
DEPTH = 2
DEC_BATCH = 8
DEC_SEQ = 4
PAST_LEN = 4096
PAGE_SIZE = 128

GDN_HEADS = 4
GDN_DK = 128
GDN_DV = 128
GLA_HEADS = 4
GLA_DK = 64
GLA_DV = 128
GLA_GATE_RANK = 16
GLA_GATE_NORMALIZER = 16.0
SSD_HEADS = 8
SSD_HEADDIM = 64
SSD_GROUPS = 2
SSD_DSTATE = 128
CONV_WIDTH = 4
CHUNK = 64
D_FF = 2816
N_BRANCHES = 3
NORM_EPS = 1e-6

GDN_QK = GDN_HEADS * GDN_DK
GDN_V = GDN_HEADS * GDN_DV
GDN_CONV_DIM = 2 * GDN_QK + GDN_V
GLA_QK = GLA_HEADS * GLA_DK
GLA_V = GLA_HEADS * GLA_DV
SSD_INNER = SSD_HEADS * SSD_HEADDIM
SSD_BC = SSD_GROUPS * SSD_DSTATE
SSD_CONV_DIM = SSD_INNER + 2 * SSD_BC
IN_SIZES = (GDN_CONV_DIM, GDN_V, GDN_HEADS, GDN_HEADS,
            GLA_QK, GLA_QK, GLA_V, GLA_V, GLA_GATE_RANK,
            SSD_INNER, SSD_CONV_DIM, SSD_HEADS,
            N_BRANCHES * D_MODEL)
D_IN = sum(IN_SIZES)

kernel_name = 'hybrid_gdn_gla_ssd_macaron_step'

def _rmsnorm(x, w):
    xf = x.astype(jnp.float32)
    y = xf * lax.rsqrt(jnp.mean(xf * xf, axis=-1, keepdims=True) + NORM_EPS)
    return (y * w.astype(jnp.float32)).astype(x.dtype)

def _l2norm(x):
    xf = x.astype(jnp.float32)
    return xf * lax.rsqrt(jnp.sum(xf * xf, axis=-1, keepdims=True) + NORM_EPS)

def _swiglu(x, w_gate, w_up, w_down):
    return (jax.nn.silu(x @ w_gate) * (x @ w_up)) @ w_down

def _causal_conv(x, buf, w, b=None):
    T = x.shape[1]
    xp = jnp.concatenate([buf.astype(x.dtype), x], axis=1)
    y = xp[:, 0:T] * w[:, 0]
    for i in range(1, CONV_WIDTH):
        y = y + xp[:, i:i + T] * w[:, i]
    if b is not None:
        y = y + b
    return jax.nn.silu(y), xp[:, T:]

def _chunked(x, L):
    Bsz, H, T = x.shape[:3]
    n = -(-T // L)
    x = jnp.pad(x, [(0, 0), (0, 0), (0, n * L - T)] + [(0, 0)] * (x.ndim - 3))
    x = x.reshape((Bsz, H, n, L) + x.shape[3:])
    return jnp.moveaxis(x, 2, 0)

def _unchunk(y, T):
    y = jnp.moveaxis(y, 0, 2)
    y = y.reshape(y.shape[:2] + (-1,) + y.shape[4:])[:, :, :T]
    return jnp.moveaxis(y, 1, 2)

def _heads_first(*arrs):
    return tuple(jnp.moveaxis(a, 2, 1) for a in arrs)

def _segment_decay(G, mask):
    diff = G[..., :, None] - G[..., None, :]
    return jnp.where(mask, jnp.exp(jnp.where(mask, diff, 0.0)), 0.0)

def _gated_delta_rule(q, k, v, g, beta, S0):
    T = q.shape[1]
    L = min(CHUNK, T)
    xs = tuple(_chunked(a, L) for a in _heads_first(q, k, v, g, beta))
    causal = jnp.tril(jnp.ones((L, L), dtype=bool))
    strict = jnp.tril(jnp.ones((L, L), dtype=bool), -1)
    eye = jnp.eye(L, dtype=jnp.float32)

    def step(S, inp):
        qc, kc, vc, gc, bc = inp
        G = jnp.cumsum(gc, axis=-1)
        dec = _segment_decay(G, causal)
        A = jnp.where(strict, bc[..., :, None] * jnp.einsum('bhid,bhjd->bhij', kc, kc) * dec, 0.0)
        rhs = jnp.concatenate([bc[..., None] * vc, (bc * jnp.exp(G))[..., None] * kc], axis=-1)
        sol = lax.linalg.triangular_solve(eye + A, rhs, left_side=True, lower=True)
        u = sol[..., :GDN_DV] - jnp.einsum('bhik,bhkv->bhiv', sol[..., GDN_DV:], S)
        o = (jnp.einsum('bhik,bhkv->bhiv', qc * jnp.exp(G)[..., None], S)
             + jnp.einsum('bhij,bhjv->bhiv', jnp.einsum('bhid,bhjd->bhij', qc, kc) * dec, u))
        G_last = G[..., -1:]
        S = (jnp.exp(G_last)[..., None] * S
             + jnp.einsum('bhjk,bhjv->bhkv', kc * jnp.exp(G_last - G)[..., None], u))
        return S, o

    S, o = lax.scan(step, S0, xs)
    return _unchunk(o, T), S

def _gla(q, k, v, gk, S0):
    T = q.shape[1]
    L = min(CHUNK, T)
    xs = tuple(_chunked(a, L) for a in _heads_first(q, k, v, gk))
    causal = jnp.tril(jnp.ones((L, L), dtype=bool))[:, :, None]

    def step(S, inp):
        qc, kc, vc, gc = inp
        Bc = jnp.cumsum(gc, axis=2)
        diff = Bc[:, :, :, None, :] - Bc[:, :, None, :, :]
        dec = jnp.where(causal, jnp.exp(jnp.where(causal, diff, 0.0)), 0.0)
        att = jnp.sum(qc[:, :, :, None, :] * kc[:, :, None, :, :] * dec, axis=-1)
        o = (jnp.einsum('bhik,bhkv->bhiv', qc * jnp.exp(Bc), S)
             + jnp.einsum('bhij,bhjv->bhiv', att, vc))
        B_last = Bc[:, :, -1:, :]
        S = (jnp.exp(B_last[:, :, 0, :])[..., None] * S
             + jnp.einsum('bhjk,bhjv->bhkv', kc * jnp.exp(B_last - Bc), vc))
        return S, o

    S, o = lax.scan(step, S0, xs)
    return _unchunk(o, T), S

def _ssd(x, dt, a, Bm, Cm, S0):
    T = x.shape[1]
    L = min(CHUNK, T)
    xs = tuple(_chunked(t, L) for t in _heads_first(x, dt, a, Bm, Cm))
    causal = jnp.tril(jnp.ones((L, L), dtype=bool))

    def step(S, inp):
        xc, dtc, ac, bc, cc = inp
        A = jnp.cumsum(ac, axis=-1)
        dec = _segment_decay(A, causal)
        xdt = xc * dtc[..., None]
        att = jnp.einsum('bhin,bhjn->bhij', cc, bc) * dec
        y = (jnp.einsum('bhij,bhjp->bhip', att, xdt)
             + jnp.einsum('bhin,bhpn->bhip', cc * jnp.exp(A)[..., None], S))
        A_last = A[..., -1:]
        S = (jnp.exp(A_last)[..., None] * S
             + jnp.einsum('bhjp,bhjn->bhpn', xdt * jnp.exp(A_last - A)[..., None], bc))
        return S, y

    S, y = lax.scan(step, S0, xs)
    return _unchunk(y, T), S

def _token_mixer(h, conv_gdn, s_gdn, s_gla, conv_ssd, s_ssd, p):
    f32 = jnp.float32
    Bsz, T, _ = h.shape
    proj = h @ p['w_in']
    (gdn_qkv, gdn_z, gdn_a, gdn_b, gla_q, gla_k, gla_v, gla_g, gla_r,
     ssd_z, ssd_xbc, ssd_dt, gate_logits) = jnp.split(
        proj, np.cumsum(IN_SIZES)[:-1].tolist(), axis=-1)

    qkv, conv_gdn_new = _causal_conv(gdn_qkv, conv_gdn, p['gdn_conv_w'])
    q, k, v = jnp.split(qkv, [GDN_QK, 2 * GDN_QK], axis=-1)
    q = _l2norm(q.reshape(Bsz, T, GDN_HEADS, GDN_DK)) * (GDN_DK ** -0.5)
    k = _l2norm(k.reshape(Bsz, T, GDN_HEADS, GDN_DK))
    v = v.reshape(Bsz, T, GDN_HEADS, GDN_DV).astype(f32)
    beta = jax.nn.sigmoid(gdn_b.astype(f32))
    g = -jnp.exp(p['gdn_A_log'].astype(f32)) * jax.nn.softplus(gdn_a.astype(f32) + p['gdn_dt_bias'].astype(f32))
    o, s_gdn_new = _gated_delta_rule(q, k, v, g, beta, s_gdn.astype(f32))
    o = _rmsnorm(o, p['gdn_norm']) * jax.nn.silu(gdn_z.reshape(Bsz, T, GDN_HEADS, GDN_DV).astype(f32))
    o_gdn = o.reshape(Bsz, T, GDN_V).astype(h.dtype)

    gk = jax.nn.log_sigmoid((gla_r @ p['gla_gate_up'] + p['gla_gate_bias']).astype(f32)) / GLA_GATE_NORMALIZER
    o, s_gla_new = _gla(gla_q.reshape(Bsz, T, GLA_HEADS, GLA_DK).astype(f32) * (GLA_DK ** -0.5),
                        gla_k.reshape(Bsz, T, GLA_HEADS, GLA_DK).astype(f32),
                        gla_v.reshape(Bsz, T, GLA_HEADS, GLA_DV).astype(f32),
                        gk.reshape(Bsz, T, GLA_HEADS, GLA_DK),
                        s_gla.astype(f32))
    o = _rmsnorm(o, p['gla_norm']) * jax.nn.silu(gla_g.reshape(Bsz, T, GLA_HEADS, GLA_DV).astype(f32))
    o_gla = o.reshape(Bsz, T, GLA_V).astype(h.dtype)

    xbc, conv_ssd_new = _causal_conv(ssd_xbc, conv_ssd, p['ssd_conv_w'], p['ssd_conv_b'])
    xs, Bm, Cm = jnp.split(xbc.astype(f32), [SSD_INNER, SSD_INNER + SSD_BC], axis=-1)
    xs = xs.reshape(Bsz, T, SSD_HEADS, SSD_HEADDIM)
    rep = SSD_HEADS // SSD_GROUPS
    Bm = jnp.repeat(Bm.reshape(Bsz, T, SSD_GROUPS, SSD_DSTATE), rep, axis=2)
    Cm = jnp.repeat(Cm.reshape(Bsz, T, SSD_GROUPS, SSD_DSTATE), rep, axis=2)
    dt = jax.nn.softplus(ssd_dt.astype(f32) + p['ssd_dt_bias'].astype(f32))
    a = -jnp.exp(p['ssd_A_log'].astype(f32)) * dt
    y, s_ssd_new = _ssd(xs, dt, a, Bm, Cm, s_ssd.astype(f32))
    y = y + p['ssd_D'].astype(f32)[:, None] * xs
    y = y.reshape(Bsz, T, SSD_INNER) * jax.nn.silu(ssd_z.astype(f32))
    y = _rmsnorm(y.reshape(Bsz, T, SSD_GROUPS, SSD_INNER // SSD_GROUPS),
                 p['ssd_norm'].reshape(SSD_GROUPS, SSD_INNER // SSD_GROUPS))
    o_ssd = y.reshape(Bsz, T, SSD_INNER).astype(h.dtype)

    gates = jax.nn.sigmoid(gate_logits.reshape(Bsz, T, N_BRANCHES, D_MODEL) + p['b_merge'])
    merged = (gates[:, :, 0] * (o_gdn @ p['w_br_gdn'])
              + gates[:, :, 1] * (o_gla @ p['w_br_gla'])
              + gates[:, :, 2] * (o_ssd @ p['w_br_ssd']))
    out = merged @ p['w_out']
    return out, (conv_gdn_new, s_gdn_new, s_gla_new, conv_ssd_new, s_ssd_new)

def _layer(x, state, p):
    f = _swiglu(_rmsnorm(x, p['ffn1_norm_pre']), p['ffn1_w_gate'], p['ffn1_w_up'], p['ffn1_w_down'])
    x = x + (0.5 * _rmsnorm(f, p['ffn1_norm_post'])).astype(x.dtype)
    m, new_state = _token_mixer(_rmsnorm(x, p['mix_norm_pre']), *state, p)
    x = x + _rmsnorm(m, p['mix_norm_post']).astype(x.dtype)
    f = _swiglu(_rmsnorm(x, p['ffn2_norm_pre']), p['ffn2_w_gate'], p['ffn2_w_up'], p['ffn2_w_down'])
    x = x + (0.5 * _rmsnorm(f, p['ffn2_norm_post'])).astype(x.dtype)
    return x, new_state

def setup_inputs(seed: int = 0) -> dict:
    key = jax.random.key(seed)
    ks = iter(jax.random.split(key, 64))
    f32 = jnp.float32

    def nrm(shape, scale):
        return scale * jax.random.normal(next(ks), shape, f32)

    def gain(shape):
        return 1.0 + nrm(shape, 0.02)

    def a_log(h):
        return jnp.log(jax.random.uniform(next(ks), (DEPTH, h), f32, 1.0, 16.0))

    def dt_bias(h):
        dt = jnp.exp(jax.random.uniform(next(ks), (DEPTH, h), f32, float(np.log(1e-3)), float(np.log(1e-1))))
        return jnp.log(jnp.expm1(dt))

    inp = {
        'x_prompt': nrm((BATCH, SEQ, D_MODEL), 1.0),
        'x_sample': nrm((DEC_BATCH, DEC_SEQ, D_MODEL), 1.0),
        'state_gdn_conv': nrm((DEPTH, DEC_BATCH, CONV_WIDTH - 1, GDN_CONV_DIM), 1.0),
        'state_gdn': nrm((DEPTH, DEC_BATCH, GDN_HEADS, GDN_DK, GDN_DV), 0.3),
        'state_gla': nrm((DEPTH, DEC_BATCH, GLA_HEADS, GLA_DK, GLA_DV), 1.0),
        'state_ssd_conv': nrm((DEPTH, DEC_BATCH, CONV_WIDTH - 1, SSD_CONV_DIM), 1.0),
        'state_ssd': nrm((DEPTH, DEC_BATCH, SSD_HEADS, SSD_HEADDIM, SSD_DSTATE), 0.3),
        'ffn1_norm_pre': gain((DEPTH, D_MODEL)),
        'ffn1_norm_post': gain((DEPTH, D_MODEL)),
        'ffn1_w_gate': nrm((DEPTH, D_MODEL, D_FF), D_MODEL ** -0.5),
        'ffn1_w_up': nrm((DEPTH, D_MODEL, D_FF), D_MODEL ** -0.5),
        'ffn1_w_down': nrm((DEPTH, D_FF, D_MODEL), D_FF ** -0.5),
        'mix_norm_pre': gain((DEPTH, D_MODEL)),
        'mix_norm_post': gain((DEPTH, D_MODEL)),
        'w_in': nrm((DEPTH, D_MODEL, D_IN), D_MODEL ** -0.5),
        'b_merge': nrm((DEPTH, N_BRANCHES, D_MODEL), 0.02),
        'gdn_conv_w': nrm((DEPTH, GDN_CONV_DIM, CONV_WIDTH), CONV_WIDTH ** -0.5),
        'gdn_A_log': a_log(GDN_HEADS),
        'gdn_dt_bias': dt_bias(GDN_HEADS),
        'gdn_norm': gain((DEPTH, GDN_DV)),
        'gla_gate_up': nrm((DEPTH, GLA_GATE_RANK, GLA_QK), GLA_GATE_RANK ** -0.5),
        'gla_gate_bias': nrm((DEPTH, GLA_QK), 0.1),
        'gla_norm': gain((DEPTH, GLA_DV)),
        'ssd_conv_w': nrm((DEPTH, SSD_CONV_DIM, CONV_WIDTH), CONV_WIDTH ** -0.5),
        'ssd_conv_b': nrm((DEPTH, SSD_CONV_DIM), 0.02),
        'ssd_A_log': a_log(SSD_HEADS),
        'ssd_dt_bias': dt_bias(SSD_HEADS),
        'ssd_D': gain((DEPTH, SSD_HEADS)),
        'ssd_norm': gain((DEPTH, SSD_INNER)),
        'w_br_gdn': nrm((DEPTH, GDN_V, D_MODEL), GDN_V ** -0.5),
        'w_br_gla': nrm((DEPTH, GLA_V, D_MODEL), GLA_V ** -0.5),
        'w_br_ssd': nrm((DEPTH, SSD_INNER, D_MODEL), SSD_INNER ** -0.5),
        'w_out': nrm((DEPTH, D_MODEL, D_MODEL), D_MODEL ** -0.5),
        'ffn2_norm_pre': gain((DEPTH, D_MODEL)),
        'ffn2_norm_post': gain((DEPTH, D_MODEL)),
        'ffn2_w_gate': nrm((DEPTH, D_MODEL, D_FF), D_MODEL ** -0.5),
        'ffn2_w_up': nrm((DEPTH, D_MODEL, D_FF), D_MODEL ** -0.5),
        'ffn2_w_down': nrm((DEPTH, D_FF, D_MODEL), D_FF ** -0.5),
    }
    return inp

def reference(x_prompt, x_sample, state_gdn_conv, state_gdn, state_gla, state_ssd_conv, state_ssd,
              ffn1_norm_pre, ffn1_norm_post, ffn1_w_gate, ffn1_w_up, ffn1_w_down,
              mix_norm_pre, mix_norm_post, w_in, b_merge,
              gdn_conv_w, gdn_A_log, gdn_dt_bias, gdn_norm,
              gla_gate_up, gla_gate_bias, gla_norm,
              ssd_conv_w, ssd_conv_b, ssd_A_log, ssd_dt_bias, ssd_D, ssd_norm,
              w_br_gdn, w_br_gla, w_br_ssd, w_out,
              ffn2_norm_pre, ffn2_norm_post, ffn2_w_gate, ffn2_w_up, ffn2_w_down):
    params = dict(
        ffn1_norm_pre=ffn1_norm_pre, ffn1_norm_post=ffn1_norm_post, ffn1_w_gate=ffn1_w_gate,
        ffn1_w_up=ffn1_w_up, ffn1_w_down=ffn1_w_down,
        mix_norm_pre=mix_norm_pre, mix_norm_post=mix_norm_post, w_in=w_in, b_merge=b_merge,
        gdn_conv_w=gdn_conv_w, gdn_A_log=gdn_A_log, gdn_dt_bias=gdn_dt_bias, gdn_norm=gdn_norm,
        gla_gate_up=gla_gate_up, gla_gate_bias=gla_gate_bias, gla_norm=gla_norm,
        ssd_conv_w=ssd_conv_w, ssd_conv_b=ssd_conv_b, ssd_A_log=ssd_A_log, ssd_dt_bias=ssd_dt_bias,
        ssd_D=ssd_D, ssd_norm=ssd_norm,
        w_br_gdn=w_br_gdn, w_br_gla=w_br_gla, w_br_ssd=w_br_ssd, w_out=w_out,
        ffn2_norm_pre=ffn2_norm_pre, ffn2_norm_post=ffn2_norm_post, ffn2_w_gate=ffn2_w_gate,
        ffn2_w_up=ffn2_w_up, ffn2_w_down=ffn2_w_down)
    f32 = jnp.float32
    bp = x_prompt.shape[0]
    prompt_init = (jnp.zeros((bp, CONV_WIDTH - 1, GDN_CONV_DIM), x_prompt.dtype),
                   jnp.zeros((bp, GDN_HEADS, GDN_DK, GDN_DV), f32),
                   jnp.zeros((bp, GLA_HEADS, GLA_DK, GLA_DV), f32),
                   jnp.zeros((bp, CONV_WIDTH - 1, SSD_CONV_DIM), x_prompt.dtype),
                   jnp.zeros((bp, SSD_HEADS, SSD_HEADDIM, SSD_DSTATE), f32))
    y_prompt, y_sample = x_prompt, x_sample
    new_p, new_s = [], []
    for l in range(DEPTH):
        p = {name: arr[l] for name, arr in params.items()}
        y_prompt, st_p = _layer(y_prompt, prompt_init, p)
        y_sample, st_s = _layer(
            y_sample,
            (state_gdn_conv[l], state_gdn[l], state_gla[l], state_ssd_conv[l], state_ssd[l]), p)
        new_p.append(st_p)
        new_s.append(st_s)
    p_gdn_conv, p_gdn, p_gla, p_ssd_conv, p_ssd = (jnp.stack(a) for a in zip(*new_p))
    s_gdn_conv, s_gdn, s_gla, s_ssd_conv, s_ssd = (jnp.stack(a) for a in zip(*new_s))
    return (y_prompt, y_sample,
            p_gdn_conv, p_gdn, p_gla, p_ssd_conv, p_ssd,
            s_gdn_conv, s_gdn, s_gla, s_ssd_conv, s_ssd)


_drawn_inputs = setup_inputs


def setup_inputs(seed=0):
    import zlib

    import numpy as np

    out = dict(_drawn_inputs(seed))
    spreads = {}
    factors = {'ffn1_norm_post': 3.057,
     'b_merge': 6.669,
     'gdn_norm': 35.902,
     'gla_norm': 37.663,
     'ssd_D': 50.44,
     'ssd_norm': 19.021,
     'ffn2_norm_pre': 4.048,
     'ffn2_norm_post': 5.814,
     'mix_norm_post': 3.152}
    for name, (base, spread) in spreads.items():
        noise = np.random.default_rng([zlib.crc32(name.encode()), seed]).standard_normal(out[name].shape)
        drawn = base * np.exp(spread * noise) if base else spread * noise
        out[name] = jnp.asarray(drawn.astype(out[name].dtype))
    for name, factor in factors.items():
        out[name] = (out[name] * factor).astype(out[name].dtype)
    return out
```

```python
from contextlib import ExitStack

import concourse.bass as bass
import numpy as np
from concourse import mybir

P = 128
D_MODEL, DEPTH, D_FF = 1024, 2, 2816
SEQ, DEC_BATCH, DEC_SEQ = 512, 8, 4
SAMPLE = DEC_BATCH * DEC_SEQ
T = SEQ + SAMPLE
HALF = T // 2
KD = D_MODEL // P
KF = D_FF // P
EPS = 1e-6
C = 128
CHUNKS = SEQ // C
STEPS = CHUNKS + 1
HEADS = 4
SSD_HEADS = 8
GDN_SCALE, GLA_SCALE = 128 ** -0.5, 64 ** -0.5
GLA_NORMALIZER = 16.0
CONV = 4
LEVELS, SAMPLE_LEVELS = 7, 2

GQ, GK, GV, GZ = 0, 4, 8, 12
LQ, LK, LV, LG = 16, 18, 20, 24
SZ, SX, SB, SC = 28, 32, 36, 38
SMALL = 40
TILES = 41
CONV_TILES = 20
ROW_A, ROW_B, ROW_DT, ROW_R = 0, 32, 64, 96

(F1PRE, F1POST, MPRE, MPOST, F2PRE, F2POST) = range(0, 48, 8)
BMERGE, CONVW, CONVB = 48, 72, 152
GDNN, GLAN, SSDN, SSDD = 172, 173, 174, 178
SBIAS, ALOG, SIGN = 182, 183, 184
GLAB, GUP, NPRM = 192, 448, 704

IDENT, TRI, REV, MASK = 0, 128, 256, 384
ONES = MASK + LEVELS * 128
TRI_S, REV_S, BMASK, EPSC, EPSROW = ONES + 128, ONES + 160, ONES + 192, ONES + 200, ONES + 201
NCONST = ONES + 204

UPS, DOWNS = 2 * KF, 3 * KD
FFN_BLOCKS = UPS + DOWNS
B_FFN1, B_PROJ = 0, FFN_BLOCKS
B_MERGE = B_PROJ + 4 + 40
B_OUT = B_MERGE + 6 * KD
B_FFN2 = B_OUT + KD
BLOCKS = B_FFN2 + FFN_BLOCKS
RAW, SPLIT = 4, 2
DOWN_K = (8, 8, 6)
assert all(b % RAW == 0 for b in (B_PROJ, B_MERGE, B_OUT, B_FFN2, BLOCKS))

F32, F32R, U32 = mybir.dt.float32, mybir.dt.float32r, mybir.dt.uint32
ACT, ALU = mybir.ActivationFunctionType, mybir.AluOpType
MULT, ADD, SUB, MIN, MAX = ALU.mult, ALU.add, ALU.subtract, ALU.min, ALU.max
LN_EXP = "natural_log_exp_and_others"


SOLVES = CHUNKS * LEVELS + SAMPLE_LEVELS
SCORES = CHUNKS * (LEVELS + 1) + SAMPLE_LEVELS + 1
SUMS = (1, 3, 4, 6, 7, 9)


class Step:

    def __init__(self, layer, branch, n, states, levels, cols, c):
        self.layer, self.n, self.states, self.levels = layer, n, states, levels
        self.cols = cols
        self.prompt = states == 1
        self.once = layer * STEPS + c
        self.both = layer * (2 * STEPS) + (branch // 2 * STEPS) + c
        self.solve = layer * SOLVES + c * LEVELS
        self.score = layer * SCORES + c * (LEVELS + 1)
        self.update = layer * (CHUNKS + HEADS) + c
        self.update2 = layer * (CHUNKS + 2) + c


def prompt_step(layer, branch, c):
    return Step(layer, branch, C, 1, LEVELS, bass.ds(c * C, C), c)


def sample_step(layer, branch):
    return Step(layer, branch, SAMPLE, DEC_BATCH, SAMPLE_LEVELS, slice(SEQ, T), CHUNKS)


def trunk(nc, io):
    ctx = ExitStack()
    with ctx:
        base = -(-nc.sbuf_base // 64) * 64

        def at(name, offset, shape, dt=F32):
            return nc.alloc_sbuf_tensor_at(name, shape, dt, offset=base + offset)

        def sem(name):
            return ctx.enter_context(nc.semaphore(name))

        TB = T * 4
        place = [0]

        def put(name, shape, dt=F32):
            size = 4 * int(np.prod(shape[1:]))
            t = at(name, place[0], shape, dt)
            place[0] += -(-size // 32) * 32
            return t

        x = put("x", [P, KD, T])
        raw = put("raw", [P, RAW, KD, P])
        wh = put("wh", [P, SPLIT, KD, P], F32R)
        wl = put("wl", [P, SPLIT, KD, P], F32R)
        cst = put("cst", [P, NCONST])
        prm = put("prm", [P, NPRM])
        rstd = put("rstd", [P, T])
        rstd_post = put("rstd_post", [P, T])
        nega = put("nega", [P, 1])
        cw = put("cw", [P, 16])
        cb = put("cb", [P, 4])
        bm = put("bm", [P, 6])
        R = place[0]
        assert base + R + 68 * TB <= nc.sbuf_usable_end, (base + R + 68 * TB, nc.sbuf_usable_end)

        def row(name, r, shape, dt=F32, more=0):
            return at(name, R + r * TB + more, shape, dt)

        hh, hl = row("hh", 0, [P, KD, T], F32R), row("hl", 8, [P, KD, T], F32R)
        ah, al = row("ah", 16, [P, KF, T], F32R), row("al", 38, [P, KF, T], F32R)
        f = row("f", 60, [P, KD, T])
        hf = row("hf", 60, [P, KD, T])
        sq = row("sq", 0, [P, KD, T])
        sil, prod = row("sil", 60, [P, 2, T]), row("prod", 62, [P, 2, T])
        proj = row("proj", 16, [P, TILES, T])
        PADW = 3 + SEQ + DEC_BATCH * (3 + DEC_SEQ)
        CW = PADW - 3
        pad = row("pad", 60, [P, 4, PADW])
        cacc = row("cacc", 57, [P, 2, PADW])
        cs_in = row("cs_in", 65, [P, CONV_TILES, DEC_BATCH, 3])
        cs_p = row("cs_p", 66, [P, CONV_TILES, 3])
        cs_s = row("cs_s", 66, [P, CONV_TILES, DEC_BATCH, 3], more=256)
        assert 4 * 4 * PADW <= 5 * TB and 2 * 4 * PADW <= 3 * TB
        sp, se, sl = row("sp", 57, [P, T]), row("se", 58, [P, T]), row("sl", 59, [P, T])
        cm = row("cm", 58, [P, T])
        cc, tm, gc = (row(s, 57, [P, P], more=512 * i) for i, s in enumerate(("cc", "tm", "gc")))
        br, rg = (row(s, 59, [P, P], more=512 * i) for i, s in enumerate(("br", "rg")))
        states = row("states", 60, [P, DEC_BATCH, 512])

        def work(name, k, units=1, dt=F32):
            return at(name, R + 2048 * k, [P, 512 * units], dt)

        (kn, qn, kg, qg, eg, dd, aa, att, al_, xx, xt, pp, rt, rr, uu, kd, gs) = (
            work(f"g{i}", i) for i in range(17))
        sq8, rs8 = work("sq8", 12, 2), work("rs8", 14, 2)
        uexp = work("uexp", 9, 2)
        lz, la, lgk, lbt, leb, ler, lqs, lqe, lkd, lks = (
            at(f"l{i}", R + 1024 * i, [P, 256]) for i in range(10))
        ldl = at("ldl", R + 10240, [P, LEVELS, 256])
        lml = at("lml", R + 10240 + 7168, [P, LEVELS, 256])
        latt, lvc, lvt = (at(f"la{i}", R + 24576 + 2048 * i, [P, 512]) for i in range(3))
        lkt, ls = (at(f"lb{i}", R + 30720 + 1024 * i, [P, 256]) for i in range(2))
        lrc = at("lrc", R + 32768, [P, P])
        vexp = at("vexp", R + 10240, [P, DEC_BATCH, P])
        sxbc, sea, sdd, sce = (work(f"s{i}", 2 * i, 2) for i in range(4))
        sxd, sxe, ss_, sbt = (work(f"s{i}", 4 + i) for i in range(4, 8))
        xexp = work("xexp", 12, 4)
        nsq, nrs, nt = row("nsq", 0, [P, 4, T]), row("nrs", 4, [P, 4, T]), row("nt", 8, [P, 4, T])
        oh = [row(f"oh{i}", 16 + r, [P, 4, T], F32R) for i, r in enumerate((GQ, LQ, SB))]
        ol = [row(f"ol{i}", 16 + r, [P, 4, T], F32R) for i, r in enumerate((GK, LV, SX))]
        mh, ml = row("mh", 16 + GV, [P, KD, T], F32R), row("ml", 16 + LG, [P, KD, T], F32R)
        sg, mt_, mac = row("sg", 60, [P, 2, T]), row("mt", 62, [P, 1, T]), row("mac", 63, [P, 2, T])

        ps = ctx.enter_context(nc.psum_tensor("ps", [P, 8, 512], F32))

        ident, tri, rev = (cst[:, a:a + P] for a in (IDENT, TRI, REV))
        ones = cst[:, ONES:ONES + P]
        epsc = cst[:, EPSC:EPSC + 1]

        def pair(slot):
            return ps[:, 2 * slot:2 * slot + 2, 0:HALF]

        def halves(ap):
            return ap.rearrange("p (a t) -> p a t", a=2)

        started = sem("started")
        loaded = sem("loaded")
        prm_in = sem("prm_in")
        raw_full = [sem(f"raw_full{i}") for i in range(RAW)]
        hi_done, lo_done = sem("hi_done"), sem("lo_done")
        blk_done = sem("blk_done")
        sq_ready, sum_ready, ln_ready, rstd_ready = (sem(s) for s in ("sq_ready", "sum_ready", "ln_ready", "rstd_ready"))
        x_tmp, x_done = sem("x_tmp"), sem("x_done")
        hf_ready, hh_ready, hl_ready = sem("hf_ready"), sem("hh_ready"), sem("hl_ready")
        sil_done, prod_done = sem("sil_done"), sem("prod_done")
        ah_done, al_done = sem("ah_done"), sem("al_done")
        out_done = sem("out_done")
        evict_done, small_done = sem("evict_done"), sem("small_done")
        pad_zero, tap, conv_done, csil_done = (sem(s) for s in ("pad_zero", "tap", "conv_done", "csil_done"))
        cs_loaded, cs_saved, cw_ready = sem("cs_loaded"), sem("cs_saved"), sem("cw_ready")
        narrow = {s: sem("n_" + s) for s in ("alog", "z", "abs", "exp", "ln", "sp", "g", "beta", "dt")}
        both = {s: sem("r_" + s) for s in "cc tmp tm cum gc rg br bc d dx dm".split()}
        g_ = {s: sem("g_" + s) for s in (
            "brb sq ss ln rs qk kk kt eg kg at atb xi kd al p pc q x "
            "tb sk rt rtt r up u o oc su sm s ue").split()}
        l_ = {s: sem("l_" + s) for s in (
            "rc z zt a1 a2 a3 g1 gk b bt qk qe dl d1 d2 ml a0 at cp vc vtp vt kdp kt o oc ve su sm s").split()}
        s_ = {s: sem("s_" + s) for s in (
            "st tr ea ce att xd xe bt y yc xe2 su sm s").split()}
        zeroed = sem("zeroed")
        st_in, st_out = sem("st_in"), sem("st_out")
        n_ = {s: sem("o_" + s) for s in ("yz", "sq", "ss", "ln", "rs", "t", "tz", "hi", "lo")}
        sg_done, mac_tmp, mac_done, mh_done, ml_done, bm_ready = (
            sem(s) for s in ("sg_done", "mac_tmp", "mac_done", "mh_done", "ml_done", "bm_ready"))
        saved = sem("saved")

        def value(eng, v):
            eng.compute_val(v)
            eng.wait_ge(started, 1)
            return v

        def further(eng, v):
            eng.compute_val(v)
            eng.wait_ge(loaded, 32)
            return v

        block = ctx.enter_context(nc.Block())

        @block.sync
        def _(sp_):
            sp_.dma_start(cst[:], io["cst"]).then_inc(loaded, 16)
            sp_.dma_start(x[:], io["x"].rearrange("p (k t) -> p k t", k=KD)).then_inc(loaded, 16)

            def blocks(layer, first, i, nks, source):
                for j, nk in enumerate(nks):
                    sp_.wait_ge(lo_done, value(sp_, layer * BLOCKS + i * len(nks) + (first + j + 1)))
                    sp_.dma_start(raw[:, j % RAW, 0:nk, :], source(j)).then_inc(raw_full[j % RAW], 16)

            def tiles(name, index):
                return io[name][bass.ds(index, 1)].rearrange("a p (k m) -> p (a k) m", m=P)

            def ffn(layer, which, first):
                with sp_.Fori(0, KF // 2) as i:
                    blocks(layer, first, i, (KD,) * 4,
                           lambda j: tiles("up", layer * (2 * UPS) + i * 4 + (which * UPS + j)))
                k0 = np.cumsum((0,) + DOWN_K)
                with sp_.Fori(0, 2) as i:
                    blocks(layer, first + UPS, i, DOWN_K * 4,
                           lambda j: tiles("down", layer * (2 * KD) + i * 4 + (which * KD + j // 3))
                           [:, k0[j % 3]:k0[j % 3 + 1], :])

            with sp_.Fori(0, DEPTH) as layer:
                sp_.wait_ge(x_done, value(sp_, layer * (3 * KD) + 1))
                sp_.dma_start(prm[:], io["prm"][bass.ds(layer, 1)].rearrange("a p n -> (a p) n")).then_inc(prm_in, 16)
                ffn(layer, 0, B_FFN1)
                blocks(layer, B_PROJ, 0, (2,) * 4,
                       lambda j: tiles("narrow", layer)[:, 2 * j:2 * j + 2, :])
                with sp_.Fori(0, 10) as i:
                    blocks(layer, B_PROJ + 4, i, (KD,) * 4, lambda j: tiles("win", layer * 40 + i * 4 + j))
                with sp_.Fori(0, KD // 2) as i:
                    blocks(layer, B_MERGE, i, (KD, 4) * 6,
                           lambda j: tiles("branch" if j % 2 else "gate", layer * 24 + i * 6 + j // 2))
                with sp_.Fori(0, 2) as i:
                    blocks(layer, B_OUT, i, (KD,) * 4, lambda j: tiles("wout", layer * KD + i * 4 + j))
                ffn(layer, 1, B_FFN2)
            sp_.wait_ge(x_done, DEPTH * 3 * KD + 1)
            sp_.dma_start(io["y"].rearrange("p (k t) -> p k t", k=KD), x[:]).then_inc(saved, 16)
            sp_.wait_ge(saved, 16)
            sp_.wait_ge(cs_saved, DEPTH * 32)
            sp_.wait_ge(st_out, DEPTH * 96)

        @block.gpsimd
        def _(pool):
            def blocks(layer, first, i, nks):
                for j, nk in enumerate(nks):
                    src = raw[:, j % RAW, 0:nk, :].rearrange("p k m -> p (k m)")
                    hi = wh[:, j % SPLIT, 0:nk, :].rearrange("p k m -> p (k m)")
                    lo = wl[:, j % SPLIT, 0:nk, :].rearrange("p k m -> p (k m)")
                    turns = len(nks) // RAW
                    pool.wait_ge(raw_full[j % RAW], value(pool, layer * (BLOCKS // RAW * 16) + i * (turns * 16) + 16 * ((first + j) // RAW + 1)))
                    pool.wait_ge(blk_done, further(pool, layer * BLOCKS + i * len(nks) + (first + j + 1)))
                    pool.tensor_scalar(hi, src, 1.0, 1.0, MULT, MULT).then_inc(hi_done, 1)
                    pool.wait_ge(hi_done, value(pool, layer * BLOCKS + i * len(nks) + (first + j + 1)))
                    pool.tensor_tensor(lo, src, hi.bitcast(F32), SUB).then_inc(lo_done, 1)

            def ffn(layer, first):
                with pool.Fori(0, KF // 2) as i:
                    blocks(layer, first, i, (KD,) * 4)
                with pool.Fori(0, 2) as i:
                    blocks(layer, first + UPS, i, DOWN_K * 4)

            with pool.Fori(0, DEPTH) as layer:
                ffn(layer, B_FFN1)
                blocks(layer, B_PROJ, 0, (2,) * 4)
                with pool.Fori(0, 10) as i:
                    blocks(layer, B_PROJ + 4, i, (KD,) * 4)
                with pool.Fori(0, KD // 2) as i:
                    blocks(layer, B_MERGE, i, (KD, 4) * 6)
                with pool.Fori(0, 2) as i:
                    blocks(layer, B_OUT, i, (KD,) * 4)
                ffn(layer, B_FFN2)

        @block.tensor
        def _(pe):
            pe.wait_ge(loaded, 32)

            def product(layer, first, i, j, per, slot, nk, moving, start=True, stop=True):
                pe.wait_ge(lo_done, value(pe, layer * BLOCKS + i * per + (first + j + 1 + RAW)))
                for k in range(nk):
                    mh_, ml_ = moving(k)
                    for h in range(2):
                        out = ps[:, 2 * slot + h, 0:HALF]
                        c = slice(h * HALF, (h + 1) * HALF)
                        a, b = start and k == 0, stop and k == nk - 1
                        pe.matmul(out, wh[:, j % SPLIT, k, :], mh_[:, c], start=a, stop=False)
                        pe.matmul(out, wh[:, j % SPLIT, k, :], ml_[:, c], start=False, stop=False)
                        last = pe.matmul(out, wl[:, j % SPLIT, k, :], mh_[:, c], start=False, stop=b)
                last.then_inc(blk_done, 1)

            def h_tiles(k):
                return hh[:, k, :], hl[:, k, :]

            def add_squares(src, start=False, stop=False):
                for h in range(2):
                    last = pe.matmul(ps[:, 6 + h, 0:HALF], ones, src[:, h * HALF:(h + 1) * HALF],
                                     start=start, stop=stop, skip_group_check=True)
                return last

            def eps_first():
                for h in range(2):
                    pe.matmul(ps[:, 6 + h, 0:HALF], ones, cst[:, EPSROW:EPSROW + 1].to_broadcast([P, HALF]),
                              start=True, stop=False, skip_group_check=True)

            def pre_stats(layer, stage):
                for k in range(KD):
                    pe.wait_ge(sq_ready, value(pe, layer * (6 * KD) + (stage * KD + k + 1)))
                    if k == 0:
                        eps_first()
                    last = add_squares(sq[:, k, :], stop=(k == KD - 1))
                last.then_inc(sum_ready, 1)

            def reduce_out(layer, stage, first, nks, moving):
                per = len(nks)
                k0 = np.cumsum((0,) + tuple(nks))
                eps_first()
                with pe.Fori(0, 2) as i:
                    for m in range(4):
                        pe.wait_ge(out_done, value(pe, layer * (3 * KD) + i * 4 + (stage // 2 * KD + m + 1)))
                        for b, nk in enumerate(nks):
                            product(layer, first, i, per * m + b, 4 * per, m % 2, nk,
                                    lambda k, b=b: moving(k0[b] + k), b == 0, b == per - 1)
                        if m:
                            pe.wait_ge(sq_ready, value(pe, layer * (6 * KD) + i * 4 + (stage * KD + m)))
                            add_squares(sq[:, m - 1, :])
                    pe.wait_ge(sq_ready, value(pe, layer * (6 * KD) + i * 4 + (stage * KD + 4)))
                    add_squares(sq[:, 3, :], stop=True).then_inc(sum_ready, 1)

            def ffn(layer, which, first):
                pre_stats(layer, 4 * which)
                pe.wait_ge(hl_ready, value(pe, layer * (4 * KD) + (3 * which * KD + KD)))
                with pe.Fori(0, KF // 2) as i:
                    for j in range(4):
                        pe.wait_ge(prod_done if j % 2 else sil_done, value(pe, layer * (2 * KF) + i * 2 + (which * KF + j // 2 + 1)))
                        product(layer, first, i, j, 4, j, KD, h_tiles)
                pe.wait_ge(al_done, value(pe, layer * (2 * KF) + (which + 1) * KF))
                reduce_out(layer, 4 * which + 1, first + UPS, DOWN_K, lambda k: (ah[:, k, :], al[:, k, :]))

            def common(step):
                n = step.n
                tri_n, rev_n = (tri, rev) if step.prompt else (
                    cst[:, TRI_S:TRI_S + 32], cst[:, REV_S:REV_S + 32])
                pe.wait_ge(both["cc"], value(pe, step.both + 1))
                pe.transpose(ps[0:n, 6, 0:P], cc[:, 0:n], ident).then_inc(both["tmp"], 1)
                pe.wait_ge(both["tm"], value(pe, step.both + 1))
                pe.matmul(ps[0:n, 7, 0:P], tri_n[0:n, 0:n], tm[0:n, :], start=True, stop=True)
                pe.matmul(ps[0:n, 7, P:2 * P], rev_n[0:n, 0:n], tm[0:n, :], start=True, stop=True)
                pe.matmul(ps[:, 7, 2 * P:2 * P + n], tm[0:n, :], tri_n[0:n, 0:n], start=True, stop=True).then_inc(both["cum"], 1)

            def spread(bank, off, rowi, n):
                return pe.matmul(ps[:, bank, off:off + n], cst[:, IDENT + rowi:IDENT + rowi + 1].to_broadcast([P, P]),
                                 br[:, 0:n], start=True, stop=True)

            def gdn(step):
                n, o = step.n, step.once
                common(step)
                pe.wait_ge(g_["sq"], value(pe, o + 1))
                w = 8 * n
                for b in range(-(-w // 512)):
                    c = min(512, w)
                    last = pe.matmul(ps[:, b, 0:c], ones, sq8[:, b * 512:b * 512 + c], start=True, stop=True)
                last.then_inc(g_["ss"], 1)
                pe.wait_ge(g_["brb"], value(pe, o + 1))
                for h in range(HEADS):
                    spread(2, h * n, ROW_A + h, n)
                for h in range(HEADS):
                    last = spread(3, h * n, ROW_B + h, n)
                last.then_inc(both["bc"], 1)
                pe.wait_ge(g_["qk"], value(pe, o + 1))
                for h in range(HEADS):
                    k_, q_ = kn[:, h * n:(h + 1) * n], qn[:, h * n:(h + 1) * n]
                    pe.matmul(ps[0:n, 4, h * n:(h + 1) * n], k_, k_, start=True, stop=True)
                    last = pe.matmul(ps[0:n, 5, h * n:(h + 1) * n], k_, q_, start=True, stop=True)
                last.then_inc(g_["kk"], 1)
                pe.wait_ge(both["rg"], value(pe, step.both + 1))
                for h in range(HEADS):
                    last = pe.transpose(ps[0:n, 7, h * P:(h + 1) * P], kn[:, h * n:(h + 1) * n], ident)
                last.then_inc(g_["kt"], 1)
                for l in range(step.levels):
                    final = l == step.levels - 1
                    pe.wait_ge(g_["al"], value(pe, step.solve + l + 1))
                    if l == 0:
                        pe.wait_ge(g_["xi"], further(pe, o + 1))
                        pe.wait_ge(g_["kd"], further(pe, o + 1))
                    else:
                        pe.wait_ge(g_["x"], further(pe, step.solve + l))
                    for h in range(HEADS):
                        c = slice(h * n, (h + 1) * n)
                        last = pe.matmul(ps[0:n, 6, c], al_[0:n, c], xx[0:n, c], start=True, stop=True)
                    last.then_inc(g_["p"], 1)
                    pe.wait_ge(g_["pc"], value(pe, step.solve + l + 1))
                    for h in range(HEADS):
                        c = slice(h * n, (h + 1) * n)
                        if not final:
                            pe.matmul(ps[0:n, 7, c], xt[0:n, c], pp[0:n, c], start=True, stop=True)
                        last = pe.matmul(ps[0:n, 2, c], pp[0:n, c], xt[0:n, c], start=True, stop=True)
                    last.then_inc(g_["q"], 1)

                def s_of(h, b):
                    return gs[:, h * P:(h + 1) * P] if step.prompt else states[:, b, h * P:(h + 1) * P]

                def through_state(bank, h, src, stop):
                    w_ = n // step.states
                    for b in range(step.states):
                        c = slice(h * n + b * w_, h * n + (b + 1) * w_)
                        last = pe.matmul(ps[:, bank, c], s_of(h, b), src[:, c], start=(b == 0), stop=stop,
                                         skip_group_check=True)
                    return last

                if step.prompt:
                    pe.wait_ge(g_["s"], value(pe, o + 1))
                    pe.wait_ge(zeroed, further(pe, step.layer * 3 + 1))
                else:
                    pe.wait_ge(st_in, further(pe, step.layer * 48 + 16))
                pe.wait_ge(g_["kg"], further(pe, o + 1))
                for h in range(HEADS):
                    last = through_state(3, h, kg, True)
                last.then_inc(g_["sk"], 1)
                pe.wait_ge(g_["rt"], value(pe, o + 1))
                for h in range(HEADS):
                    last = pe.transpose(ps[0:n, 4, h * P:(h + 1) * P], rt[:, h * n:(h + 1) * n], ident)
                last.then_inc(g_["rtt"], 1)
                pe.wait_ge(g_["r"], value(pe, o + 1))
                pe.wait_ge(g_["tb"], further(pe, o + 1))
                for h in range(HEADS):
                    last = pe.matmul(ps[0:n, 5, h * P:(h + 1) * P], xt[0:n, h * n:(h + 1) * n],
                                     rr[0:n, h * P:(h + 1) * P], start=True, stop=True)
                last.then_inc(g_["up"], 1)
                pe.wait_ge(g_["u"], value(pe, o + 1))
                for h in range(HEADS):
                    through_state(6, h, qg, False)
                    last = pe.matmul(ps[:, 6, h * n:(h + 1) * n], uu[0:n, h * P:(h + 1) * P],
                                     att[0:n, h * n:(h + 1) * n], start=False, stop=True, skip_group_check=True)
                last.then_inc(g_["o"], 1)
                if step.prompt:
                    for h in range(HEADS):
                        last = pe.matmul(ps[:, 0, h * P:(h + 1) * P], kd[0:n, h * P:(h + 1) * P],
                                         uu[0:n, h * P:(h + 1) * P], start=True, stop=True)
                    last.then_inc(g_["su"], 1)
                else:
                    for h in range(HEADS):
                        pe.wait_ge(g_["ue"], value(pe, step.layer * HEADS + h + 1))
                        for b in range(2):
                            last = pe.matmul(ps[:, b, :], kd[0:n, h * P:(h + 1) * P], uexp[0:n, b * 512:(b + 1) * 512],
                                             start=True, stop=True)
                        last.then_inc(g_["su"], 1)

            def gla(step):
                n, o = step.n, step.once
                tri_n, rev_n = (tri, rev) if step.prompt else (
                    cst[:, TRI_S:TRI_S + 32], cst[:, REV_S:REV_S + 32])
                pe.wait_ge(l_["rc"], value(pe, o + 1))
                pe.matmul(ps[0:n, 0, 0:256], lrc[96:112, 0:n], prm[96:112, GUP:GUP + 256],
                          start=True, stop=True).then_inc(l_["z"], 1)
                pe.wait_ge(l_["gk"], value(pe, o + 1))
                for g in range(2):
                    pe.matmul(ps[:, 1, g * n:(g + 1) * n], lgk[0:n, g * P:(g + 1) * P], tri_n[0:n, 0:n], start=True, stop=True)
                for g in range(2):
                    last = pe.matmul(ps[:, 1, (2 + g) * n:(3 + g) * n], lgk[0:n, g * P:(g + 1) * P], rev_n[0:n, 0:n],
                                     start=True, stop=True)
                last.then_inc(l_["b"], 1)
                pe.wait_ge(l_["vc"], value(pe, o + 1))
                for h in range(HEADS):
                    last = pe.transpose(ps[0:n, 4, h * P:(h + 1) * P], lvc[:, h * n:(h + 1) * n], ident)
                last.then_inc(l_["vtp"], 1)
                pe.wait_ge(l_["qe"], value(pe, o + 1))
                for g in range(2):
                    last = pe.transpose(ps[0:n, 5, g * P:(g + 1) * P], lkd[:, g * n:(g + 1) * n], ident)
                last.then_inc(l_["kdp"], 1)
                for l in range(step.levels + 1):
                    if l == 0:
                        pe.wait_ge(l_["ml"], value(pe, o + 1))
                    elif l >= 2:
                        pe.wait_ge(l_["cp"], further(pe, step.score + l - 1))
                    for h in range(HEADS):
                        r = slice(64 * (h % 2), 64 * (h % 2) + 64)
                        c = slice(h // 2 * n, (h // 2 + 1) * n)
                        a, b = (lml[r, l, c], lml[r, l, c]) if l < step.levels else (lks[r, c], lqs[r, c])
                        last = pe.matmul(ps[0:n, 2 - l % 2 * 2 + h % 2, c], a, b, start=True, stop=True)
                    last.then_inc(l_["at"], 1)
                if step.prompt:
                    pe.wait_ge(l_["s"], value(pe, o + 1))
                    pe.wait_ge(zeroed, further(pe, step.layer * 3 + 2))
                else:
                    pe.wait_ge(st_in, further(pe, step.layer * 48 + 32))
                pe.wait_ge(l_["cp"], further(pe, step.score + step.levels + 1))
                pe.wait_ge(l_["vt"], further(pe, o + 1))
                w_ = n // step.states
                for h in range(HEADS):
                    r = slice(64 * (h % 2), 64 * (h % 2) + 64)
                    g = h // 2
                    for b in range(step.states):
                        s_b = ls[r, g * P:(g + 1) * P] if step.prompt else states[r, b, g * P:(g + 1) * P]
                        pe.matmul(ps[:, 6 + h % 2, g * n + b * w_:g * n + (b + 1) * w_], s_b,
                                  lqe[r, g * n + b * w_:g * n + (b + 1) * w_], start=(b == 0), stop=False,
                                  skip_group_check=True)
                    a = (h % 2 * 2 + g) * n
                    last = pe.matmul(ps[:, 6 + h % 2, g * n:(g + 1) * n], lvt[0:n, h * P:(h + 1) * P],
                                     latt[0:n, a:a + n], start=False, stop=True, skip_group_check=True)
                last.then_inc(l_["o"], 1)
                pe.wait_ge(l_["kt"], value(pe, o + 1))
                if step.prompt:
                    for h in range(HEADS):
                        r = slice(64 * (h % 2), 64 * (h % 2) + 64)
                        last = pe.matmul(ps[r, 4, h // 2 * P:(h // 2 + 1) * P], lkt[0:n, h * 64:(h + 1) * 64],
                                         lvt[0:n, h * P:(h + 1) * P], start=True, stop=True)
                    last.then_inc(l_["su"], 1)
                else:
                    for h in range(HEADS):
                        r = slice(64 * (h % 2), 64 * (h % 2) + 64)
                        pe.wait_ge(l_["ve"], value(pe, step.layer * HEADS + h + 1))
                        for b in range(2):
                            last = pe.matmul(ps[r, b, :], lkt[0:n, h * 64:(h + 1) * 64],
                                             vexp[0:n, 4 * b:4 * b + 4, :].rearrange("p a b -> p (a b)"),
                                             start=True, stop=True)
                        last.then_inc(l_["su"], 1)

            def ssd(step):
                n, o = step.n, step.once
                common(step)
                pe.wait_ge(both["br"], value(pe, step.both + 1))
                for h in range(SSD_HEADS):
                    last = spread(h // 4, h % 4 * n, ROW_DT + h, n)
                last.then_inc(both["bc"], 1)
                pe.wait_ge(s_["st"], value(pe, o + 1))
                for g in range(2):
                    pe.matmul(ps[0:n, 2, g * n:(g + 1) * n], sxbc[:, (4 + g) * n:(5 + g) * n],
                              sxbc[:, (6 + g) * n:(7 + g) * n], start=True, stop=True)
                for t in range(4):
                    pe.transpose(ps[0:n, 3, t * P:(t + 1) * P], sxbc[:, t * n:(t + 1) * n], ident)
                for g in range(2):
                    last = pe.transpose(ps[0:n, 4, g * P:(g + 1) * P], sxbc[:, (4 + g) * n:(5 + g) * n], ident)
                last.then_inc(s_["tr"], 1)
                if step.prompt:
                    pe.wait_ge(s_["s"], value(pe, o + 1))
                    pe.wait_ge(zeroed, further(pe, step.layer * 3 + 3))
                else:
                    pe.wait_ge(st_in, further(pe, step.layer * 48 + 48))
                pe.wait_ge(s_["att"], further(pe, o + 1))
                pe.wait_ge(s_["xe"], further(pe, o + 1))
                pe.wait_ge(s_["ce"], further(pe, o + 1))
                w_ = n // step.states
                for h in range(SSD_HEADS):
                    r = slice(64 * (h % 2), 64 * (h % 2) + 64)
                    t = h // 2
                    for b in range(step.states):
                        s_b = ss_[:, h * 64:(h + 1) * 64] if step.prompt else states[:, b, h * 64:(h + 1) * 64]
                        pe.matmul(ps[r, 5, t * n + b * w_:t * n + (b + 1) * w_], s_b,
                                  sce[:, h * n + b * w_:h * n + (b + 1) * w_], start=(b == 0), stop=False,
                                  skip_group_check=True)
                    last = pe.matmul(ps[r, 5, t * n:(t + 1) * n], sxd[0:n, h * 64:(h + 1) * 64],
                                     sdd[0:n, h * n:(h + 1) * n], start=False, stop=True, skip_group_check=True)
                last.then_inc(s_["y"], 1)
                pe.wait_ge(s_["bt"], value(pe, o + 1))
                if step.prompt:
                    for g in range(2):
                        last = pe.matmul(ps[:, 6, g * 256:(g + 1) * 256], sbt[0:n, g * P:(g + 1) * P],
                                         sxe[0:n, g * 256:(g + 1) * 256], start=True, stop=True)
                    last.then_inc(s_["su"], 1)
                else:
                    for g in range(2):
                        pe.wait_ge(s_["xe2"], value(pe, step.layer * 2 + g + 1))
                        for b in range(4):
                            last = pe.matmul(ps[:, b, :], sbt[0:n, g * P:(g + 1) * P],
                                             xexp[0:n, b * 512:(b + 1) * 512], start=True, stop=True)
                        last.then_inc(s_["su"], 1)

            def branch_stats(layer, branch):
                pe.wait_ge(n_["sq"], value(pe, layer * 3 + branch + 1))
                if branch < 2:
                    for t in range(4):
                        for h in range(2):
                            last = pe.matmul(ps[:, 2 * t + h, 0:HALF], ones, nsq[:, t, h * HALF:(h + 1) * HALF],
                                             start=True, stop=True)
                else:
                    for g in range(2):
                        for t in range(2):
                            for h in range(2):
                                last = pe.matmul(ps[:, 2 * g + h, 0:HALF], ones,
                                                 nsq[:, 2 * g + t, h * HALF:(h + 1) * HALF],
                                                 start=(t == 0), stop=(t == 1))
                last.then_inc(n_["ss"], 1)

            with pe.Fori(0, DEPTH) as layer:
                ffn(layer, 0, B_FFN1)
                pre_stats(layer, 2)
                pe.wait_ge(hl_ready, value(pe, layer * (4 * KD) + 2 * KD))
                for j in range(4):
                    product(layer, B_PROJ, 0, j, 4, 0, 2, lambda k: h_tiles(2 * j + k), j == 0, j == 3)
                pe.wait_ge(small_done, value(pe, layer + 1))
                with pe.Fori(0, 10) as i:
                    for j in range(4):
                        pe.wait_ge(evict_done, value(pe, layer * 40 + i * 4 + (j + 1)))
                        product(layer, B_PROJ + 4, i, j, 4, j, KD, h_tiles)
                pe.wait_ge(evict_done, value(pe, layer * 40 + 44))
                for b, chunk in enumerate((gdn, gla, ssd)):
                    with pe.Fori(0, CHUNKS) as c:
                        chunk(prompt_step(layer, b, c))
                    chunk(sample_step(layer, b))
                    branch_stats(layer, b)
                pe.wait_ge(hl_ready, value(pe, layer * (4 * KD) + 3 * KD))
                with pe.Fori(0, KD // 2) as i:
                    for j in range(12):
                        u = j // 2
                        if j % 2:
                            pe.wait_ge(mac_done, value(pe, layer * 24 + i * 6 + (u + 1)))
                            product(layer, B_MERGE, i, j, 12, j % 4, 4,
                                    lambda k, u=u: (oh[u % 3][:, k, :], ol[u % 3][:, k, :]))
                        else:
                            pe.wait_ge(sg_done, value(pe, layer * 24 + i * 6 + (u + 1)))
                            product(layer, B_MERGE, i, j, 12, j % 4, KD, h_tiles)
                pe.wait_ge(ml_done, value(pe, layer * KD + KD))
                reduce_out(layer, 3, B_OUT, (KD,), lambda k: (mh[:, k, :], ml[:, k, :]))
                ffn(layer, 1, B_FFN2)

        @block.scalar
        def _(act):
            act.wait_ge(loaded, 32)

            def rsqrt_stats(layer, stage, out):
                act.preload_act_table_set(LN_EXP)
                act.wait_ge(sum_ready, value(act, layer * SUMS[-1] + SUMS[stage]))
                act.activation(halves(out[:, :]), ps[:, 6:8, 0:HALF], ACT.Ln, scale=1.0 / D_MODEL).then_inc(ln_ready, 1)
                act.wait_ge(ln_ready, value(act, layer * 6 + (stage + 1)))
                act.activation(out[:, :], out[:, :], ACT.Exp, scale=-0.5).then_inc(rstd_ready, 1)

            def split_h(layer, number):
                for k in range(KD):
                    act.wait_ge(hf_ready, value(act, layer * (4 * KD) + (number * KD + k + 1)))
                    act.activation(hh[:, k, :], hf[:, k, :], ACT.Copy).then_inc(hh_ready, 1)

            def pre_norm(layer, stage, number):
                for k in range(KD):
                    act.wait_ge(x_done, value(act, layer * (3 * KD) + ((stage // 2 - 1) * KD + k + 2 if stage else 1)))
                    act.activation(sq[:, k, :], x[:, k, :], ACT.Square).then_inc(sq_ready, 1)
                rsqrt_stats(layer, stage, rstd)
                split_h(layer, number)

            def reduce_out(layer, stage, first, per):
                with act.Fori(0, 2) as i:
                    for m in range(4):
                        act.wait_ge(blk_done, value(act, layer * BLOCKS + i * (4 * per) + (first + per * m + per + SPLIT)))
                        act.activation(sq[:, m, :].rearrange("p (a t) -> p a t", a=2), pair(m % 2), ACT.Square).then_inc(sq_ready, 1)
                        act.activation(f[:, bass.ds(i * 4 + m, 1), :].rearrange("p k (a t) -> p (k a) t", a=2),
                                       pair(m % 2), ACT.Copy).then_inc(out_done, 1)
                rsqrt_stats(layer, stage, rstd_post)

            def ffn(layer, which, first):
                pre_norm(layer, 4 * which, 3 * which)
                with act.Fori(0, KF // 2) as i:
                    for j in range(2):
                        n = layer * (2 * KF) + i * 2 + (which * KF + j)
                        act.wait_ge(blk_done, value(act, layer * BLOCKS + i * 4 + (first + 2 * j + 1 + SPLIT)))
                        act.wait_ge(prod_done, further(act, n + 1))
                        act.activation(halves(sil[:, j, :]), pair(2 * j), ACT.Silu).then_inc(sil_done, 1)
                        act.wait_ge(prod_done, value(act, n + 3))
                        act.activation(ah[:, bass.ds(i * 2 + j, 1), :].rearrange("p k t -> p (k t)"), prod[:, j, :],
                                       ACT.Copy).then_inc(ah_done, 1)
                reduce_out(layer, 4 * which + 1, first + UPS, 3)

            def common(step, gdn_cols):
                n, o = step.n, step.once
                act.wait_ge(both["tmp"], value(act, step.both + 1))
                act.activation(tm[0:n, :], ps[0:n, 6, 0:P], ACT.Copy).then_inc(both["tm"], 1)
                act.wait_ge(both["cum"], value(act, step.both + 1))
                act.activation(gc[0:n, :], ps[0:n, 7, 0:P], ACT.Copy).then_inc(both["gc"], 1)
                act.activation(br[:, 0:n], ps[:, 7, 2 * P:2 * P + n], ACT.Copy).then_inc(both["br"], 1)
                r = slice(ROW_A, ROW_A + 4) if gdn_cols else slice(ROW_DT, ROW_DT + 8)
                act.activation(rg[0:n, r], ps[0:n, 7, P + r.start:P + r.stop], ACT.Exp).then_inc(both["rg"], 1)

            def view(a, k, n):
                return a[:, 0:k * n].rearrange("p (k t) -> p k t", k=k)

            def gdn(step):
                n, o = step.n, step.once
                act.wait_ge(g_["s"], value(act, o + 1))
                act.activation(view(sq8, 8, n), proj[:, GQ:GQ + 8, step.cols], ACT.Square).then_inc(g_["sq"], 1)
                common(step, True)
                act.wait_ge(g_["ss"], value(act, o + 1))
                w = min(512, 8 * n)
                act.activation(rs8[:, 0:8 * n].rearrange("p (b c) -> p b c", c=w), ps[:, 0:8 * n // w, 0:w], ACT.Ln,
                               bias=epsc).then_inc(g_["ln"], 1)
                act.wait_ge(g_["ln"], value(act, o + 1))
                act.activation(rs8[:, 0:8 * n], rs8[:, 0:8 * n], ACT.Exp, scale=-0.5).then_inc(g_["rs"], 1)
                act.wait_ge(both["bc"], value(act, step.both + 1))
                act.activation(eg[:, 0:4 * n], ps[:, 2, 0:4 * n], ACT.Exp).then_inc(g_["eg"], 1)
                act.wait_ge(both["d"], value(act, step.both + 1))
                act.activation(dd[0:n, 0:4 * n], dd[0:n, 0:4 * n], ACT.Exp).then_inc(both["dx"], 1)
                for l in range(step.levels):
                    act.wait_ge(g_["p"], value(act, step.solve + l + 1))
                    act.activation(pp[0:n, 0:4 * n], ps[0:n, 6, 0:4 * n], ACT.Copy).then_inc(g_["pc"], 1)
                act.wait_ge(g_["rtt"], value(act, o + 1))
                act.activation(rr[0:n, :], ps[0:n, 4, :], ACT.Copy).then_inc(g_["r"], 1)
                act.wait_ge(g_["up"], value(act, o + 1))
                act.activation(uu[0:n, :], ps[0:n, 5, :], ACT.Copy).then_inc(g_["u"], 1)
                act.wait_ge(g_["o"], value(act, o + 1))
                act.activation(proj[:, GV:GV + 4, step.cols], view(ps[:, 6, :], 4, n), ACT.Copy).then_inc(g_["oc"], 1)

            def gla(step):
                n, o = step.n, step.once
                for a, (want, done, func, scale, bias) in enumerate((
                        ("zt", "a1", ACT.Abs, 1.0, 0.0), ("a1", "a2", ACT.Exp, -1.0, 0.0), ("a2", "a3", ACT.Ln, 1.0, 1.0))):
                    act.wait_ge(l_[want], value(act, o + 1))
                    act.activation(la[0:n, :], (lz if a == 0 else la)[0:n, :], func, scale=scale, bias=bias).then_inc(l_[done], 1)
                act.wait_ge(l_["b"], value(act, o + 1))
                act.activation(lbt[:, 0:2 * n], ps[:, 1, 0:2 * n], ACT.Copy)
                act.activation(leb[:, 0:2 * n], ps[:, 1, 0:2 * n], ACT.Exp)
                act.activation(ler[:, 0:2 * n], ps[:, 1, 2 * n:4 * n], ACT.Exp).then_inc(l_["bt"], 1)
                act.wait_ge(l_["vtp"], value(act, o + 1))
                act.activation(lvt[0:n, :], ps[0:n, 4, :], ACT.Copy).then_inc(l_["vt"], 1)
                act.wait_ge(l_["kdp"], value(act, o + 1))
                act.activation(lkt[0:n, :], ps[0:n, 5, 0:256], ACT.Copy).then_inc(l_["kt"], 1)
                act.wait_ge(l_["dl"], value(act, o + 1))
                d = ldl[:, 0:step.levels, 0:2 * n]
                act.activation(d, d, ACT.Abs).then_inc(l_["d1"], 1)
                act.wait_ge(l_["d1"], value(act, o + 1))
                act.activation(d, d, ACT.Exp, scale=-1.0).then_inc(l_["d2"], 1)
                act.wait_ge(l_["o"], value(act, o + 1))
                for e in range(2):
                    last = act.activation(proj[:, LV + e:LV + 4:2, step.cols], view(ps[:, 6 + e, :], 2, n), ACT.Copy)
                last.then_inc(l_["oc"], 1)

            def ssd(step):
                n, o = step.n, step.once
                act.wait_ge(n_["lo"], value(act, step.layer * 3 + 2))
                act.wait_ge(s_["s"], further(act, o + 1))
                act.wait_ge(s_["yc"], further(act, o + 1))
                act.activation(view(sxbc, 8, n), proj[:, SX:SX + 8, step.cols], ACT.Copy).then_inc(s_["st"], 1)
                common(step, False)
                act.wait_ge(both["bc"], value(act, step.both + 1))
                act.activation(sea[:, 0:8 * n].rearrange("p (b c) -> p b c", b=2), ps[:, 0:2, 0:4 * n], ACT.Exp).then_inc(s_["ea"], 1)
                act.wait_ge(s_["tr"], value(act, o + 1))
                act.activation(sbt[0:n, 0:256], ps[0:n, 4, 0:256], ACT.Copy).then_inc(s_["bt"], 1)
                act.wait_ge(both["d"], value(act, step.both + 1))
                act.activation(sdd[0:n, 0:8 * n], sdd[0:n, 0:8 * n], ACT.Exp).then_inc(both["dx"], 1)

            def branch_norm(layer, b):
                last = (g_, l_)[b]["oc"] if b < 2 else n_["yz"]
                if b < 2:
                    act.wait_ge(last, value(act, layer * STEPS + (STEPS + 1)))
                    act.wait_ge((g_, l_)[b]["s"], further(act, layer * STEPS + (STEPS + 1)))
                else:
                    act.wait_ge(last, further(act, layer + 1))
                act.wait_ge(st_out, further(act, layer * 96 + 32 * b + 32))
                src = proj[:, (GV, LV, SX)[b]:(GV, LV, SX)[b] + 4, :]
                act.activation(nsq[:, :, :], src, ACT.Square).then_inc(n_["sq"], 1)
                act.wait_ge(n_["ss"], value(act, layer * 3 + b + 1))
                k = 4 if b < 2 else 2
                o = nrs[:, 0:k, :].rearrange("p k (a t) -> p (k a) t", a=2)
                act.activation(o, ps[:, 0:2 * k, 0:HALF], ACT.Ln, scale=1.0 / (128 if b < 2 else 256), bias=epsc).then_inc(n_["ln"], 1)
                act.wait_ge(n_["ln"], value(act, layer * 3 + b + 1))
                act.activation(nrs[:, 0:k, :], nrs[:, 0:k, :], ACT.Exp, scale=-0.5).then_inc(n_["rs"], 1)
                act.wait_ge(n_["tz"], value(act, layer * 3 + b + 1))
                act.activation(oh[b][:, :, :], nt[:, :, :], ACT.Copy).then_inc(n_["hi"], 1)

            def save_states(layer, b):
                s = (g_, l_, s_)[b]
                act.wait_ge(s["s"], value(act, layer * STEPS + (STEPS + 1)))
                name = ("gdn", "gla", "ssd")[b]
                cols = (512, 256, 512)[b]
                live = (gs, ls, ss_)[b]
                act.dma_start(io["out_p_" + name][bass.ds(layer, 1)].rearrange("a p n -> (a p) n"), live[:, 0:cols]).then_inc(st_out, 16)
                act.dma_start(io["out_s_" + name][bass.ds(layer, 1)].rearrange("a p b n -> (a p) b n"),
                              states[:, :, 0:cols]).then_inc(st_out, 16)

            def load_states(layer, b):
                name = ("gdn", "gla", "ssd")[b]
                cols = (512, 256, 512)[b]
                act.dma_start(states[:, :, 0:cols], io["in_" + name][bass.ds(layer, 1)].rearrange("a p b n -> (a p) b n")).then_inc(st_in, 16)

            def save_conv(layer):
                act.wait_ge(conv_done, value(act, layer * CONV_TILES + CONV_TILES))
                act.dma_start(io["out_p_conv"][bass.ds(layer, 1)].rearrange("a p t c -> (a p) t c"), cs_p[:, :, :]).then_inc(cs_saved, 16)
                act.dma_start(io["out_s_conv"][bass.ds(layer, 1)].rearrange("a p t n -> (a p) t n"),
                              cs_s[:, :, :, :].rearrange("p t b c -> p t (b c)")).then_inc(cs_saved, 16)

            def project(layer):
                def block_in(i, first, j):
                    act.wait_ge(blk_done, value(act, layer * BLOCKS + i * 4 + (B_PROJ + 4 + 4 * first + j + 1 + SPLIT)))

                def by_batch(a):
                    return a.rearrange("p (b s) -> p b s", s=3 + DEC_SEQ)

                def conv_group(i, first, tile, number):
                    def silu(j):
                        act.wait_ge(conv_done, value(act, layer * CONV_TILES + i * 4 + (number + j + 1)))
                        t = bass.ds(i * 4 + (tile + j), 1)
                        act.activation(proj[:, t, 0:SEQ].rearrange("p k t -> p (k t)"), cacc[:, j % 2, 0:SEQ],
                                       ACT.Silu, bias=cb[:, j:j + 1])
                        act.activation(proj[:, t, SEQ:T].rearrange("p k (b s) -> p (k b) s", s=DEC_SEQ),
                                       by_batch(cacc[:, j % 2, 3 + SEQ:PADW])[:, :, 0:DEC_SEQ],
                                       ACT.Silu, bias=cb[:, j:j + 1]).then_inc(csil_done, 1)

                    for j in range(4):
                        block_in(i, first, j)
                        a, b = ps[:, 2 * j, :], ps[:, 2 * j + 1, :]
                        s = by_batch(pad[:, j, 3 + SEQ:PADW])
                        act.activation(pad[:, j, 3:3 + HALF], a[:, 0:HALF], ACT.Copy)
                        act.activation(pad[:, j, 3 + HALF:3 + SEQ], b[:, 0:SEQ - HALF], ACT.Copy)
                        act.activation(s[:, :, 0:3], cs_in[:, bass.ds(i * 4 + (number + j), 1), :, :].rearrange(
                            "p k b c -> p (k b) c"), ACT.Copy)
                        act.activation(s[:, :, 3:], b[:, SEQ - HALF:HALF].rearrange("p (b s) -> p b s", s=DEC_SEQ),
                                       ACT.Copy).then_inc(evict_done, 1)
                        if j:
                            silu(j - 1)
                    silu(3)

                def direct_group(i, first, tile, func):
                    for j in range(4):
                        block_in(i, first, j)
                        act.activation(proj[:, bass.ds(i * 4 + (tile + j), 1), :].rearrange("p k (a t) -> p (k a) t", a=2),
                                       pair(j), func).then_inc(evict_done, 1)

                act.wait_ge(blk_done, value(act, layer * BLOCKS + (B_PROJ + 4 + SPLIT)))
                act.activation(halves(proj[:, SMALL, :]), pair(0), ACT.Copy).then_inc(small_done, 1)
                act.wait_ge(cs_loaded, value(act, layer * 16 + 16))
                act.wait_ge(pad_zero, further(act, layer + 1))
                with act.Fori(0, 3) as i:
                    conv_group(i, 0, GQ, 0)
                direct_group(0, 3, GZ, ACT.Silu)
                with act.Fori(0, 2) as i:
                    direct_group(i, 4, LQ, ACT.Copy)
                direct_group(0, 6, LG, ACT.Silu)
                direct_group(0, 7, SZ, ACT.Silu)
                with act.Fori(0, 2) as i:
                    conv_group(i, 8, SX, 12)

            with act.Fori(0, DEPTH) as layer:
                act.wait_ge(prm_in, value(act, layer * 16 + 16))
                ffn(layer, 0, B_FFN1)
                pre_norm(layer, 2, 1)
                act.wait_ge(hl_ready, value(act, layer * (4 * KD) + 2 * KD))
                act.dma_start(cs_in[:, :, :, :].rearrange("p t b c -> p (t b c)"),
                              io["in_conv"][bass.ds(layer, 1)].rearrange("a p n -> (a p) n")).then_inc(cs_loaded, 16)
                project(layer)
                save_conv(layer)
                act.preload_act_table_set(LN_EXP)
                act.wait_ge(cs_saved, value(act, layer * 32 + 32))
                load_states(layer, 0)
                act.activation(nega[:, :], prm[:, ALOG:ALOG + 1], ACT.Exp).then_inc(narrow["alog"], 1)
                for want, done, src, dst, func, scale, bias in (
                        ("z", "abs", sp, se, ACT.Abs, 1.0, 0.0), ("abs", "exp", se, se, ACT.Exp, -1.0, 0.0),
                        ("exp", "ln", se, sl, ACT.Ln, 1.0, 1.0)):
                    act.wait_ge(narrow[want], value(act, layer + 1))
                    act.activation(dst[:, :], src[:, :], func, scale=scale, bias=bias).then_inc(narrow[done], 1)
                act.wait_ge(narrow["g"], value(act, layer + 1))
                act.activation(cm[32:64, :], sp[32:64, :], ACT.Exp, scale=-1.0).then_inc(narrow["beta"], 1)
                for b, chunk in enumerate((gdn, gla, ssd)):
                    with act.Fori(0, CHUNKS) as c:
                        chunk(prompt_step(layer, b, c))
                    chunk(sample_step(layer, b))
                    save_states(layer, b)
                    branch_norm(layer, b)
                    if b < 2:
                        load_states(layer, b + 1)
                split_h(layer, 2)
                with act.Fori(0, KD // 2) as i:
                    for u in range(6):
                        if u == 0:
                            act.wait_ge(bm_ready, value(act, layer * 4 + i + 1))
                        act.wait_ge(blk_done, further(act, layer * BLOCKS + i * 12 + (B_MERGE + 2 * u + 1 + SPLIT)))
                        act.wait_ge(mac_done, further(act, layer * 24 + i * 6 + (u + 1)))
                        act.activation(halves(sg[:, u % 2, :]), pair(2 * u % 4), ACT.Sigmoid,
                                       bias=bm[:, u % 3 * 2 + u // 3:u % 3 * 2 + u // 3 + 1]).then_inc(sg_done, 1)
                        if u % 3 == 2:
                            act.wait_ge(mac_done, value(act, layer * 24 + i * 6 + (u + 3)))
                            act.activation(mh[:, bass.ds(i * 2 + u // 3, 1), :].rearrange("p k t -> p (k t)"),
                                           mac[:, u // 3, :], ACT.Copy).then_inc(mh_done, 1)
                reduce_out(layer, 3, B_OUT, 1)
                ffn(layer, 1, B_FFN2)

        @block.vector
        def _(dve):
            for n, (s, free) in enumerate(((blk_done, SPLIT), (sil_done, 2), (prod_done, 2), (out_done, 2),
                                           (evict_done, 4), (csil_done, 2), (sg_done, 2), (mac_done, 2),
                                           (lo_done, RAW), (x_done, 1), (g_["s"], 1), (l_["s"], 1),
                                           (s_["s"], 1), (g_["oc"], 1), (l_["oc"], 1))):
                dve.memset(cw[:, n:n + 1], 0.0).then_inc(s, free)
            dve.memset(cb[:, 0:1], 0.0).then_inc(s_["yc"], 1)
            dve.memset(cb[:, 1:2], 0.0).then_inc(started, 1)
            dve.wait_ge(loaded, 32)

            def split_in(layer, number, wcol):
                def low(k):
                    dve.wait_ge(hh_ready, value(dve, layer * (4 * KD) + (number * KD + k + 1)))
                    dve.tensor_tensor(hl[:, k, :], hf[:, k, :], hh[:, k, :].bitcast(F32), SUB).then_inc(hl_ready, 1)

                for k in range(KD):
                    dve.scalar_tensor_tensor(out=hf[:, k, :], in0=x[:, k, :], scalar=prm[:, wcol + k:wcol + k + 1],
                                             in1=rstd[:, :], op0=MULT, op1=MULT).then_inc(hf_ready, 1)
                    if k:
                        low(k - 1)
                low(KD - 1)

            def pre_norm(layer, stage, number, wcol):
                dve.wait_ge(rstd_ready, value(dve, layer * 6 + (stage + 1)))
                dve.wait_ge(x_done, further(dve, layer * (3 * KD) + (stage // 2 * KD + 1)))
                split_in(layer, number, wcol)

            def post_norm(layer, stage, wcol, scale):
                q = stage // 2
                dve.wait_ge(rstd_ready, value(dve, layer * 6 + (stage + 1)))
                for k in range(KD):
                    dve.scalar_tensor_tensor(out=f[:, k, :], in0=f[:, k, :], scalar=prm[:, wcol + k:wcol + k + 1],
                                             in1=rstd_post[:, :], op0=MULT, op1=MULT).then_inc(x_tmp, 1)
                for k in range(KD):
                    dve.wait_ge(x_tmp, value(dve, layer * (3 * KD) + (q * KD + k + 1)))
                    dve.scalar_tensor_tensor(out=x[:, k, :], in0=f[:, k, :], scalar=scale, in1=x[:, k, :],
                                             op0=MULT, op1=ADD).then_inc(x_done, 1)

            def ffn(layer, which, first, wpre, wpost):
                pre_norm(layer, 4 * which, 3 * which, wpre)
                with dve.Fori(0, KF // 2) as i:
                    for j in range(2):
                        n = layer * (2 * KF) + i * 2 + (which * KF + j)
                        dve.wait_ge(blk_done, value(dve, layer * BLOCKS + i * 4 + (first + 2 * j + 2 + SPLIT)))
                        dve.wait_ge(sil_done, further(dve, n + 3))
                        dve.tensor_tensor(halves(prod[:, j, :]), halves(sil[:, j, :]), pair(2 * j + 1), MULT).then_inc(prod_done, 1)
                        dve.wait_ge(prod_done, value(dve, n + 3))
                        dve.wait_ge(ah_done, further(dve, n + 1))
                        m = bass.ds(i * 2 + j, 1)
                        dve.tensor_tensor(al[:, m, :].rearrange("p k t -> p (k t)"), prod[:, j, :],
                                          ah[:, m, :].rearrange("p k t -> p (k t)").bitcast(F32), SUB).then_inc(al_done, 1)
                post_norm(layer, 4 * which + 1, wpost, 0.5)

            def project(layer):
                def conv_group(i, first, number):
                    c0 = layer * CONV_TILES + i * 4 + number
                    dve.wait_ge(csil_done, value(dve, c0 + 2))
                    dve.tensor_copy(cw[:, :], prm[:, bass.ds(i * 16 + (CONVW + 4 * number), 16)])
                    dve.tensor_copy(cb[:, :], prm[:, bass.ds(i * 4 + (CONVB + number), 4)]).then_inc(cw_ready, 1)
                    dve.wait_ge(cw_ready, value(dve, layer * 5 + i + (number // 4 + 1)))
                    for j in range(4):
                        dve.wait_ge(evict_done, value(dve, layer * 40 + i * 4 + (4 * first + j + 5)))
                        dve.wait_ge(csil_done, further(dve, c0 + j + 1))
                        a = cacc[:, j % 2, 0:CW]
                        dve.tensor_scalar(a, pad[:, j, 0:CW], cw[:, 4 * j:4 * j + 1], None, MULT).then_inc(tap, 1)
                        for t in range(1, CONV):
                            dve.wait_ge(tap, value(dve, c0 * 3 + 3 * j + t))
                            last = dve.scalar_tensor_tensor(out=a, in0=pad[:, j, t:t + CW],
                                                            scalar=cw[:, 4 * j + t:4 * j + t + 1], in1=a,
                                                            op0=MULT, op1=ADD)
                            if t < CONV - 1:
                                last.then_inc(tap, 1)
                        tile = bass.ds(i * 4 + (number + j), 1)
                        dve.tensor_copy(cs_p[:, tile, :].rearrange("p k c -> p (k c)"), pad[:, j, SEQ:SEQ + 3])
                        dve.tensor_copy(cs_s[:, tile, :, :].rearrange("p k b c -> p (k b) c"),
                                        pad[:, j, 3 + SEQ:PADW].rearrange("p (b s) -> p b s", s=3 + DEC_SEQ)
                                        [:, :, DEC_SEQ:]).then_inc(conv_done, 1)

                dve.memset(pad[:, :, 0:3], 0.0).then_inc(pad_zero, 1)
                with dve.Fori(0, 3) as i:
                    conv_group(i, 0, 0)
                with dve.Fori(0, 2) as i:
                    conv_group(i, 8, 12)

            def narrow_columns(layer):
                dve.wait_ge(small_done, value(dve, layer + 1))
                dve.wait_ge(narrow["alog"], further(dve, layer + 1))
                dve.tensor_scalar(nega[:, :], nega[:, :], -1.0, None, MULT)
                dve.tensor_scalar(sp[:, :], proj[:, SMALL, :], prm[:, SIGN:SIGN + 1], prm[:, SBIAS:SBIAS + 1],
                                  MULT, ADD).then_inc(narrow["z"], 1)
                dve.wait_ge(narrow["ln"], value(dve, layer + 1))
                dve.scalar_tensor_tensor(out=sp[:, :], in0=sp[:, :], scalar=0.0, in1=sl[:, :], op0=MAX, op1=ADD).then_inc(narrow["sp"], 1)
                dve.wait_ge(narrow["sp"], value(dve, layer + 1))
                dve.tensor_scalar(cm[:, :], sp[:, :], nega[:, 0:1], None, MULT).then_inc(narrow["g"], 1)
                dve.wait_ge(narrow["g"], value(dve, layer + 1))
                dve.tensor_copy(cm[96:128, :], sp[64:96, :]).then_inc(narrow["dt"], 1)
                dve.wait_ge(narrow["beta"], value(dve, layer + 1))
                dve.wait_ge(narrow["dt"], further(dve, layer + 1))

            def view(a, k):
                return a.rearrange("p (k t) -> p k t", k=k)

            def over(a, k):
                n, m = a.shape
                return a.rearrange("p (k t) -> p k t", k=1).to_broadcast([n, k, m])

            def each(a, m):
                n, k = a.shape
                return a.rearrange("p (k t) -> p k t", t=1).to_broadcast([n, k, m])

            def tri_of(step):
                return tri if step.prompt else cst[0:SAMPLE, TRI_S:TRI_S + SAMPLE]

            def copy_narrow(step):
                dve.tensor_copy(cc[:, 0:step.n], cm[:, step.cols]).then_inc(both["cc"], 1)

            def gdn(step):
                n, o = step.n, step.once
                w = HEADS * n
                dve.wait_ge(g_["oc"], value(dve, o + 1))
                dve.wait_ge(g_["s"], further(dve, o + 1))
                copy_narrow(step)
                dve.wait_ge(both["br"], value(dve, step.both + 1))
                dve.wait_ge(both["cc"], further(dve, step.both + 1))
                dve.tensor_copy(br[32:64, 0:n], cc[32:64, 0:n]).then_inc(g_["brb"], 1)
                dve.wait_ge(g_["rs"], value(dve, o + 1))
                dve.tensor_tensor(view(kn[:, 0:w], 4), proj[:, GK:GK + 4, step.cols], view(rs8[:, w:2 * w], 4), MULT)
                dve.scalar_tensor_tensor(out=view(qn[:, 0:w], 4), in0=proj[:, GQ:GQ + 4, step.cols], scalar=GDN_SCALE,
                                         in1=view(rs8[:, 0:w], 4), op0=MULT, op1=MULT).then_inc(g_["qk"], 1)
                dve.wait_ge(both["bc"], value(dve, step.both + 1))
                dve.wait_ge(g_["eg"], further(dve, o + 1))
                for h in range(HEADS):
                    last = dve.tensor_scalar(dd[0:n, h * n:(h + 1) * n], ps[0:n, 2, h * n:(h + 1) * n],
                                             gc[0:n, ROW_A + h:ROW_A + h + 1], 0.0, SUB, MIN)
                last.then_inc(both["d"], 1)
                dve.tensor_copy(view(xx[0:n, 0:w], 4), over(ident[0:n, 0:n], 4))
                dve.tensor_copy(view(xt[0:n, 0:w], 4), over(ident[0:n, 0:n], 4)).then_inc(g_["xi"], 1)
                dve.wait_ge(g_["qk"], value(dve, o + 1))
                dve.tensor_tensor(kg[:, 0:w], kn[:, 0:w], eg[:, 0:w], MULT)
                dve.tensor_tensor(qg[:, 0:w], qn[:, 0:w], eg[:, 0:w], MULT).then_inc(g_["kg"], 1)
                dve.wait_ge(g_["kt"], value(dve, o + 1))
                dve.tensor_tensor(view(kd[0:n, :], 4), view(ps[0:n, 7, :], 4), each(rg[0:n, ROW_A:ROW_A + 4], P), MULT).then_inc(g_["kd"], 1)
                dve.wait_ge(both["dx"], value(dve, step.both + 1))
                dve.tensor_tensor(view(dd[0:n, 0:w], 4), view(dd[0:n, 0:w], 4), over(tri_of(step), 4), MULT).then_inc(both["dm"], 1)
                dve.wait_ge(g_["kk"], value(dve, o + 1))
                dve.wait_ge(both["dm"], further(dve, step.both + 1))
                dve.tensor_tensor(att[0:n, 0:w], ps[0:n, 5, 0:w], dd[0:n, 0:w], MULT)
                dve.tensor_tensor(aa[0:n, 0:w], ps[0:n, 4, 0:w], dd[0:n, 0:w], MULT).then_inc(g_["at"], 1)
                dve.wait_ge(g_["at"], value(dve, o + 1))
                dve.tensor_tensor(aa[0:n, 0:w], ps[0:n, 3, 0:w], aa[0:n, 0:w], MULT).then_inc(g_["atb"], 1)
                dve.wait_ge(g_["atb"], value(dve, o + 1))

                def level(l):
                    m = cst[0:n, MASK + l * P:MASK + l * P + n]
                    dve.tensor_tensor(view(al_[0:n, 0:w], 4), view(aa[0:n, 0:w], 4), over(m, 4), MULT).then_inc(g_["al"], 1)

                level(0)
                for l in range(step.levels):
                    dve.wait_ge(g_["p"], value(dve, step.solve + l + 1))
                    if l < step.levels - 1:
                        level(l + 1)
                    dve.wait_ge(g_["q"], value(dve, step.solve + l + 1))
                    if l:
                        dve.wait_ge(g_["x"], further(dve, step.solve + l))
                    else:
                        dve.wait_ge(g_["xi"], further(dve, o + 1))
                    if l < step.levels - 1:
                        dve.tensor_tensor(xx[0:n, 0:w], xx[0:n, 0:w], ps[0:n, 7, 0:w], SUB)
                    dve.tensor_tensor(xt[0:n, 0:w], xt[0:n, 0:w], ps[0:n, 2, 0:w], SUB).then_inc(g_["x"], 1)
                dve.wait_ge(g_["x"], value(dve, step.solve + step.levels))
                dve.tensor_tensor(view(xt[0:n, 0:w], 4), view(xt[0:n, 0:w], 4), each(tm[0:n, ROW_B:ROW_B + 4], n), MULT).then_inc(g_["tb"], 1)
                dve.wait_ge(g_["sk"], value(dve, o + 1))
                dve.tensor_tensor(view(rt[:, 0:w], 4), proj[:, GV:GV + 4, step.cols], view(ps[:, 3, 0:w], 4), SUB).then_inc(g_["rt"], 1)
                if step.prompt:
                    dve.wait_ge(g_["su"], value(dve, step.update + 1))
                    for h in range(HEADS):
                        s = gs[:, h * P:(h + 1) * P]
                        last = dve.scalar_tensor_tensor(out=s, in0=s, scalar=eg[:, h * n + n - 1:h * n + n],
                                                        in1=ps[:, 0, h * P:(h + 1) * P], op0=MULT, op1=ADD)
                    last.then_inc(g_["s"], 1)
                else:
                    dve.wait_ge(g_["u"], value(dve, o + 1))
                    for h in range(HEADS):
                        dve.tensor_tensor(view(uexp[0:n, :], 8), over(uu[0:n, h * P:(h + 1) * P], 8),
                                          each(cst[0:n, BMASK:BMASK + 8], P), MULT).then_inc(g_["ue"], 1)
                        dve.wait_ge(g_["su"], value(dve, step.update + h + 1))
                        s = states[:, :, h * P:(h + 1) * P]
                        dve.tensor_tensor(s, s, each(eg[:, h * n + 3:(h + 1) * n:4], P), MULT).then_inc(g_["sm"], 1)
                        dve.wait_ge(g_["sm"], value(dve, step.layer * HEADS + h + 1))
                        last = dve.tensor_tensor(s, s, ps[:, 0:2, :].rearrange("p a (b m) -> p (a b) m", m=P), ADD)
                    last.then_inc(g_["s"], 1)

            def gla(step):
                n, o = step.n, step.once
                w = 2 * n
                dve.wait_ge(l_["oc"], value(dve, o + 1))
                dve.wait_ge(l_["s"], further(dve, o + 1))
                dve.tensor_copy(lrc[96:128, 0:n], proj[96:128, SMALL, step.cols]).then_inc(l_["rc"], 1)
                dve.tensor_copy(view(lvc[:, 0:4 * n], 4), proj[:, LV:LV + 4, step.cols]).then_inc(l_["vc"], 1)
                dve.memset(latt[0:n, 0:4 * n], 0.0).then_inc(l_["a0"], 1)
                dve.tensor_scalar(view(lqs[:, 0:w], 2), proj[:, LQ:LQ + 2, step.cols], GLA_SCALE, None, MULT)
                dve.tensor_copy(view(lks[:, 0:w], 2), proj[:, LK:LK + 2, step.cols]).then_inc(l_["qk"], 1)
                dve.wait_ge(l_["z"], value(dve, o + 1))
                dve.tensor_tensor(lz[0:n, :], ps[0:n, 0, 0:256], prm[0:n, GLAB:GLAB + 256], ADD).then_inc(l_["zt"], 1)
                dve.wait_ge(l_["a3"], value(dve, o + 1))
                dve.wait_ge(l_["zt"], further(dve, o + 1))
                dve.scalar_tensor_tensor(out=lgk[0:n, :], in0=lz[0:n, :], scalar=0.0, in1=la[0:n, :], op0=MIN, op1=SUB).then_inc(l_["g1"], 1)
                dve.wait_ge(l_["g1"], value(dve, o + 1))
                dve.tensor_scalar(lgk[0:n, :], lgk[0:n, :], 1.0 / GLA_NORMALIZER, None, MULT).then_inc(l_["gk"], 1)
                dve.wait_ge(l_["bt"], value(dve, o + 1))
                dve.wait_ge(l_["qk"], further(dve, o + 1))
                dve.tensor_tensor(lqe[:, 0:w], lqs[:, 0:w], leb[:, 0:w], MULT)
                dve.tensor_tensor(lkd[:, 0:w], lks[:, 0:w], ler[:, 0:w], MULT).then_inc(l_["qe"], 1)

                def by_block(a, m):
                    return a.rearrange("p (b s) -> p b s", s=2 * m)

                for l in range(step.levels):
                    m = 1 << l
                    b = by_block(lbt[:, 0:w], m)
                    last = dve.tensor_tensor(by_block(ldl[:, l, 0:w], m), b,
                                             b[:, :, m:m + 1].to_broadcast([P, w // (2 * m), 2 * m]), SUB)
                last.then_inc(l_["dl"], 1)
                dve.wait_ge(l_["d2"], value(dve, o + 1))
                for l in range(step.levels):
                    m = 1 << l
                    e, d = by_block(ldl[:, l, 0:w], m), by_block(lml[:, l, 0:w], m)
                    dve.tensor_tensor(d[:, :, 0:m], by_block(lks[:, 0:w], m)[:, :, 0:m], e[:, :, 0:m], MULT)
                    last = dve.tensor_tensor(d[:, :, m:], by_block(lqs[:, 0:w], m)[:, :, m:], e[:, :, m:], MULT)
                last.then_inc(l_["ml"], 1)
                dve.wait_ge(l_["a0"], value(dve, o + 1))
                for l in range(step.levels + 1):
                    dve.wait_ge(l_["at"], value(dve, step.score + l + 1))
                    if l:
                        dve.wait_ge(l_["cp"], further(dve, step.score + l))
                    c = MASK + l * P if l < step.levels else IDENT
                    for e in range(2):
                        last = dve.copy_predicated(view(latt[0:n, e * w:(e + 1) * w], 2), over(cst[0:n, c:c + n], 2).bitcast(U32),
                                                   view(ps[0:n, 2 - l % 2 * 2 + e, 0:w], 2))
                    last.then_inc(l_["cp"], 1)
                if step.prompt:
                    dve.wait_ge(l_["su"], value(dve, step.update + 1))
                    for g in range(2):
                        s = ls[:, g * P:(g + 1) * P]
                        last = dve.scalar_tensor_tensor(out=s, in0=s, scalar=leb[:, g * n + n - 1:g * n + n],
                                                        in1=ps[:, 4, g * P:(g + 1) * P], op0=MULT, op1=ADD)
                    last.then_inc(l_["s"], 1)
                else:
                    dve.wait_ge(l_["vt"], value(dve, o + 1))
                    for h in range(HEADS):
                        r, g = slice(64 * (h % 2), 64 * (h % 2) + 64), h // 2
                        dve.tensor_tensor(vexp[0:n, :, :], over(lvt[0:n, h * P:(h + 1) * P], 8),
                                          each(cst[0:n, BMASK:BMASK + 8], P), MULT).then_inc(l_["ve"], 1)
                        dve.wait_ge(l_["su"], value(dve, step.update + h + 1))
                        s = states[r, :, g * P:(g + 1) * P]
                        dve.tensor_tensor(s, s, each(leb[r, g * n + 3:(g + 1) * n:4], P), MULT).then_inc(l_["sm"], 1)
                        dve.wait_ge(l_["sm"], value(dve, step.layer * HEADS + h + 1))
                        last = dve.tensor_tensor(s, s, ps[r, 0:2, :].rearrange("p a (b m) -> p (a b) m", m=P), ADD)
                    last.then_inc(l_["s"], 1)

            def ssd(step):
                n, o = step.n, step.once
                w = SSD_HEADS * n
                dve.wait_ge(s_["yc"], value(dve, o + 1))
                dve.wait_ge(s_["s"], further(dve, o + 1))
                copy_narrow(step)
                dve.wait_ge(both["bc"], value(dve, step.both + 1))
                dve.wait_ge(s_["ea"], further(dve, o + 1))
                for h in range(SSD_HEADS):
                    last = dve.tensor_scalar(sdd[0:n, h * n:(h + 1) * n], ps[0:n, h // 4, h % 4 * n:(h % 4 + 1) * n],
                                             gc[0:n, ROW_DT + h:ROW_DT + h + 1], 0.0, SUB, MIN)
                last.then_inc(both["d"], 1)
                dve.wait_ge(s_["st"], value(dve, o + 1))
                for g in range(2):
                    c = slice(4 * g * n, 4 * (g + 1) * n)
                    last = dve.tensor_tensor(view(sce[:, c], 4), view(sea[:, c], 4), over(sxbc[:, (6 + g) * n:(7 + g) * n], 4), MULT)
                last.then_inc(s_["ce"], 1)
                dve.wait_ge(s_["tr"], value(dve, o + 1))
                dve.tensor_tensor(view(sxd[0:n, :], 8), view(ps[0:n, 3, :], 8), each(tm[0:n, 96:104], 64), MULT).then_inc(s_["xd"], 1)
                dve.wait_ge(s_["xd"], value(dve, o + 1))
                dve.wait_ge(both["rg"], further(dve, step.both + 1))
                dve.tensor_tensor(view(sxe[0:n, :], 8), view(sxd[0:n, :], 8), each(rg[0:n, ROW_DT:ROW_DT + 8], 64), MULT).then_inc(s_["xe"], 1)
                dve.wait_ge(both["dx"], value(dve, step.both + 1))
                dve.tensor_tensor(view(sdd[0:n, 0:w], 8), view(sdd[0:n, 0:w], 8), over(tri_of(step), 8), MULT).then_inc(both["dm"], 1)
                dve.wait_ge(both["dm"], value(dve, step.both + 1))
                for g in range(2):
                    c = slice(4 * g * n, 4 * (g + 1) * n)
                    last = dve.tensor_tensor(view(sdd[0:n, c], 4), view(sdd[0:n, c], 4), over(ps[0:n, 2, g * n:(g + 1) * n], 4), MULT)
                last.then_inc(s_["att"], 1)
                dve.wait_ge(s_["y"], value(dve, o + 1))
                for t in range(4):
                    last = dve.scalar_tensor_tensor(out=proj[:, SX + t, step.cols], in0=sxbc[:, t * n:(t + 1) * n],
                                                    scalar=prm[:, SSDD + t:SSDD + t + 1],
                                                    in1=ps[:, 5, t * n:(t + 1) * n], op0=MULT, op1=ADD)
                last.then_inc(s_["yc"], 1)
                if step.prompt:
                    dve.tensor_tensor(view(ss_[:, :], 8), view(ss_[:, :], 8), each(sea[:, n - 1:w:n], 64), MULT).then_inc(s_["sm"], 1)
                    dve.wait_ge(s_["su"], value(dve, step.update2 + 1))
                    dve.wait_ge(s_["sm"], further(dve, step.update2 + 1))
                    dve.tensor_tensor(ss_[:, :], ss_[:, :], ps[:, 6, :], ADD).then_inc(s_["s"], 1)
                else:
                    for g in range(2):
                        dve.tensor_tensor(view(xexp[0:n, :], 8), over(sxe[0:n, g * 256:(g + 1) * 256], 8),
                                          each(cst[0:n, BMASK:BMASK + 8], 256), MULT).then_inc(s_["xe2"], 1)
                        dve.wait_ge(s_["su"], value(dve, step.update2 + g + 1))
                        for h in range(4 * g, 4 * g + 4):
                            s = states[:, :, h * 64:(h + 1) * 64]
                            last = dve.tensor_tensor(s, s, each(sea[:, h * n + 3:(h + 1) * n:4], 64), MULT)
                        last.then_inc(s_["sm"], 1)
                        dve.wait_ge(s_["sm"], value(dve, step.update2 + g + 1))
                        s = states[:, :, g * 256:(g + 1) * 256]
                        last = dve.tensor_tensor(s, s, ps[:, 0:4, :].rearrange("p a (b m) -> p (a b) m", m=256), ADD)
                    last.then_inc(s_["s"], 1)

            def branch_norm(layer, b):
                if b == 2:
                    dve.wait_ge(s_["yc"], value(dve, layer * STEPS + (STEPS + 1)))
                    y = proj[:, SX:SX + 4, :]
                    dve.tensor_tensor(y, y, proj[:, SZ:SZ + 4, :], MULT).then_inc(n_["yz"], 1)
                    dve.wait_ge(n_["yz"], value(dve, layer + 1))
                dve.wait_ge(n_["rs"], further(dve, layer * 3 + b + 1))
                o = layer * 3 + b
                if b < 2:
                    c = (GDNN, GLAN)[b]
                    v = (GV, LV)[b]
                    for t in range(4):
                        last = dve.scalar_tensor_tensor(out=nt[:, t, :], in0=proj[:, v + t, :], scalar=prm[:, c:c + 1],
                                                        in1=nrs[:, t, :], op0=MULT, op1=MULT)
                    last.then_inc(n_["t"], 1)
                    dve.wait_ge(n_["t"], value(dve, layer * 2 + b + 1))
                    z = (GZ, LG)[b]
                    dve.tensor_tensor(nt[:, :, :], nt[:, :, :], proj[:, z:z + 4, :], MULT).then_inc(n_["tz"], 1)
                else:
                    for t in range(4):
                        last = dve.scalar_tensor_tensor(out=nt[:, t, :], in0=proj[:, SX + t, :],
                                                        scalar=prm[:, SSDN + t:SSDN + t + 1],
                                                        in1=nrs[:, t // 2, :], op0=MULT, op1=MULT)
                    last.then_inc(n_["tz"], 1)
                dve.wait_ge(n_["hi"], value(dve, o + 1))
                dve.wait_ge(n_["tz"], further(dve, o + 1))
                dve.tensor_tensor(ol[b][:, :, :], nt[:, :, :], oh[b][:, :, :].bitcast(F32), SUB).then_inc(n_["lo"], 1)
                dve.wait_ge(n_["lo"], value(dve, o + 1))

            with dve.Fori(0, DEPTH) as layer:
                dve.wait_ge(prm_in, value(dve, layer * 16 + 16))
                ffn(layer, 0, B_FFN1, F1PRE, F1POST)
                pre_norm(layer, 2, 1, MPRE)
                project(layer)
                dve.wait_ge(evict_done, value(dve, layer * 40 + 44))
                narrow_columns(layer)
                for b, (chunk, state) in enumerate(((gdn, gs), (gla, ls), (ssd, ss_))):
                    dve.memset(state[:, :], 0.0).then_inc(zeroed, 1)
                    with dve.Fori(0, CHUNKS) as c:
                        chunk(prompt_step(layer, b, c))
                    chunk(sample_step(layer, b))
                    branch_norm(layer, b)
                dve.wait_ge(st_out, value(dve, layer * 96 + 96))
                split_in(layer, 2, MPRE)
                with dve.Fori(0, KD // 2) as i:
                    dve.wait_ge(sg_done, value(dve, layer * 24 + i * 6 + 2))
                    dve.tensor_copy(bm[:, :].rearrange("p (r k) -> p r k", k=2),
                                    prm[:, BMERGE:BMERGE + 24].rearrange("p (r m) -> p r m", m=8)
                                    [:, :, bass.ds(i * 2, 2)]).then_inc(bm_ready, 1)
                    for u in range(6):
                        r, k = u % 3, u // 3
                        dve.wait_ge(blk_done, value(dve, layer * BLOCKS + i * 12 + (B_MERGE + 2 * u + 2 + SPLIT)))
                        dve.wait_ge(sg_done, further(dve, layer * 24 + i * 6 + (u + 3)))
                        dve.wait_ge(mac_done, further(dve, layer * 24 + i * 6 + (u + 2)))
                        dst = mac[:, k, :] if r == 0 else mt_[:, 0, :]
                        last = dve.tensor_tensor(halves(dst), halves(sg[:, u % 2, :]), pair((2 * u + 1) % 4), MULT)
                        if r:
                            last.then_inc(mac_tmp, 1)
                            dve.wait_ge(mac_tmp, value(dve, layer * 16 + i * 4 + (2 * k + r)))
                            last = dve.tensor_tensor(mac[:, k, :], mac[:, k, :], mt_[:, 0, :], ADD)
                        last.then_inc(mac_done, 1)
                        if r == 2:
                            dve.wait_ge(mac_done, value(dve, layer * 24 + i * 6 + (u + 3)))
                            dve.wait_ge(mh_done, further(dve, layer * KD + i * 2 + (k + 1)))
                            m = bass.ds(i * 2 + k, 1)
                            dve.tensor_tensor(ml[:, m, :].rearrange("p k t -> p (k t)"), mac[:, k, :],
                                              mh[:, m, :].rearrange("p k t -> p (k t)").bitcast(F32), SUB).then_inc(ml_done, 1)
                post_norm(layer, 3, MPOST, 1.0)
                ffn(layer, 1, B_FFN2, F2PRE, F2POST)


COLS = dict(qkv=0, z=1536, a=2048, b=2052, q=2056, r=3592, sz=3608, dt=5144, gate=5152)


def tiles(w):
    w = np.asarray(w)
    n, k, m = w.shape
    return np.ascontiguousarray(w.reshape(n, k // P, P, m // P, P).transpose(0, 3, 2, 1, 4).reshape(n * m // P, P, k))


def pack(a):
    a = {k: np.asarray(v) for k, v in a.items()}
    out = {}
    tokens = np.concatenate([a["x_prompt"].reshape(SEQ, D_MODEL), a["x_sample"].reshape(SAMPLE, D_MODEL)])
    out["x"] = tokens.T.reshape(KD, P, T).transpose(1, 0, 2).reshape(P, KD * T)

    ups, downs = [], []
    for l in range(DEPTH):
        for f in ("ffn1", "ffn2"):
            g, u = tiles(a[f + "_w_gate"][l:l + 1]), tiles(a[f + "_w_up"][l:l + 1])
            ups.append(np.stack([g, u], 1).reshape(UPS, P, D_MODEL))
            downs.append(tiles(a[f + "_w_down"][l:l + 1]))
    out["up"], out["down"] = np.concatenate(ups), np.concatenate(downs)
    w = a["w_in"]
    wide = np.concatenate([w[:, :, COLS["qkv"]:COLS["a"]], w[:, :, COLS["q"]:COLS["r"]], w[:, :, COLS["sz"]:COLS["dt"]]], 2)
    out["win"] = tiles(wide)
    small = np.zeros((DEPTH, D_MODEL, P), w.dtype)
    small[:, :, ROW_A:ROW_A + 4] = w[:, :, COLS["a"]:COLS["a"] + 4]
    small[:, :, ROW_B:ROW_B + 4] = w[:, :, COLS["b"]:COLS["b"] + 4]
    small[:, :, ROW_DT:ROW_DT + 8] = w[:, :, COLS["dt"]:COLS["dt"] + 8]
    small[:, :, ROW_R:ROW_R + 16] = w[:, :, COLS["r"]:COLS["r"] + 16]
    out["narrow"] = tiles(small)
    gate = tiles(w[:, :, COLS["gate"]:]).reshape(DEPTH, 3, KD, P, D_MODEL)
    out["gate"] = gate.transpose(0, 2, 1, 3, 4).reshape(DEPTH * 24, P, D_MODEL)
    br = np.stack([tiles(a["w_br_" + s]).reshape(DEPTH, KD, P, 512) for s in ("gdn", "gla", "ssd")], 2)
    out["branch"] = br.reshape(DEPTH * 24, P, 512)
    out["wout"] = tiles(a["w_out"])

    prm = np.zeros((DEPTH, P, NPRM), np.float32)

    def cols(c, v):
        v = v.reshape(DEPTH, -1, P)
        prm[:, :, c:c + v.shape[1]] = v.transpose(0, 2, 1)

    for c, s in ((F1PRE, "ffn1_norm_pre"), (F1POST, "ffn1_norm_post"), (MPRE, "mix_norm_pre"), (MPOST, "mix_norm_post"),
                 (F2PRE, "ffn2_norm_pre"), (F2POST, "ffn2_norm_post"), (BMERGE, "b_merge"), (GDNN, "gdn_norm"),
                 (GLAN, "gla_norm"), (SSDN, "ssd_norm")):
        cols(c, a[s])
    conv = np.concatenate([a["gdn_conv_w"], a["ssd_conv_w"]], 1).reshape(DEPTH, CONV_TILES, P, CONV)
    prm[:, :, CONVW:CONVW + 80] = conv.transpose(0, 2, 1, 3).reshape(DEPTH, P, 80)
    cols(CONVB + 12, a["ssd_conv_b"])
    cols(SSDD, np.repeat(a["ssd_D"], 64, axis=1))
    prm[:, ROW_A:ROW_A + 4, SBIAS] = a["gdn_dt_bias"]
    prm[:, ROW_DT:ROW_DT + 8, SBIAS] = a["ssd_dt_bias"]
    prm[:, ROW_A:ROW_A + 4, ALOG] = a["gdn_A_log"]
    prm[:, ROW_DT:ROW_DT + 8, ALOG] = a["ssd_A_log"]
    prm[:, :, SIGN] = 1.0
    prm[:, ROW_B:ROW_B + 32, SIGN] = -1.0
    prm[:, :, GLAB:GLAB + 256] = a["gla_gate_bias"][:, None, :]
    prm[:, ROW_R:ROW_R + 16, GUP:GUP + 256] = a["gla_gate_up"]
    out["prm"] = prm

    cst = np.zeros((P, NCONST), np.float32)
    j, i = np.meshgrid(np.arange(P), np.arange(P), indexing="ij")
    cst[:, IDENT:IDENT + P] = j == i
    cst[:, TRI:TRI + P] = i >= j
    cst[:, REV:REV + P] = j > i
    for l in range(LEVELS):
        m = 1 << l
        cst[:, MASK + l * P:MASK + (l + 1) * P] = (j // (2 * m) == i // (2 * m)) & (j % (2 * m) < m) & (i % (2 * m) >= m)
    cst[:, ONES:ONES + P] = 1.0
    n = SAMPLE
    same = (j // DEC_SEQ == i // DEC_SEQ)[:n, :n]
    cst[:n, TRI_S:TRI_S + n] = same & (i >= j)[:n, :n]
    cst[:n, REV_S:REV_S + n] = same & (j > i)[:n, :n]
    cst[:n, BMASK:BMASK + 8] = np.arange(n)[:, None] // DEC_SEQ == np.arange(8)[None, :]
    cst[:, EPSC] = EPS
    cst[:, EPSROW] = EPS * D_MODEL / P
    out["cst"] = cst

    cs = np.concatenate([a["state_gdn_conv"], a["state_ssd_conv"]], 3)
    cs = cs.reshape(DEPTH, DEC_BATCH, 3, CONV_TILES, P).transpose(0, 4, 3, 1, 2)
    out["in_conv"] = cs.reshape(DEPTH, P, CONV_TILES * DEC_BATCH * 3)
    out["in_gdn"] = a["state_gdn"].transpose(0, 3, 1, 2, 4).reshape(DEPTH, P, DEC_BATCH, 512)
    gla = a["state_gla"].reshape(DEPTH, DEC_BATCH, 2, 2, 64, P)
    out["in_gla"] = gla.transpose(0, 3, 4, 1, 2, 5).reshape(DEPTH, P, DEC_BATCH, 256)
    out["in_ssd"] = a["state_ssd"].transpose(0, 4, 1, 2, 3).reshape(DEPTH, P, DEC_BATCH, 512)
    return {k: np.ascontiguousarray(v) for k, v in out.items()}


OUTS = {
    "y": (P, KD * T),
    "out_p_conv": (DEPTH, P, CONV_TILES, 3), "out_s_conv": (DEPTH, P, CONV_TILES, DEC_BATCH * 3),
    "out_p_gdn": (DEPTH, P, 512), "out_p_gla": (DEPTH, P, 256), "out_p_ssd": (DEPTH, P, 512),
    "out_s_gdn": (DEPTH, P, DEC_BATCH, 512), "out_s_gla": (DEPTH, P, DEC_BATCH, 256), "out_s_ssd": (DEPTH, P, DEC_BATCH, 512),
}


def unpack(r):
    y = r["y"].reshape(P, KD, T).transpose(2, 1, 0).reshape(T, D_MODEL)
    outs = [y[:SEQ].reshape(1, SEQ, D_MODEL), y[SEQ:].reshape(DEC_BATCH, DEC_SEQ, D_MODEL)]
    for k, nb in (("p", 1), ("s", DEC_BATCH)):
        conv = r[f"out_{k}_conv"].reshape(DEPTH, P, CONV_TILES, nb, 3).transpose(0, 3, 4, 2, 1).reshape(DEPTH, nb, 3, CONV_TILES * P)
        gdn = r[f"out_{k}_gdn"].reshape(DEPTH, P, nb, HEADS, P).transpose(0, 2, 3, 1, 4)
        gla = r[f"out_{k}_gla"].reshape(DEPTH, 2, 64, nb, 2, P).transpose(0, 3, 4, 1, 2, 5).reshape(DEPTH, nb, HEADS, 64, P)
        ssd = r[f"out_{k}_ssd"].reshape(DEPTH, P, nb, SSD_HEADS, 64).transpose(0, 2, 3, 4, 1)
        outs += [conv[..., :12 * P], gdn, gla, conv[..., 12 * P:], ssd]
    return tuple(np.ascontiguousarray(o) for o in outs)


def kernel(**inputs):
    import concourse.bacc as bacc
    from concourse.bass_utils import run_bass_kernel_spmd

    arrays = pack(inputs)
    nc = bacc.Bacc("TRN2", target_bir_lowering=False, num_devices=1)
    io = {k: nc.dram_tensor("in_" + k, v.shape, mybir.dt.from_np(v.dtype), kind="ExternalInput").ap() for k, v in arrays.items()}
    for k, shape in OUTS.items():
        io[k] = nc.dram_tensor("res_" + k, shape, F32, kind="ExternalOutput").ap()
    trunk(nc, io)
    r = run_bass_kernel_spmd(nc, [{"in_" + k: v for k, v in arrays.items()}], core_ids=[0])
    return unpack({k: r.results[0]["res_" + k] for k in OUTS})
```

```python
from contextlib import ExitStack

import concourse.bass as bass
import numpy as np
from concourse import mybir

P = 128
D_MODEL, DEPTH, D_FF = 1024, 2, 2816
SEQ, DEC_BATCH, DEC_SEQ = 512, 8, 4
SAMPLE = DEC_BATCH * DEC_SEQ
T = SEQ + SAMPLE
HALF = T // 2
KD = D_MODEL // P
KF = D_FF // P
EPS = 1e-6
C = 128
CHUNKS = SEQ // C
STEPS = CHUNKS + 1
HEADS = 4
SSD_HEADS = 8
GDN_SCALE, GLA_SCALE = 128 ** -0.5, 64 ** -0.5
GLA_NORMALIZER = 16.0
CONV = 4
LEVELS, SAMPLE_LEVELS = 7, 2

GQ, GK, GV, GZ = 0, 4, 8, 12
LQ, LK, LV, LG = 16, 18, 20, 24
SZ, SX, SB, SC = 28, 32, 36, 38
SMALL = 40
TILES = 41
CONV_TILES = 20
ROW_A, ROW_B, ROW_DT, ROW_R = 0, 32, 64, 96

(F1PRE, F1POST, MPRE, MPOST, F2PRE, F2POST) = range(0, 48, 8)
BMERGE, CONVW, CONVB = 48, 72, 152
GDNN, GLAN, SSDN, SSDD = 172, 173, 174, 178
SBIAS, ALOG, SIGN = 182, 183, 184
GLAB, GUP, NPRM = 192, 448, 704

IDENT, TRI, REV, MASK = 0, 128, 256, 384
ONES = MASK + LEVELS * 128
TRI_S, REV_S, BMASK, EPSC, EPSROW = ONES + 128, ONES + 160, ONES + 192, ONES + 200, ONES + 201
NCONST = ONES + 204

UPS, DOWNS = 2 * KF, 3 * KD
FFN_BLOCKS = UPS + DOWNS
B_FFN1, B_PROJ = 0, FFN_BLOCKS
B_MERGE = B_PROJ + 4 + 40
B_OUT = B_MERGE + 6 * KD
B_FFN2 = B_OUT + KD
BLOCKS = B_FFN2 + FFN_BLOCKS
RAW, SPLIT = 4, 2
DOWN_K = (8, 8, 6)
assert all(b % RAW == 0 for b in (B_PROJ, B_MERGE, B_OUT, B_FFN2, BLOCKS))

F32, F32R, U32 = mybir.dt.float32, mybir.dt.float32r, mybir.dt.uint32
ACT, ALU = mybir.ActivationFunctionType, mybir.AluOpType
MULT, ADD, SUB, MIN, MAX = ALU.mult, ALU.add, ALU.subtract, ALU.min, ALU.max
LN_EXP = "natural_log_exp_and_others"


SOLVES = CHUNKS * LEVELS + SAMPLE_LEVELS
SCORES = CHUNKS * (LEVELS + 1) + SAMPLE_LEVELS + 1
SUMS = (1, 3, 4, 6, 7, 9)


class Step:

    def __init__(self, layer, n, states, levels, cols, c):
        self.layer, self.n, self.states, self.levels = layer, n, states, levels
        self.cols = cols
        self.prompt = states == 1
        self.once = layer * STEPS + c
        self.solve = layer * SOLVES + c * LEVELS
        self.score = layer * SCORES + c * (LEVELS + 1)
        self.update = layer * (CHUNKS + HEADS) + c
        self.update2 = layer * (CHUNKS + 2) + c


def prompt_step(layer, c):
    return Step(layer, C, 1, LEVELS, bass.ds(c * C, C), c)


def sample_step(layer):
    return Step(layer, SAMPLE, DEC_BATCH, SAMPLE_LEVELS, slice(SEQ, T), CHUNKS)


COMMON_STAGES, GDN_STAGES, GLA_STAGES, SSD_STAGES = 3, 3 + 2 * LEVELS + 1, 5 + LEVELS + 3, 6
ORDER = "clclclg" + "gl" * 3 + "gslgslgslgslgslgslglglglglglglglggg"


def together(common, gdn, gla, ssd):
    branch = dict(c=common, g=gdn, l=gla, s=ssd)
    for name in ORDER:
        next(branch[name], None)
    for stages in branch.values():
        assert next(stages, "through") == "through"


def alone(*branches):
    for stages in branches:
        for _ in stages:
            pass


def trunk(nc, io):
    ctx = ExitStack()
    with ctx:
        base = -(-nc.sbuf_base // 64) * 64

        def at(name, offset, shape, dt=F32):
            return nc.alloc_sbuf_tensor_at(name, shape, dt, offset=base + offset)

        def sem(name):
            return ctx.enter_context(nc.semaphore(name))

        TB = T * 4
        place = [0]

        def put(name, shape, dt=F32):
            size = 4 * int(np.prod(shape[1:]))
            t = at(name, place[0], shape, dt)
            place[0] += -(-size // 32) * 32
            return t

        x = put("x", [P, KD, T])
        RING = place[0]
        raw = put("raw", [P, RAW, KD, P])
        wh = put("wh", [P, SPLIT, KD, P], F32R)
        wl = put("wl", [P, SPLIT, KD, P], F32R)
        cst = put("cst", [P, NCONST])
        prm = put("prm", [P, NPRM])
        rstd = put("rstd", [P, T])
        RSTD_POST = place[0]
        rstd_post = put("rstd_post", [P, T])
        nega = put("nega", [P, 1])
        cw = put("cw", [P, 16])
        cb = put("cb", [P, 4])
        bm = put("bm", [P, 6])
        R = place[0]
        assert base + R + 68 * TB <= nc.sbuf_usable_end, (base + R + 68 * TB, nc.sbuf_usable_end)

        def row(name, r, shape, dt=F32, more=0):
            return at(name, R + r * TB + more, shape, dt)

        hh, hl = row("hh", 0, [P, KD, T], F32R), row("hl", 8, [P, KD, T], F32R)
        ah, al = row("ah", 16, [P, KF, T], F32R), row("al", 38, [P, KF, T], F32R)
        f = row("f", 60, [P, KD, T])
        hf = row("hf", 60, [P, KD, T])
        sq = row("sq", 0, [P, KD, T])
        sil, prod = row("sil", 60, [P, 2, T]), row("prod", 62, [P, 2, T])
        proj = row("proj", 16, [P, TILES, T])
        PADW = 3 + SEQ + DEC_BATCH * (3 + DEC_SEQ)
        CW = PADW - 3
        pad = row("pad", 60, [P, 4, PADW])
        cacc = row("cacc", 57, [P, 2, PADW])
        cs_in = row("cs_in", 65, [P, CONV_TILES, DEC_BATCH, 3])
        cs_p = row("cs_p", 66, [P, CONV_TILES, 3])
        cs_s = row("cs_s", 66, [P, CONV_TILES, DEC_BATCH, 3], more=256)
        assert 4 * 4 * PADW <= 5 * TB and 2 * 4 * PADW <= 3 * TB
        sp, se, sl = row("sp", 57, [P, T]), row("se", 58, [P, T]), row("sl", 59, [P, T])
        cm = row("cm", 58, [P, T])
        cc, tm, gc = (row(s, 57, [P, P], more=512 * i) for i, s in enumerate(("cc", "tm", "gc")))
        br, rg = (row(s, 59, [P, P], more=512 * i) for i, s in enumerate(("br", "rg")))
        states = row("states", 60, [P, DEC_BATCH, 512])

        def work(name, k, units=1, dt=F32):
            return at(name, R + 2048 * k, [P, 512 * units], dt)

        (kn, qn, kg, qg, eg, dd, aa, att, al_, xx, xt, pp, rt, rr, uu, kd, gs) = (
            work(f"g{i}", i) for i in range(17))
        sq8, rs8 = work("sq8", 12, 2), work("rs8", 14, 2)
        uexp = work("uexp", 9, 2)
        gla_sample = dict(
            {n: at(f"t_{n}", R + 1024 * i, [P, 256]) for i, n in enumerate("z a gk bt eb er qs qe kd ks".split())},
            dl=at("t_dl", R + 10240, [P, LEVELS, 256]),
            **{n: at(f"t_{n}", R + 24576 + 2048 * i, [P, 512]) for i, n in enumerate(("att", "vc", "vt"))},
            kt=at("t_kt", R + 30720, [P, 256]), rc=at("t_rc", R + 32768, [P, P]))
        vexp = at("vexp", R + 17408, [P, DEC_BATCH, P])
        F0, W0 = R + 60 * TB, RING + 24576
        gla_prompt = dict(
            dl=at("l_dl", F0, [P, LEVELS, 256]),
            **{n: at(f"l_{n}", F0 + 7168 + 2048 * i, [P, 512]) for i, n in enumerate(("att", "vc", "vt"))},
            **{n: at(f"l_{n}", F0 + 13312 + 1024 * i, [P, 256]) for i, n in enumerate("z a gk bt".split())},
            **{n: at(f"l_{n}", W0 + 1024 * i, [P, 256]) for i, n in enumerate("eb er qs qe kd ks kt s".split())},
            rc=at("l_rc", RSTD_POST, [P, P]))
        ls = gla_prompt["s"]
        ssd_sample, ssd_prompt = (dict(
            {n: at(f"{w}_{n}", base_ + 4096 * i, [P, 1024]) for i, n in enumerate("xbc ea dd ce".split())},
            **{n: at(f"{w}_{n}", base_ + 16384 + 2048 * i, [P, 512]) for i, n in enumerate("xd xe s bt".split())})
            for w, base_ in (("u", R), ("s", RING)))
        ss_ = ssd_prompt["s"]
        xexp = work("xexp", 12, 4)
        nsq, nrs, nt = row("nsq", 0, [P, 4, T]), row("nrs", 4, [P, 4, T]), row("nt", 8, [P, 4, T])
        oh = [row(f"oh{i}", 16 + r, [P, 4, T], F32R) for i, r in enumerate((GQ, LQ, SB))]
        ol = [row(f"ol{i}", 16 + r, [P, 4, T], F32R) for i, r in enumerate((GK, LV, SX))]
        mh, ml = row("mh", 16 + GV, [P, KD, T], F32R), row("ml", 16 + LG, [P, KD, T], F32R)
        sg, mt_, mac = row("sg", 60, [P, 2, T]), row("mt", 62, [P, 1, T]), row("mac", 63, [P, 2, T])

        ps = ctx.enter_context(nc.psum_tensor("ps", [P, 8, 512], F32))

        ident, tri, rev = (cst[:, a:a + P] for a in (IDENT, TRI, REV))
        ones = cst[:, ONES:ONES + P]
        epsc = cst[:, EPSC:EPSC + 1]

        def pair(slot):
            return ps[:, 2 * slot:2 * slot + 2, 0:HALF]

        def halves(ap):
            return ap.rearrange("p (a t) -> p a t", a=2)

        started = sem("started")
        loaded = sem("loaded")
        prm_in = sem("prm_in")
        raw_full = [sem(f"raw_full{i}") for i in range(RAW)]
        hi_done, lo_done = sem("hi_done"), sem("lo_done")
        blk_done = sem("blk_done")
        sq_ready, sum_ready, ln_ready, rstd_ready = (sem(s) for s in ("sq_ready", "sum_ready", "ln_ready", "rstd_ready"))
        x_tmp, x_done = sem("x_tmp"), sem("x_done")
        hf_ready, hh_ready, hl_ready = sem("hf_ready"), sem("hh_ready"), sem("hl_ready")
        sil_done, prod_done = sem("sil_done"), sem("prod_done")
        ah_done, al_done = sem("ah_done"), sem("al_done")
        out_done = sem("out_done")
        evict_done, small_done = sem("evict_done"), sem("small_done")
        pad_zero, tap, conv_done, csil_done = (sem(s) for s in ("pad_zero", "tap", "conv_done", "csil_done"))
        cs_loaded, cs_saved, cw_ready = sem("cs_loaded"), sem("cs_saved"), sem("cw_ready")
        narrow = {s: sem("n_" + s) for s in ("alog", "z", "abs", "exp", "ln", "sp", "g", "beta", "dt")}
        both = {s: sem("r_" + s) for s in "cc tmp tm cum gc rg br".split()}
        g_ = {s: sem("g_" + s) for s in (
            "bc d dx dm brb sq ss ln rs qk kk kt eg kg at atb xi kd al p pc q x "
            "tb sk rt rtt r up u o oc su sm s ue").split()}
        l_ = {s: sem("l_" + s) for s in (
            "rc z zt a1 a2 a3 g1 gk b bt qk qe dl d1 d2 ml a0 at cp vc vtp vt kdp kt o oc ve su sm s").split()}
        s_ = {s: sem("s_" + s) for s in (
            "bc d dx dm st tr ea ce att xd xe bt y yc xe2 su sm s").split()}
        zeroed = sem("zeroed")
        st_in, st_out = sem("st_in"), sem("st_out")
        n_ = {s: sem("o_" + s) for s in ("yz", "sq", "ss", "ln", "rs", "t", "tz", "hi", "lo")}
        sg_done, mac_tmp, mac_done, mh_done, ml_done, bm_ready = (
            sem(s) for s in ("sg_done", "mac_tmp", "mac_done", "mh_done", "ml_done", "bm_ready"))
        saved = sem("saved")

        def value(eng, v):
            eng.compute_val(v)
            eng.wait_ge(started, 1)
            return v

        def further(eng, v):
            eng.compute_val(v)
            eng.wait_ge(loaded, 32)
            return v

        block = ctx.enter_context(nc.Block())

        @block.sync
        def _(sp_):
            sp_.dma_start(cst[:], io["cst"]).then_inc(loaded, 16)
            sp_.dma_start(x[:], io["x"].rearrange("p (k t) -> p k t", k=KD)).then_inc(loaded, 16)

            def blocks(layer, first, i, nks, source):
                for j, nk in enumerate(nks):
                    sp_.wait_ge(lo_done, value(sp_, layer * BLOCKS + i * len(nks) + (first + j + 1)))
                    sp_.dma_start(raw[:, j % RAW, 0:nk, :], source(j)).then_inc(raw_full[j % RAW], 16)

            def tiles(name, index):
                return io[name][bass.ds(index, 1)].rearrange("a p (k m) -> p (a k) m", m=P)

            def ffn(layer, which, first):
                with sp_.Fori(0, KF // 2) as i:
                    blocks(layer, first, i, (KD,) * 4,
                           lambda j: tiles("up", layer * (2 * UPS) + i * 4 + (which * UPS + j)))
                k0 = np.cumsum((0,) + DOWN_K)
                with sp_.Fori(0, 2) as i:
                    blocks(layer, first + UPS, i, DOWN_K * 4,
                           lambda j: tiles("down", layer * (2 * KD) + i * 4 + (which * KD + j // 3))
                           [:, k0[j % 3]:k0[j % 3 + 1], :])

            with sp_.Fori(0, DEPTH) as layer:
                sp_.wait_ge(x_done, value(sp_, layer * (3 * KD) + 1))
                sp_.dma_start(prm[:], io["prm"][bass.ds(layer, 1)].rearrange("a p n -> (a p) n")).then_inc(prm_in, 16)
                ffn(layer, 0, B_FFN1)
                blocks(layer, B_PROJ, 0, (2,) * 4,
                       lambda j: tiles("narrow", layer)[:, 2 * j:2 * j + 2, :])
                with sp_.Fori(0, 10) as i:
                    blocks(layer, B_PROJ + 4, i, (KD,) * 4, lambda j: tiles("win", layer * 40 + i * 4 + j))
                sp_.wait_ge(st_out, value(sp_, layer * 96 + 48))
                with sp_.Fori(0, KD // 2) as i:
                    blocks(layer, B_MERGE, i, (KD, 4) * 6,
                           lambda j: tiles("branch" if j % 2 else "gate", layer * 24 + i * 6 + j // 2))
                with sp_.Fori(0, 2) as i:
                    blocks(layer, B_OUT, i, (KD,) * 4, lambda j: tiles("wout", layer * KD + i * 4 + j))
                ffn(layer, 1, B_FFN2)
            sp_.wait_ge(x_done, DEPTH * 3 * KD + 1)
            sp_.dma_start(io["y"].rearrange("p (k t) -> p k t", k=KD), x[:]).then_inc(saved, 16)
            sp_.wait_ge(saved, 16)
            sp_.wait_ge(cs_saved, DEPTH * 32)
            sp_.wait_ge(st_out, DEPTH * 96)

        @block.gpsimd
        def _(pool):
            def blocks(layer, first, i, nks):
                for j, nk in enumerate(nks):
                    src = raw[:, j % RAW, 0:nk, :].rearrange("p k m -> p (k m)")
                    hi = wh[:, j % SPLIT, 0:nk, :].rearrange("p k m -> p (k m)")
                    lo = wl[:, j % SPLIT, 0:nk, :].rearrange("p k m -> p (k m)")
                    turns = len(nks) // RAW
                    pool.wait_ge(raw_full[j % RAW], value(pool, layer * (BLOCKS // RAW * 16) + i * (turns * 16) + 16 * ((first + j) // RAW + 1)))
                    pool.wait_ge(blk_done, further(pool, layer * BLOCKS + i * len(nks) + (first + j + 1)))
                    pool.tensor_scalar(hi, src, 1.0, 1.0, MULT, MULT).then_inc(hi_done, 1)
                    pool.wait_ge(hi_done, value(pool, layer * BLOCKS + i * len(nks) + (first + j + 1)))
                    pool.tensor_tensor(lo, src, hi.bitcast(F32), SUB).then_inc(lo_done, 1)

            def ffn(layer, first):
                with pool.Fori(0, KF // 2) as i:
                    blocks(layer, first, i, (KD,) * 4)
                with pool.Fori(0, 2) as i:
                    blocks(layer, first + UPS, i, DOWN_K * 4)

            with pool.Fori(0, DEPTH) as layer:
                ffn(layer, B_FFN1)
                blocks(layer, B_PROJ, 0, (2,) * 4)
                with pool.Fori(0, 10) as i:
                    blocks(layer, B_PROJ + 4, i, (KD,) * 4)
                with pool.Fori(0, KD // 2) as i:
                    blocks(layer, B_MERGE, i, (KD, 4) * 6)
                with pool.Fori(0, 2) as i:
                    blocks(layer, B_OUT, i, (KD,) * 4)
                ffn(layer, B_FFN2)

        @block.tensor
        def _(pe):
            pe.wait_ge(loaded, 32)

            def product(layer, first, i, j, per, slot, nk, moving, start=True, stop=True):
                pe.wait_ge(lo_done, value(pe, layer * BLOCKS + i * per + (first + j + 1 + RAW)))
                for k in range(nk):
                    mh_, ml_ = moving(k)
                    for h in range(2):
                        out = ps[:, 2 * slot + h, 0:HALF]
                        c = slice(h * HALF, (h + 1) * HALF)
                        a, b = start and k == 0, stop and k == nk - 1
                        pe.matmul(out, wh[:, j % SPLIT, k, :], mh_[:, c], start=a, stop=False)
                        pe.matmul(out, wh[:, j % SPLIT, k, :], ml_[:, c], start=False, stop=False)
                        last = pe.matmul(out, wl[:, j % SPLIT, k, :], mh_[:, c], start=False, stop=b)
                last.then_inc(blk_done, 1)

            def h_tiles(k):
                return hh[:, k, :], hl[:, k, :]

            def add_squares(src, start=False, stop=False):
                for h in range(2):
                    last = pe.matmul(ps[:, 6 + h, 0:HALF], ones, src[:, h * HALF:(h + 1) * HALF],
                                     start=start, stop=stop, skip_group_check=True)
                return last

            def eps_first():
                for h in range(2):
                    pe.matmul(ps[:, 6 + h, 0:HALF], ones, cst[:, EPSROW:EPSROW + 1].to_broadcast([P, HALF]),
                              start=True, stop=False, skip_group_check=True)

            def pre_stats(layer, stage):
                for k in range(KD):
                    pe.wait_ge(sq_ready, value(pe, layer * (6 * KD) + (stage * KD + k + 1)))
                    if k == 0:
                        eps_first()
                    last = add_squares(sq[:, k, :], stop=(k == KD - 1))
                last.then_inc(sum_ready, 1)

            def reduce_out(layer, stage, first, nks, moving):
                per = len(nks)
                k0 = np.cumsum((0,) + tuple(nks))
                eps_first()
                with pe.Fori(0, 2) as i:
                    for m in range(4):
                        pe.wait_ge(out_done, value(pe, layer * (3 * KD) + i * 4 + (stage // 2 * KD + m + 1)))
                        for b, nk in enumerate(nks):
                            product(layer, first, i, per * m + b, 4 * per, m % 2, nk,
                                    lambda k, b=b: moving(k0[b] + k), b == 0, b == per - 1)
                        if m:
                            pe.wait_ge(sq_ready, value(pe, layer * (6 * KD) + i * 4 + (stage * KD + m)))
                            add_squares(sq[:, m - 1, :])
                    pe.wait_ge(sq_ready, value(pe, layer * (6 * KD) + i * 4 + (stage * KD + 4)))
                    add_squares(sq[:, 3, :], stop=True).then_inc(sum_ready, 1)

            def ffn(layer, which, first):
                pre_stats(layer, 4 * which)
                pe.wait_ge(hl_ready, value(pe, layer * (4 * KD) + (3 * which * KD + KD)))
                with pe.Fori(0, KF // 2) as i:
                    for j in range(4):
                        pe.wait_ge(prod_done if j % 2 else sil_done, value(pe, layer * (2 * KF) + i * 2 + (which * KF + j // 2 + 1)))
                        product(layer, first, i, j, 4, j, KD, h_tiles)
                pe.wait_ge(al_done, value(pe, layer * (2 * KF) + (which + 1) * KF))
                reduce_out(layer, 4 * which + 1, first + UPS, DOWN_K, lambda k: (ah[:, k, :], al[:, k, :]))

            def common(step):
                n = step.n
                tri_n, rev_n = (tri, rev) if step.prompt else (
                    cst[:, TRI_S:TRI_S + 32], cst[:, REV_S:REV_S + 32])
                pe.wait_ge(both["cc"], value(pe, step.once + 1))
                pe.transpose(ps[0:n, 2, 0:P], cc[:, 0:n], ident).then_inc(both["tmp"], 1)
                yield
                pe.wait_ge(both["tm"], value(pe, step.once + 1))
                pe.matmul(ps[0:n, 3, 0:P], tri_n[0:n, 0:n], tm[0:n, :], start=True, stop=True)
                pe.matmul(ps[0:n, 3, P:2 * P], rev_n[0:n, 0:n], tm[0:n, :], start=True, stop=True)
                pe.matmul(ps[:, 3, 2 * P:2 * P + n], tm[0:n, :], tri_n[0:n, 0:n], start=True, stop=True).then_inc(both["cum"], 1)
                pe.wait_ge(g_["sq"], value(pe, step.once + 1))
                w = 8 * n
                for b in range(-(-w // 512)):
                    c = min(512, w)
                    last = pe.matmul(ps[:, b, 0:c], ones, sq8[:, b * 512:b * 512 + c], start=True, stop=True)
                last.then_inc(g_["ss"], 1)
                yield
                yield

            def spread(bank, off, rowi, n):
                return pe.matmul(ps[:, bank, off:off + n], cst[:, IDENT + rowi:IDENT + rowi + 1].to_broadcast([P, P]),
                                 br[:, 0:n], start=True, stop=True)

            def gdn(step):
                n, o = step.n, step.once
                pe.wait_ge(g_["brb"], value(pe, o + 1))
                pe.wait_ge(both["rg"], further(pe, o + 1))
                for h in range(HEADS):
                    spread(2, h * n, ROW_A + h, n)
                for h in range(HEADS):
                    last = spread(3, h * n, ROW_B + h, n)
                last.then_inc(g_["bc"], 1)
                yield
                pe.wait_ge(g_["qk"], value(pe, o + 1))
                for h in range(HEADS):
                    k_, q_ = kn[:, h * n:(h + 1) * n], qn[:, h * n:(h + 1) * n]
                    pe.matmul(ps[0:n, 0, h * n:(h + 1) * n], k_, k_, start=True, stop=True)
                    last = pe.matmul(ps[0:n, 1, h * n:(h + 1) * n], k_, q_, start=True, stop=True)
                last.then_inc(g_["kk"], 1)
                pe.wait_ge(g_["d"], value(pe, o + 1))
                for h in range(HEADS):
                    last = pe.transpose(ps[0:n, 2, h * P:(h + 1) * P], kn[:, h * n:(h + 1) * n], ident)
                last.then_inc(g_["kt"], 1)
                yield
                yield

                def s_of(h, b):
                    return gs[:, h * P:(h + 1) * P] if step.prompt else states[:, b, h * P:(h + 1) * P]

                def through_state(bank, h, src, stop):
                    w_ = n // step.states
                    for b in range(step.states):
                        c = slice(h * n + b * w_, h * n + (b + 1) * w_)
                        last = pe.matmul(ps[:, bank, c], s_of(h, b), src[:, c], start=(b == 0), stop=stop,
                                         skip_group_check=True)
                    return last

                for l in range(step.levels):
                    final = l == step.levels - 1
                    pe.wait_ge(g_["al"], value(pe, step.solve + l + 1))
                    if l == 0:
                        pe.wait_ge(g_["xi"], further(pe, o + 1))
                        pe.wait_ge(g_["kd"], further(pe, o + 1))
                    else:
                        pe.wait_ge(g_["x"], further(pe, step.solve + l))
                    for h in range(HEADS):
                        c = slice(h * n, (h + 1) * n)
                        last = pe.matmul(ps[0:n, 0, c], al_[0:n, c], xx[0:n, c], start=True, stop=True)
                    last.then_inc(g_["p"], 1)
                    if l == 0:
                        if step.prompt:
                            pe.wait_ge(g_["s"], value(pe, o + 1))
                            pe.wait_ge(zeroed, further(pe, step.layer * 3 + 1))
                        else:
                            pe.wait_ge(st_in, further(pe, step.layer * 48 + 16))
                        pe.wait_ge(g_["kg"], further(pe, o + 1))
                        for h in range(HEADS):
                            last = through_state(3, h, kg, True)
                        last.then_inc(g_["sk"], 1)
                    if l == 1:
                        pe.wait_ge(g_["rt"], value(pe, o + 1))
                        for h in range(HEADS):
                            last = pe.transpose(ps[0:n, 3, h * P:(h + 1) * P], rt[:, h * n:(h + 1) * n], ident)
                        last.then_inc(g_["rtt"], 1)
                    yield
                    pe.wait_ge(g_["pc"], value(pe, step.solve + l + 1))
                    for h in range(HEADS):
                        c = slice(h * n, (h + 1) * n)
                        if not final:
                            pe.matmul(ps[0:n, 1, c], xt[0:n, c], pp[0:n, c], start=True, stop=True)
                        last = pe.matmul(ps[0:n, 2, c], pp[0:n, c], xt[0:n, c], start=True, stop=True)
                    last.then_inc(g_["q"], 1)
                    yield
                pe.wait_ge(g_["r"], value(pe, o + 1))
                pe.wait_ge(g_["tb"], further(pe, o + 1))
                for h in range(HEADS):
                    last = pe.matmul(ps[0:n, 1, h * P:(h + 1) * P], xt[0:n, h * n:(h + 1) * n],
                                     rr[0:n, h * P:(h + 1) * P], start=True, stop=True)
                last.then_inc(g_["up"], 1)
                for h in range(HEADS):
                    through_state(2, h, qg, False)
                    if h == 0:
                        pe.wait_ge(g_["u"], value(pe, o + 1))
                    last = pe.matmul(ps[:, 2, h * n:(h + 1) * n], uu[0:n, h * P:(h + 1) * P],
                                     att[0:n, h * n:(h + 1) * n], start=False, stop=True, skip_group_check=True)
                last.then_inc(g_["o"], 1)
                if step.prompt:
                    for h in range(HEADS):
                        last = pe.matmul(ps[:, 3, h * P:(h + 1) * P], kd[0:n, h * P:(h + 1) * P],
                                         uu[0:n, h * P:(h + 1) * P], start=True, stop=True)
                    last.then_inc(g_["su"], 1)
                else:
                    for h in range(HEADS):
                        pe.wait_ge(g_["ue"], value(pe, step.layer * HEADS + h + 1))
                        for b in range(2):
                            last = pe.matmul(ps[:, 4 + b, :], kd[0:n, h * P:(h + 1) * P], uexp[0:n, b * 512:(b + 1) * 512],
                                             start=True, stop=True)
                        last.then_inc(g_["su"], 1)
                yield

            def gla(step):
                n, o = step.n, step.once
                L = gla_prompt if step.prompt else gla_sample
                tri_n, rev_n = (tri, rev) if step.prompt else (
                    cst[:, TRI_S:TRI_S + 32], cst[:, REV_S:REV_S + 32])
                pe.wait_ge(l_["rc"], value(pe, o + 1))
                pe.matmul(ps[0:n, 4, 0:256], L["rc"][96:112, 0:n], prm[96:112, GUP:GUP + 256],
                          start=True, stop=True).then_inc(l_["z"], 1)
                yield
                pe.wait_ge(l_["gk"], value(pe, o + 1))
                for g in range(2):
                    pe.matmul(ps[:, 5, g * n:(g + 1) * n], L["gk"][0:n, g * P:(g + 1) * P], tri_n[0:n, 0:n], start=True, stop=True)
                for g in range(2):
                    last = pe.matmul(ps[:, 5, (2 + g) * n:(3 + g) * n], L["gk"][0:n, g * P:(g + 1) * P], rev_n[0:n, 0:n],
                                     start=True, stop=True)
                last.then_inc(l_["b"], 1)
                pe.wait_ge(l_["vc"], value(pe, o + 1))
                for h in range(HEADS):
                    last = pe.transpose(ps[0:n, 4, h * P:(h + 1) * P], L["vc"][:, h * n:(h + 1) * n], ident)
                last.then_inc(l_["vtp"], 1)
                yield
                pe.wait_ge(l_["qe"], value(pe, o + 1))
                for g in range(2):
                    last = pe.transpose(ps[0:n, 5, g * P:(g + 1) * P], L["kd"][:, g * n:(g + 1) * n], ident)
                last.then_inc(l_["kdp"], 1)
                yield
                yield
                yield
                for l in range(step.levels + 1):
                    if l == 0:
                        pe.wait_ge(l_["ml"], value(pe, o + 1))
                        pe.wait_ge(l_["vt"], further(pe, o + 1))
                        pe.wait_ge(l_["kt"], further(pe, o + 1))
                    else:
                        pe.wait_ge(l_["cp"], value(pe, step.score + l))
                    for h in range(HEADS):
                        r = slice(64 * (h % 2), 64 * (h % 2) + 64)
                        c = slice(h // 2 * n, (h // 2 + 1) * n)
                        a, b = (L["dl"][r, l, c], L["dl"][r, l, c]) if l < step.levels else (L["ks"][r, c], L["qs"][r, c])
                        last = pe.matmul(ps[0:n, 4 + h % 2, c], a, b, start=True, stop=True)
                    last.then_inc(l_["at"], 1)
                    yield
                if step.prompt:
                    pe.wait_ge(l_["s"], value(pe, o + 1))
                    pe.wait_ge(zeroed, further(pe, step.layer * 3 + 2))
                else:
                    pe.wait_ge(st_in, further(pe, step.layer * 48 + 32))
                pe.wait_ge(l_["cp"], further(pe, step.score + step.levels + 1))
                w_ = n // step.states
                for h in range(HEADS):
                    r = slice(64 * (h % 2), 64 * (h % 2) + 64)
                    g = h // 2
                    for b in range(step.states):
                        s_b = ls[r, g * P:(g + 1) * P] if step.prompt else states[r, b, g * P:(g + 1) * P]
                        pe.matmul(ps[:, 4 + h % 2, g * n + b * w_:g * n + (b + 1) * w_], s_b,
                                  L["qe"][r, g * n + b * w_:g * n + (b + 1) * w_], start=(b == 0), stop=False,
                                  skip_group_check=True)
                    a = (h % 2 * 2 + g) * n
                    last = pe.matmul(ps[:, 4 + h % 2, g * n:(g + 1) * n], L["vt"][0:n, h * P:(h + 1) * P],
                                     L["att"][0:n, a:a + n], start=False, stop=True, skip_group_check=True)
                last.then_inc(l_["o"], 1)
                yield
                if step.prompt:
                    pe.wait_ge(l_["oc"], value(pe, o + 2))
                    for h in range(HEADS):
                        r = slice(64 * (h % 2), 64 * (h % 2) + 64)
                        last = pe.matmul(ps[r, 4, h // 2 * P:(h // 2 + 1) * P], L["kt"][0:n, h * 64:(h + 1) * 64],
                                         L["vt"][0:n, h * P:(h + 1) * P], start=True, stop=True)
                    last.then_inc(l_["su"], 1)
                else:
                    for h in range(HEADS):
                        r = slice(64 * (h % 2), 64 * (h % 2) + 64)
                        pe.wait_ge(l_["ve"], value(pe, step.layer * HEADS + h + 1))
                        for b in range(2):
                            last = pe.matmul(ps[r, b, :], L["kt"][0:n, h * 64:(h + 1) * 64],
                                             vexp[0:n, 4 * b:4 * b + 4, :].rearrange("p a b -> p (a b)"),
                                             start=True, stop=True)
                        last.then_inc(l_["su"], 1)
                yield

            def ssd(step):
                n, o = step.n, step.once
                S = ssd_prompt if step.prompt else ssd_sample
                pe.wait_ge(both["br"], value(pe, o + 1))
                pe.wait_ge(g_["brb"], further(pe, o + 1))
                if not step.prompt:
                    pe.wait_ge(n_["lo"], further(pe, step.layer * 3 + 2))
                for h in range(SSD_HEADS):
                    last = spread(6 + h // 4, h % 4 * n, ROW_DT + h, n)
                last.then_inc(s_["bc"], 1)
                yield
                pe.wait_ge(s_["st"], value(pe, o + 1))
                pe.wait_ge(s_["d"], further(pe, o + 1))
                for g in range(2):
                    pe.matmul(ps[0:n, 7, g * n:(g + 1) * n], S["xbc"][:, (4 + g) * n:(5 + g) * n],
                              S["xbc"][:, (6 + g) * n:(7 + g) * n], start=True, stop=True)
                for t in range(4):
                    pe.transpose(ps[0:n, 6, t * P:(t + 1) * P], S["xbc"][:, t * n:(t + 1) * n], ident)
                for g in range(2):
                    last = pe.transpose(ps[0:n, 7, 256 + g * P:256 + (g + 1) * P], S["xbc"][:, (4 + g) * n:(5 + g) * n], ident)
                last.then_inc(s_["tr"], 1)
                yield
                yield
                if step.prompt:
                    pe.wait_ge(s_["s"], value(pe, o + 1))
                    pe.wait_ge(zeroed, further(pe, step.layer * 3 + 3))
                else:
                    pe.wait_ge(st_in, further(pe, step.layer * 48 + 48))
                pe.wait_ge(s_["att"], further(pe, o + 1))
                pe.wait_ge(s_["xe"], further(pe, o + 1))
                pe.wait_ge(s_["ce"], further(pe, o + 1))
                w_ = n // step.states
                for h in range(SSD_HEADS):
                    r = slice(64 * (h % 2), 64 * (h % 2) + 64)
                    t = h // 2
                    for b in range(step.states):
                        s_b = ss_[:, h * 64:(h + 1) * 64] if step.prompt else states[:, b, h * 64:(h + 1) * 64]
                        pe.matmul(ps[r, 6, t * n + b * w_:t * n + (b + 1) * w_], s_b,
                                  S["ce"][:, h * n + b * w_:h * n + (b + 1) * w_], start=(b == 0), stop=False,
                                  skip_group_check=True)
                    last = pe.matmul(ps[r, 6, t * n:(t + 1) * n], S["xd"][0:n, h * 64:(h + 1) * 64],
                                     S["dd"][0:n, h * n:(h + 1) * n], start=False, stop=True, skip_group_check=True)
                last.then_inc(s_["y"], 1)
                yield
                pe.wait_ge(s_["bt"], value(pe, o + 1))
                if step.prompt:
                    for g in range(2):
                        last = pe.matmul(ps[:, 7, g * 256:(g + 1) * 256], S["bt"][0:n, g * P:(g + 1) * P],
                                         S["xe"][0:n, g * 256:(g + 1) * 256], start=True, stop=True)
                    last.then_inc(s_["su"], 1)
                else:
                    for g in range(2):
                        pe.wait_ge(s_["xe2"], value(pe, step.layer * 2 + g + 1))
                        for b in range(4):
                            last = pe.matmul(ps[:, b, :], S["bt"][0:n, g * P:(g + 1) * P],
                                             xexp[0:n, b * 512:(b + 1) * 512], start=True, stop=True)
                        last.then_inc(s_["su"], 1)
                yield
                yield

            def branch_stats(layer, branch):
                pe.wait_ge(n_["sq"], value(pe, layer * 3 + branch + 1))
                if branch < 2:
                    for t in range(4):
                        for h in range(2):
                            last = pe.matmul(ps[:, 2 * t + h, 0:HALF], ones, nsq[:, t, h * HALF:(h + 1) * HALF],
                                             start=True, stop=True)
                else:
                    for g in range(2):
                        for t in range(2):
                            for h in range(2):
                                last = pe.matmul(ps[:, 2 * g + h, 0:HALF], ones,
                                                 nsq[:, 2 * g + t, h * HALF:(h + 1) * HALF],
                                                 start=(t == 0), stop=(t == 1))
                last.then_inc(n_["ss"], 1)

            with pe.Fori(0, DEPTH) as layer:
                ffn(layer, 0, B_FFN1)
                pre_stats(layer, 2)
                pe.wait_ge(hl_ready, value(pe, layer * (4 * KD) + 2 * KD))
                for j in range(4):
                    product(layer, B_PROJ, 0, j, 4, 0, 2, lambda k: h_tiles(2 * j + k), j == 0, j == 3)
                pe.wait_ge(small_done, value(pe, layer + 1))
                with pe.Fori(0, 10) as i:
                    for j in range(4):
                        pe.wait_ge(evict_done, value(pe, layer * 40 + i * 4 + (j + 1)))
                        product(layer, B_PROJ + 4, i, j, 4, j, KD, h_tiles)
                pe.wait_ge(evict_done, value(pe, layer * 40 + 44))
                with pe.Fori(0, CHUNKS) as c:
                    step = prompt_step(layer, c)
                    together(common(step), gdn(step), gla(step), ssd(step))
                step = sample_step(layer)
                for b, stages in enumerate(((common(step), gdn(step)), (gla(step),), (ssd(step),))):
                    alone(*stages)
                    branch_stats(layer, b)
                pe.wait_ge(hl_ready, value(pe, layer * (4 * KD) + 3 * KD))
                with pe.Fori(0, KD // 2) as i:
                    for j in range(12):
                        u = j // 2
                        if j % 2:
                            pe.wait_ge(mac_done, value(pe, layer * 24 + i * 6 + (u + 1)))
                            product(layer, B_MERGE, i, j, 12, j % 4, 4,
                                    lambda k, u=u: (oh[u % 3][:, k, :], ol[u % 3][:, k, :]))
                        else:
                            pe.wait_ge(sg_done, value(pe, layer * 24 + i * 6 + (u + 1)))
                            product(layer, B_MERGE, i, j, 12, j % 4, KD, h_tiles)
                pe.wait_ge(ml_done, value(pe, layer * KD + KD))
                reduce_out(layer, 3, B_OUT, (KD,), lambda k: (mh[:, k, :], ml[:, k, :]))
                ffn(layer, 1, B_FFN2)

        @block.scalar
        def _(act):
            act.wait_ge(loaded, 32)

            def rsqrt_stats(layer, stage, out):
                act.preload_act_table_set(LN_EXP)
                act.wait_ge(sum_ready, value(act, layer * SUMS[-1] + SUMS[stage]))
                act.activation(halves(out[:, :]), ps[:, 6:8, 0:HALF], ACT.Ln, scale=1.0 / D_MODEL).then_inc(ln_ready, 1)
                act.wait_ge(ln_ready, value(act, layer * 6 + (stage + 1)))
                act.activation(out[:, :], out[:, :], ACT.Exp, scale=-0.5).then_inc(rstd_ready, 1)

            def split_h(layer, number):
                for k in range(KD):
                    act.wait_ge(hf_ready, value(act, layer * (4 * KD) + (number * KD + k + 1)))
                    act.activation(hh[:, k, :], hf[:, k, :], ACT.Copy).then_inc(hh_ready, 1)

            def pre_norm(layer, stage, number):
                for k in range(KD):
                    act.wait_ge(x_done, value(act, layer * (3 * KD) + ((stage // 2 - 1) * KD + k + 2 if stage else 1)))
                    act.activation(sq[:, k, :], x[:, k, :], ACT.Square).then_inc(sq_ready, 1)
                rsqrt_stats(layer, stage, rstd)
                split_h(layer, number)

            def reduce_out(layer, stage, first, per):
                with act.Fori(0, 2) as i:
                    for m in range(4):
                        act.wait_ge(blk_done, value(act, layer * BLOCKS + i * (4 * per) + (first + per * m + per + SPLIT)))
                        act.activation(sq[:, m, :].rearrange("p (a t) -> p a t", a=2), pair(m % 2), ACT.Square).then_inc(sq_ready, 1)
                        act.activation(f[:, bass.ds(i * 4 + m, 1), :].rearrange("p k (a t) -> p (k a) t", a=2),
                                       pair(m % 2), ACT.Copy).then_inc(out_done, 1)
                rsqrt_stats(layer, stage, rstd_post)

            def ffn(layer, which, first):
                pre_norm(layer, 4 * which, 3 * which)
                with act.Fori(0, KF // 2) as i:
                    for j in range(2):
                        n = layer * (2 * KF) + i * 2 + (which * KF + j)
                        act.wait_ge(blk_done, value(act, layer * BLOCKS + i * 4 + (first + 2 * j + 1 + SPLIT)))
                        act.wait_ge(prod_done, further(act, n + 1))
                        act.activation(halves(sil[:, j, :]), pair(2 * j), ACT.Silu).then_inc(sil_done, 1)
                        act.wait_ge(prod_done, value(act, n + 3))
                        act.activation(ah[:, bass.ds(i * 2 + j, 1), :].rearrange("p k t -> p (k t)"), prod[:, j, :],
                                       ACT.Copy).then_inc(ah_done, 1)
                reduce_out(layer, 4 * which + 1, first + UPS, 3)

            def view(a, k, n):
                return a[:, 0:k * n].rearrange("p (k t) -> p k t", k=k)

            def common(step):
                n, o = step.n, step.once
                act.wait_ge(g_["s"], value(act, o + 1))
                act.activation(view(sq8, 8, n), proj[:, GQ:GQ + 8, step.cols], ACT.Square).then_inc(g_["sq"], 1)
                act.wait_ge(both["tmp"], value(act, o + 1))
                act.activation(tm[0:n, :], ps[0:n, 2, 0:P], ACT.Copy).then_inc(both["tm"], 1)
                yield
                act.wait_ge(both["cum"], value(act, o + 1))
                act.activation(br[:, 0:n], ps[:, 3, 2 * P:2 * P + n], ACT.Copy).then_inc(both["br"], 1)
                act.activation(gc[0:n, :], ps[0:n, 3, 0:P], ACT.Copy).then_inc(both["gc"], 1)
                act.activation(rg[0:n, ROW_A:ROW_A + 4], ps[0:n, 3, P + ROW_A:P + ROW_A + 4], ACT.Exp)
                act.activation(rg[0:n, ROW_DT:ROW_DT + 8], ps[0:n, 3, P + ROW_DT:P + ROW_DT + 8], ACT.Exp).then_inc(both["rg"], 1)
                yield
                act.wait_ge(g_["ss"], value(act, o + 1))
                w = min(512, 8 * n)
                act.activation(rs8[:, 0:8 * n].rearrange("p (b c) -> p b c", c=w), ps[:, 0:8 * n // w, 0:w], ACT.Ln,
                               bias=epsc).then_inc(g_["ln"], 1)
                act.wait_ge(g_["ln"], value(act, o + 1))
                act.activation(rs8[:, 0:8 * n], rs8[:, 0:8 * n], ACT.Exp, scale=-0.5).then_inc(g_["rs"], 1)
                yield

            def gdn(step):
                n, o = step.n, step.once
                act.wait_ge(g_["bc"], value(act, o + 1))
                act.activation(eg[:, 0:4 * n], ps[:, 2, 0:4 * n], ACT.Exp).then_inc(g_["eg"], 1)
                yield
                act.wait_ge(g_["d"], value(act, o + 1))
                act.activation(dd[0:n, 0:4 * n], dd[0:n, 0:4 * n], ACT.Exp).then_inc(g_["dx"], 1)
                yield
                yield
                for l in range(step.levels):
                    act.wait_ge(g_["p"], value(act, step.solve + l + 1))
                    act.activation(pp[0:n, 0:4 * n], ps[0:n, 0, 0:4 * n], ACT.Copy).then_inc(g_["pc"], 1)
                    if l == 1:
                        act.wait_ge(g_["rtt"], value(act, o + 1))
                        act.activation(rr[0:n, :], ps[0:n, 3, :], ACT.Copy).then_inc(g_["r"], 1)
                    yield
                    yield
                act.wait_ge(g_["up"], value(act, o + 1))
                act.activation(uu[0:n, :], ps[0:n, 1, :], ACT.Copy).then_inc(g_["u"], 1)
                act.wait_ge(g_["o"], value(act, o + 1))
                act.activation(proj[:, GV:GV + 4, step.cols], view(ps[:, 2, :], 4, n), ACT.Copy).then_inc(g_["oc"], 1)
                yield

            def gla(step):
                n, o = step.n, step.once
                L = gla_prompt if step.prompt else gla_sample
                for a, (want, done, func, scale, bias) in enumerate((
                        ("zt", "a1", ACT.Abs, 1.0, 0.0), ("a1", "a2", ACT.Exp, -1.0, 0.0), ("a2", "a3", ACT.Ln, 1.0, 1.0))):
                    act.wait_ge(l_[want], value(act, o + 1))
                    act.activation(L["a"][0:n, :], L["z" if a == 0 else "a"][0:n, :], func, scale=scale, bias=bias).then_inc(l_[done], 1)
                yield
                act.wait_ge(l_["b"], value(act, o + 1))
                act.activation(L["bt"][:, 0:2 * n], ps[:, 5, 0:2 * n], ACT.Copy)
                act.activation(L["eb"][:, 0:2 * n], ps[:, 5, 0:2 * n], ACT.Exp)
                act.activation(L["er"][:, 0:2 * n], ps[:, 5, 2 * n:4 * n], ACT.Exp).then_inc(l_["bt"], 1)
                yield
                act.wait_ge(l_["vtp"], value(act, o + 1))
                act.activation(L["vt"][0:n, :], ps[0:n, 4, :], ACT.Copy).then_inc(l_["vt"], 1)
                yield
                act.wait_ge(l_["kdp"], value(act, o + 1))
                act.activation(L["kt"][0:n, :], ps[0:n, 5, 0:256], ACT.Copy).then_inc(l_["kt"], 1)
                act.wait_ge(l_["dl"], value(act, o + 1))
                d = L["dl"][:, 0:step.levels, 0:2 * n]
                act.activation(d, d, ACT.Abs).then_inc(l_["d1"], 1)
                yield
                act.wait_ge(l_["d1"], value(act, o + 1))
                act.activation(d, d, ACT.Exp, scale=-1.0).then_inc(l_["d2"], 1)
                yield
                for l in range(step.levels + 1):
                    yield
                act.wait_ge(l_["o"], value(act, o + 1))
                for e in range(2):
                    last = act.activation(proj[:, LV + e:LV + 4:2, step.cols], view(ps[:, 4 + e, :], 2, n), ACT.Copy)
                last.then_inc(l_["oc"], 1)
                yield
                yield

            def ssd(step):
                n, o = step.n, step.once
                S = ssd_prompt if step.prompt else ssd_sample
                act.wait_ge(s_["s"], value(act, o + 1))
                act.wait_ge(s_["yc"], further(act, o + 1))
                if not step.prompt:
                    act.wait_ge(n_["lo"], further(act, step.layer * 3 + 2))
                act.activation(view(S["xbc"], 8, n), proj[:, SX:SX + 8, step.cols], ACT.Copy).then_inc(s_["st"], 1)
                act.wait_ge(s_["bc"], value(act, o + 1))
                act.activation(S["ea"][:, 0:8 * n].rearrange("p (b c) -> p b c", b=2), ps[:, 6:8, 0:4 * n], ACT.Exp).then_inc(s_["ea"], 1)
                yield
                act.wait_ge(s_["d"], value(act, o + 1))
                act.activation(S["dd"][0:n, 0:8 * n], S["dd"][0:n, 0:8 * n], ACT.Exp).then_inc(s_["dx"], 1)
                act.wait_ge(s_["tr"], value(act, o + 1))
                act.activation(S["bt"][0:n, 0:256], ps[0:n, 7, 256:512], ACT.Copy).then_inc(s_["bt"], 1)
                yield
                yield
                yield
                yield
                yield

            def branch_norm(layer, b):
                last = (g_, l_)[b]["oc"] if b < 2 else n_["yz"]
                if b < 2:
                    act.wait_ge(last, value(act, layer * STEPS + (STEPS + 1)))
                    act.wait_ge((g_, l_)[b]["s"], further(act, layer * STEPS + (STEPS + 1)))
                else:
                    act.wait_ge(last, further(act, layer + 1))
                src = proj[:, (GV, LV, SX)[b]:(GV, LV, SX)[b] + 4, :]
                act.activation(nsq[:, :, :], src, ACT.Square).then_inc(n_["sq"], 1)
                act.wait_ge(n_["ss"], value(act, layer * 3 + b + 1))
                k = 4 if b < 2 else 2
                o = nrs[:, 0:k, :].rearrange("p k (a t) -> p (k a) t", a=2)
                act.activation(o, ps[:, 0:2 * k, 0:HALF], ACT.Ln, scale=1.0 / (128 if b < 2 else 256), bias=epsc).then_inc(n_["ln"], 1)
                act.wait_ge(n_["ln"], value(act, layer * 3 + b + 1))
                act.activation(nrs[:, 0:k, :], nrs[:, 0:k, :], ACT.Exp, scale=-0.5).then_inc(n_["rs"], 1)
                act.wait_ge(n_["tz"], value(act, layer * 3 + b + 1))
                act.activation(oh[b][:, :, :], nt[:, :, :], ACT.Copy).then_inc(n_["hi"], 1)

            def save_prompt_states(layer):
                for b, (name, cols, live) in enumerate((("gdn", 512, gs), ("gla", 256, ls), ("ssd", 512, ss_))):
                    act.wait_ge((g_, l_, s_)[b]["s"], value(act, layer * STEPS + (CHUNKS + 1)))
                    act.dma_start(io["out_p_" + name][bass.ds(layer, 1)].rearrange("a p n -> (a p) n"), live[:, 0:cols]).then_inc(st_out, 16)

            def save_states(layer, b):
                name = ("gdn", "gla", "ssd")[b]
                cols = (512, 256, 512)[b]
                act.wait_ge((g_, l_, s_)[b]["s"], value(act, layer * STEPS + (STEPS + 1)))
                act.dma_start(io["out_s_" + name][bass.ds(layer, 1)].rearrange("a p b n -> (a p) b n"),
                              states[:, :, 0:cols]).then_inc(st_out, 16)

            def load_states(layer, b):
                name = ("gdn", "gla", "ssd")[b]
                cols = (512, 256, 512)[b]
                act.wait_ge(st_out, value(act, layer * 96 + 48 + 16 * b))
                act.dma_start(states[:, :, 0:cols], io["in_" + name][bass.ds(layer, 1)].rearrange("a p b n -> (a p) b n")).then_inc(st_in, 16)

            def save_conv(layer):
                act.wait_ge(conv_done, value(act, layer * CONV_TILES + CONV_TILES))
                act.dma_start(io["out_p_conv"][bass.ds(layer, 1)].rearrange("a p t c -> (a p) t c"), cs_p[:, :, :]).then_inc(cs_saved, 16)
                act.dma_start(io["out_s_conv"][bass.ds(layer, 1)].rearrange("a p t n -> (a p) t n"),
                              cs_s[:, :, :, :].rearrange("p t b c -> p t (b c)")).then_inc(cs_saved, 16)

            def project(layer):
                def block_in(i, first, j):
                    act.wait_ge(blk_done, value(act, layer * BLOCKS + i * 4 + (B_PROJ + 4 + 4 * first + j + 1 + SPLIT)))

                def by_batch(a):
                    return a.rearrange("p (b s) -> p b s", s=3 + DEC_SEQ)

                def conv_group(i, first, tile, number):
                    def silu(j):
                        act.wait_ge(conv_done, value(act, layer * CONV_TILES + i * 4 + (number + j + 1)))
                        t = bass.ds(i * 4 + (tile + j), 1)
                        act.activation(proj[:, t, 0:SEQ].rearrange("p k t -> p (k t)"), cacc[:, j % 2, 0:SEQ],
                                       ACT.Silu, bias=cb[:, j:j + 1])
                        act.activation(proj[:, t, SEQ:T].rearrange("p k (b s) -> p (k b) s", s=DEC_SEQ),
                                       by_batch(cacc[:, j % 2, 3 + SEQ:PADW])[:, :, 0:DEC_SEQ],
                                       ACT.Silu, bias=cb[:, j:j + 1]).then_inc(csil_done, 1)

                    for j in range(4):
                        block_in(i, first, j)
                        a, b = ps[:, 2 * j, :], ps[:, 2 * j + 1, :]
                        s = by_batch(pad[:, j, 3 + SEQ:PADW])
                        act.activation(pad[:, j, 3:3 + HALF], a[:, 0:HALF], ACT.Copy)
                        act.activation(pad[:, j, 3 + HALF:3 + SEQ], b[:, 0:SEQ - HALF], ACT.Copy)
                        act.activation(s[:, :, 0:3], cs_in[:, bass.ds(i * 4 + (number + j), 1), :, :].rearrange(
                            "p k b c -> p (k b) c"), ACT.Copy)
                        act.activation(s[:, :, 3:], b[:, SEQ - HALF:HALF].rearrange("p (b s) -> p b s", s=DEC_SEQ),
                                       ACT.Copy).then_inc(evict_done, 1)
                        if j:
                            silu(j - 1)
                    silu(3)

                def direct_group(i, first, tile, func):
                    for j in range(4):
                        block_in(i, first, j)
                        act.activation(proj[:, bass.ds(i * 4 + (tile + j), 1), :].rearrange("p k (a t) -> p (k a) t", a=2),
                                       pair(j), func).then_inc(evict_done, 1)

                act.wait_ge(blk_done, value(act, layer * BLOCKS + (B_PROJ + 4 + SPLIT)))
                act.activation(halves(proj[:, SMALL, :]), pair(0), ACT.Copy).then_inc(small_done, 1)
                act.wait_ge(cs_loaded, value(act, layer * 16 + 16))
                act.wait_ge(pad_zero, further(act, layer + 1))
                with act.Fori(0, 3) as i:
                    conv_group(i, 0, GQ, 0)
                direct_group(0, 3, GZ, ACT.Silu)
                with act.Fori(0, 2) as i:
                    direct_group(i, 4, LQ, ACT.Copy)
                direct_group(0, 6, LG, ACT.Silu)
                direct_group(0, 7, SZ, ACT.Silu)
                with act.Fori(0, 2) as i:
                    conv_group(i, 8, SX, 12)

            with act.Fori(0, DEPTH) as layer:
                act.wait_ge(prm_in, value(act, layer * 16 + 16))
                ffn(layer, 0, B_FFN1)
                pre_norm(layer, 2, 1)
                act.wait_ge(hl_ready, value(act, layer * (4 * KD) + 2 * KD))
                act.dma_start(cs_in[:, :, :, :].rearrange("p t b c -> p (t b c)"),
                              io["in_conv"][bass.ds(layer, 1)].rearrange("a p n -> (a p) n")).then_inc(cs_loaded, 16)
                project(layer)
                save_conv(layer)
                act.preload_act_table_set(LN_EXP)
                act.activation(nega[:, :], prm[:, ALOG:ALOG + 1], ACT.Exp).then_inc(narrow["alog"], 1)
                for want, done, src, dst, func, scale, bias in (
                        ("z", "abs", sp, se, ACT.Abs, 1.0, 0.0), ("abs", "exp", se, se, ACT.Exp, -1.0, 0.0),
                        ("exp", "ln", se, sl, ACT.Ln, 1.0, 1.0)):
                    act.wait_ge(narrow[want], value(act, layer + 1))
                    act.activation(dst[:, :], src[:, :], func, scale=scale, bias=bias).then_inc(narrow[done], 1)
                act.wait_ge(narrow["g"], value(act, layer + 1))
                act.activation(cm[32:64, :], sp[32:64, :], ACT.Exp, scale=-1.0).then_inc(narrow["beta"], 1)
                with act.Fori(0, CHUNKS) as c:
                    step = prompt_step(layer, c)
                    together(common(step), gdn(step), gla(step), ssd(step))
                save_prompt_states(layer)
                load_states(layer, 0)
                step = sample_step(layer)
                for b, stages in enumerate(((common(step), gdn(step)), (gla(step),), (ssd(step),))):
                    alone(*stages)
                    save_states(layer, b)
                    branch_norm(layer, b)
                    if b < 2:
                        load_states(layer, b + 1)
                split_h(layer, 2)
                with act.Fori(0, KD // 2) as i:
                    for u in range(6):
                        if u == 0:
                            act.wait_ge(bm_ready, value(act, layer * 4 + i + 1))
                        act.wait_ge(blk_done, further(act, layer * BLOCKS + i * 12 + (B_MERGE + 2 * u + 1 + SPLIT)))
                        act.wait_ge(mac_done, further(act, layer * 24 + i * 6 + (u + 1)))
                        act.activation(halves(sg[:, u % 2, :]), pair(2 * u % 4), ACT.Sigmoid,
                                       bias=bm[:, u % 3 * 2 + u // 3:u % 3 * 2 + u // 3 + 1]).then_inc(sg_done, 1)
                        if u % 3 == 2:
                            act.wait_ge(mac_done, value(act, layer * 24 + i * 6 + (u + 3)))
                            act.activation(mh[:, bass.ds(i * 2 + u // 3, 1), :].rearrange("p k t -> p (k t)"),
                                           mac[:, u // 3, :], ACT.Copy).then_inc(mh_done, 1)
                reduce_out(layer, 3, B_OUT, 1)
                ffn(layer, 1, B_FFN2)

        @block.vector
        def _(dve):
            for n, (s, free) in enumerate(((blk_done, SPLIT), (sil_done, 2), (prod_done, 2), (out_done, 2),
                                           (evict_done, 4), (csil_done, 2), (sg_done, 2), (mac_done, 2),
                                           (lo_done, RAW), (x_done, 1), (g_["s"], 1), (l_["s"], 1),
                                           (s_["s"], 1), (g_["oc"], 1), (l_["oc"], 1))):
                dve.memset(cw[:, n:n + 1], 0.0).then_inc(s, free)
            dve.memset(cb[:, 0:1], 0.0).then_inc(s_["yc"], 1)
            dve.memset(cb[:, 1:2], 0.0).then_inc(started, 1)
            dve.wait_ge(loaded, 32)

            def split_in(layer, number, wcol):
                def low(k):
                    dve.wait_ge(hh_ready, value(dve, layer * (4 * KD) + (number * KD + k + 1)))
                    dve.tensor_tensor(hl[:, k, :], hf[:, k, :], hh[:, k, :].bitcast(F32), SUB).then_inc(hl_ready, 1)

                for k in range(KD):
                    dve.scalar_tensor_tensor(out=hf[:, k, :], in0=x[:, k, :], scalar=prm[:, wcol + k:wcol + k + 1],
                                             in1=rstd[:, :], op0=MULT, op1=MULT).then_inc(hf_ready, 1)
                    if k:
                        low(k - 1)
                low(KD - 1)

            def pre_norm(layer, stage, number, wcol):
                dve.wait_ge(rstd_ready, value(dve, layer * 6 + (stage + 1)))
                dve.wait_ge(x_done, further(dve, layer * (3 * KD) + (stage // 2 * KD + 1)))
                split_in(layer, number, wcol)

            def post_norm(layer, stage, wcol, scale):
                q = stage // 2
                dve.wait_ge(rstd_ready, value(dve, layer * 6 + (stage + 1)))
                for k in range(KD):
                    dve.scalar_tensor_tensor(out=f[:, k, :], in0=f[:, k, :], scalar=prm[:, wcol + k:wcol + k + 1],
                                             in1=rstd_post[:, :], op0=MULT, op1=MULT).then_inc(x_tmp, 1)
                for k in range(KD):
                    dve.wait_ge(x_tmp, value(dve, layer * (3 * KD) + (q * KD + k + 1)))
                    dve.scalar_tensor_tensor(out=x[:, k, :], in0=f[:, k, :], scalar=scale, in1=x[:, k, :],
                                             op0=MULT, op1=ADD).then_inc(x_done, 1)

            def ffn(layer, which, first, wpre, wpost):
                pre_norm(layer, 4 * which, 3 * which, wpre)
                with dve.Fori(0, KF // 2) as i:
                    for j in range(2):
                        n = layer * (2 * KF) + i * 2 + (which * KF + j)
                        dve.wait_ge(blk_done, value(dve, layer * BLOCKS + i * 4 + (first + 2 * j + 2 + SPLIT)))
                        dve.wait_ge(sil_done, further(dve, n + 3))
                        dve.tensor_tensor(halves(prod[:, j, :]), halves(sil[:, j, :]), pair(2 * j + 1), MULT).then_inc(prod_done, 1)
                        dve.wait_ge(prod_done, value(dve, n + 3))
                        dve.wait_ge(ah_done, further(dve, n + 1))
                        m = bass.ds(i * 2 + j, 1)
                        dve.tensor_tensor(al[:, m, :].rearrange("p k t -> p (k t)"), prod[:, j, :],
                                          ah[:, m, :].rearrange("p k t -> p (k t)").bitcast(F32), SUB).then_inc(al_done, 1)
                post_norm(layer, 4 * which + 1, wpost, 0.5)

            def project(layer):
                def conv_group(i, first, number):
                    c0 = layer * CONV_TILES + i * 4 + number
                    dve.wait_ge(csil_done, value(dve, c0 + 2))
                    dve.tensor_copy(cw[:, :], prm[:, bass.ds(i * 16 + (CONVW + 4 * number), 16)])
                    dve.tensor_copy(cb[:, :], prm[:, bass.ds(i * 4 + (CONVB + number), 4)]).then_inc(cw_ready, 1)
                    dve.wait_ge(cw_ready, value(dve, layer * 5 + i + (number // 4 + 1)))
                    for j in range(4):
                        dve.wait_ge(evict_done, value(dve, layer * 40 + i * 4 + (4 * first + j + 5)))
                        dve.wait_ge(csil_done, further(dve, c0 + j + 1))
                        a = cacc[:, j % 2, 0:CW]
                        dve.tensor_scalar(a, pad[:, j, 0:CW], cw[:, 4 * j:4 * j + 1], None, MULT).then_inc(tap, 1)
                        for t in range(1, CONV):
                            dve.wait_ge(tap, value(dve, c0 * 3 + 3 * j + t))
                            last = dve.scalar_tensor_tensor(out=a, in0=pad[:, j, t:t + CW],
                                                            scalar=cw[:, 4 * j + t:4 * j + t + 1], in1=a,
                                                            op0=MULT, op1=ADD)
                            if t < CONV - 1:
                                last.then_inc(tap, 1)
                        tile = bass.ds(i * 4 + (number + j), 1)
                        dve.tensor_copy(cs_p[:, tile, :].rearrange("p k c -> p (k c)"), pad[:, j, SEQ:SEQ + 3])
                        dve.tensor_copy(cs_s[:, tile, :, :].rearrange("p k b c -> p (k b) c"),
                                        pad[:, j, 3 + SEQ:PADW].rearrange("p (b s) -> p b s", s=3 + DEC_SEQ)
                                        [:, :, DEC_SEQ:]).then_inc(conv_done, 1)

                dve.memset(pad[:, :, 0:3], 0.0).then_inc(pad_zero, 1)
                with dve.Fori(0, 3) as i:
                    conv_group(i, 0, 0)
                with dve.Fori(0, 2) as i:
                    conv_group(i, 8, 12)

            def narrow_columns(layer):
                dve.wait_ge(small_done, value(dve, layer + 1))
                dve.wait_ge(narrow["alog"], further(dve, layer + 1))
                dve.tensor_scalar(nega[:, :], nega[:, :], -1.0, None, MULT)
                dve.tensor_scalar(sp[:, :], proj[:, SMALL, :], prm[:, SIGN:SIGN + 1], prm[:, SBIAS:SBIAS + 1],
                                  MULT, ADD).then_inc(narrow["z"], 1)
                dve.wait_ge(narrow["ln"], value(dve, layer + 1))
                dve.scalar_tensor_tensor(out=sp[:, :], in0=sp[:, :], scalar=0.0, in1=sl[:, :], op0=MAX, op1=ADD).then_inc(narrow["sp"], 1)
                dve.wait_ge(narrow["sp"], value(dve, layer + 1))
                dve.tensor_scalar(cm[:, :], sp[:, :], nega[:, 0:1], None, MULT).then_inc(narrow["g"], 1)
                dve.wait_ge(narrow["g"], value(dve, layer + 1))
                dve.tensor_copy(cm[96:128, :], sp[64:96, :]).then_inc(narrow["dt"], 1)
                dve.wait_ge(narrow["beta"], value(dve, layer + 1))
                dve.wait_ge(narrow["dt"], further(dve, layer + 1))

            def view(a, k):
                return a.rearrange("p (k t) -> p k t", k=k)

            def over(a, k):
                n, m = a.shape
                return a.rearrange("p (k t) -> p k t", k=1).to_broadcast([n, k, m])

            def each(a, m):
                n, k = a.shape
                return a.rearrange("p (k t) -> p k t", t=1).to_broadcast([n, k, m])

            def tri_of(step):
                return tri if step.prompt else cst[0:SAMPLE, TRI_S:TRI_S + SAMPLE]

            def common(step):
                n, o = step.n, step.once
                dve.wait_ge(g_["oc"], value(dve, o + 1))
                dve.wait_ge(g_["s"], further(dve, o + 1))
                if step.prompt:
                    dve.wait_ge(s_["s"], further(dve, o + 1))
                    dve.wait_ge(s_["yc"], further(dve, o + 1))
                dve.tensor_copy(cc[:, 0:n], cm[:, step.cols]).then_inc(both["cc"], 1)
                yield
                yield
                dve.wait_ge(both["br"], value(dve, o + 1))
                dve.wait_ge(both["cc"], further(dve, o + 1))
                dve.tensor_copy(br[32:64, 0:n], cc[32:64, 0:n]).then_inc(g_["brb"], 1)
                yield

            def gdn(step):
                n, o = step.n, step.once
                w = HEADS * n
                dve.wait_ge(g_["rs"], value(dve, o + 1))
                dve.tensor_tensor(view(kn[:, 0:w], 4), proj[:, GK:GK + 4, step.cols], view(rs8[:, w:2 * w], 4), MULT)
                dve.scalar_tensor_tensor(out=view(qn[:, 0:w], 4), in0=proj[:, GQ:GQ + 4, step.cols], scalar=GDN_SCALE,
                                         in1=view(rs8[:, 0:w], 4), op0=MULT, op1=MULT).then_inc(g_["qk"], 1)
                dve.wait_ge(g_["bc"], value(dve, o + 1))
                dve.wait_ge(g_["eg"], further(dve, o + 1))
                for h in range(HEADS):
                    last = dve.tensor_scalar(dd[0:n, h * n:(h + 1) * n], ps[0:n, 2, h * n:(h + 1) * n],
                                             gc[0:n, ROW_A + h:ROW_A + h + 1], 0.0, SUB, MIN)
                last.then_inc(g_["d"], 1)
                yield
                dve.tensor_copy(view(xx[0:n, 0:w], 4), over(ident[0:n, 0:n], 4))
                dve.tensor_copy(view(xt[0:n, 0:w], 4), over(ident[0:n, 0:n], 4)).then_inc(g_["xi"], 1)
                dve.wait_ge(g_["qk"], value(dve, o + 1))
                dve.tensor_tensor(kg[:, 0:w], kn[:, 0:w], eg[:, 0:w], MULT)
                dve.tensor_tensor(qg[:, 0:w], qn[:, 0:w], eg[:, 0:w], MULT).then_inc(g_["kg"], 1)
                dve.wait_ge(g_["kt"], value(dve, o + 1))
                dve.tensor_tensor(view(kd[0:n, :], 4), view(ps[0:n, 2, :], 4), each(rg[0:n, ROW_A:ROW_A + 4], P), MULT).then_inc(g_["kd"], 1)
                dve.wait_ge(g_["dx"], value(dve, o + 1))
                dve.tensor_tensor(view(dd[0:n, 0:w], 4), view(dd[0:n, 0:w], 4), over(tri_of(step), 4), MULT).then_inc(g_["dm"], 1)
                yield
                dve.wait_ge(g_["kk"], value(dve, o + 1))
                dve.wait_ge(g_["dm"], further(dve, o + 1))
                dve.tensor_tensor(aa[0:n, 0:w], ps[0:n, 0, 0:w], dd[0:n, 0:w], MULT)
                dve.tensor_tensor(att[0:n, 0:w], ps[0:n, 1, 0:w], dd[0:n, 0:w], MULT).then_inc(g_["at"], 1)
                dve.wait_ge(g_["at"], value(dve, o + 1))
                dve.tensor_tensor(aa[0:n, 0:w], ps[0:n, 3, 0:w], aa[0:n, 0:w], MULT).then_inc(g_["atb"], 1)
                dve.wait_ge(g_["atb"], value(dve, o + 1))

                def level(l):
                    m = cst[0:n, MASK + l * P:MASK + l * P + n]
                    dve.tensor_tensor(view(al_[0:n, 0:w], 4), view(aa[0:n, 0:w], 4), over(m, 4), MULT).then_inc(g_["al"], 1)

                level(0)
                yield
                for l in range(step.levels):
                    dve.wait_ge(g_["p"], value(dve, step.solve + l + 1))
                    if l < step.levels - 1:
                        level(l + 1)
                    if l == 0:
                        dve.wait_ge(g_["sk"], value(dve, o + 1))
                        dve.tensor_tensor(view(rt[:, 0:w], 4), proj[:, GV:GV + 4, step.cols], view(ps[:, 3, 0:w], 4), SUB).then_inc(g_["rt"], 1)
                    yield
                    dve.wait_ge(g_["q"], value(dve, step.solve + l + 1))
                    if l:
                        dve.wait_ge(g_["x"], further(dve, step.solve + l))
                    else:
                        dve.wait_ge(g_["xi"], further(dve, o + 1))
                    if l < step.levels - 1:
                        dve.tensor_tensor(xx[0:n, 0:w], xx[0:n, 0:w], ps[0:n, 1, 0:w], SUB)
                    dve.tensor_tensor(xt[0:n, 0:w], xt[0:n, 0:w], ps[0:n, 2, 0:w], SUB).then_inc(g_["x"], 1)
                    if l == step.levels - 1:
                        dve.wait_ge(g_["x"], value(dve, step.solve + step.levels))
                        dve.tensor_tensor(view(xt[0:n, 0:w], 4), view(xt[0:n, 0:w], 4), each(tm[0:n, ROW_B:ROW_B + 4], n), MULT).then_inc(g_["tb"], 1)
                    yield
                if step.prompt:
                    dve.wait_ge(g_["su"], value(dve, step.update + 1))
                    for h in range(HEADS):
                        s = gs[:, h * P:(h + 1) * P]
                        last = dve.scalar_tensor_tensor(out=s, in0=s, scalar=eg[:, h * n + n - 1:h * n + n],
                                                        in1=ps[:, 3, h * P:(h + 1) * P], op0=MULT, op1=ADD)
                    last.then_inc(g_["s"], 1)
                else:
                    dve.wait_ge(g_["u"], value(dve, o + 1))
                    for h in range(HEADS):
                        dve.tensor_tensor(view(uexp[0:n, :], 8), over(uu[0:n, h * P:(h + 1) * P], 8),
                                          each(cst[0:n, BMASK:BMASK + 8], P), MULT).then_inc(g_["ue"], 1)
                        dve.wait_ge(g_["su"], value(dve, step.update + h + 1))
                        s = states[:, :, h * P:(h + 1) * P]
                        dve.tensor_tensor(s, s, each(eg[:, h * n + 3:(h + 1) * n:4], P), MULT).then_inc(g_["sm"], 1)
                        dve.wait_ge(g_["sm"], value(dve, step.layer * HEADS + h + 1))
                        last = dve.tensor_tensor(s, s, ps[:, 4:6, :].rearrange("p a (b m) -> p (a b) m", m=P), ADD)
                    last.then_inc(g_["s"], 1)
                yield

            def gla(step):
                n, o = step.n, step.once
                L = gla_prompt if step.prompt else gla_sample
                w = 2 * n
                dve.wait_ge(l_["oc"], value(dve, o + 1))
                dve.wait_ge(l_["s"], further(dve, o + 1))
                dve.tensor_copy(L["rc"][96:128, 0:n], proj[96:128, SMALL, step.cols]).then_inc(l_["rc"], 1)
                dve.tensor_copy(view(L["vc"][:, 0:4 * n], 4), proj[:, LV:LV + 4, step.cols]).then_inc(l_["vc"], 1)
                dve.memset(L["att"][0:n, 0:4 * n], 0.0).then_inc(l_["a0"], 1)
                dve.wait_ge(l_["z"], value(dve, o + 1))
                dve.tensor_tensor(L["z"][0:n, :], ps[0:n, 4, 0:256], prm[0:n, GLAB:GLAB + 256], ADD).then_inc(l_["zt"], 1)
                dve.tensor_scalar(view(L["qs"][:, 0:w], 2), proj[:, LQ:LQ + 2, step.cols], GLA_SCALE, None, MULT)
                dve.tensor_copy(view(L["ks"][:, 0:w], 2), proj[:, LK:LK + 2, step.cols]).then_inc(l_["qk"], 1)
                yield
                dve.wait_ge(l_["a3"], value(dve, o + 1))
                dve.wait_ge(l_["zt"], further(dve, o + 1))
                dve.scalar_tensor_tensor(out=L["gk"][0:n, :], in0=L["z"][0:n, :], scalar=0.0, in1=L["a"][0:n, :], op0=MIN, op1=SUB).then_inc(l_["g1"], 1)
                dve.wait_ge(l_["g1"], value(dve, o + 1))
                dve.tensor_scalar(L["gk"][0:n, :], L["gk"][0:n, :], 1.0 / GLA_NORMALIZER, None, MULT).then_inc(l_["gk"], 1)
                yield
                dve.wait_ge(l_["bt"], value(dve, o + 1))
                dve.wait_ge(l_["qk"], further(dve, o + 1))
                dve.tensor_tensor(L["qe"][:, 0:w], L["qs"][:, 0:w], L["eb"][:, 0:w], MULT)
                dve.tensor_tensor(L["kd"][:, 0:w], L["ks"][:, 0:w], L["er"][:, 0:w], MULT).then_inc(l_["qe"], 1)
                yield

                def by_block(a, m):
                    return a.rearrange("p (b s) -> p b s", s=2 * m)

                for l in range(step.levels):
                    m = 1 << l
                    b = by_block(L["bt"][:, 0:w], m)
                    last = dve.tensor_tensor(by_block(L["dl"][:, l, 0:w], m), b,
                                             b[:, :, m:m + 1].to_broadcast([P, w // (2 * m), 2 * m]), SUB)
                last.then_inc(l_["dl"], 1)
                yield
                dve.wait_ge(l_["d2"], value(dve, o + 1))
                for l in range(step.levels):
                    m = 1 << l
                    d = by_block(L["dl"][:, l, 0:w], m)
                    dve.tensor_tensor(d[:, :, 0:m], by_block(L["ks"][:, 0:w], m)[:, :, 0:m], d[:, :, 0:m], MULT)
                    last = dve.tensor_tensor(d[:, :, m:], by_block(L["qs"][:, 0:w], m)[:, :, m:], d[:, :, m:], MULT)
                last.then_inc(l_["ml"], 1)
                yield
                for l in range(step.levels + 1):
                    dve.wait_ge(l_["at"], value(dve, step.score + l + 1))
                    if l:
                        dve.wait_ge(l_["cp"], further(dve, step.score + l))
                    else:
                        dve.wait_ge(l_["a0"], further(dve, o + 1))
                    c = MASK + l * P if l < step.levels else IDENT
                    for e in range(2):
                        last = dve.copy_predicated(view(L["att"][0:n, e * w:(e + 1) * w], 2), over(cst[0:n, c:c + n], 2).bitcast(U32),
                                                   view(ps[0:n, 4 + e, 0:w], 2))
                    last.then_inc(l_["cp"], 1)
                    yield
                yield
                if step.prompt:
                    dve.wait_ge(l_["su"], value(dve, step.update + 1))
                    for g in range(2):
                        s = ls[:, g * P:(g + 1) * P]
                        last = dve.scalar_tensor_tensor(out=s, in0=s, scalar=L["eb"][:, g * n + n - 1:g * n + n],
                                                        in1=ps[:, 4, g * P:(g + 1) * P], op0=MULT, op1=ADD)
                    last.then_inc(l_["s"], 1)
                else:
                    dve.wait_ge(l_["vt"], value(dve, o + 1))
                    for h in range(HEADS):
                        r, g = slice(64 * (h % 2), 64 * (h % 2) + 64), h // 2
                        dve.tensor_tensor(vexp[0:n, :, :], over(L["vt"][0:n, h * P:(h + 1) * P], 8),
                                          each(cst[0:n, BMASK:BMASK + 8], P), MULT).then_inc(l_["ve"], 1)
                        dve.wait_ge(l_["su"], value(dve, step.update + h + 1))
                        s = states[r, :, g * P:(g + 1) * P]
                        dve.tensor_tensor(s, s, each(L["eb"][r, g * n + 3:(g + 1) * n:4], P), MULT).then_inc(l_["sm"], 1)
                        dve.wait_ge(l_["sm"], value(dve, step.layer * HEADS + h + 1))
                        last = dve.tensor_tensor(s, s, ps[r, 0:2, :].rearrange("p a (b m) -> p (a b) m", m=P), ADD)
                    last.then_inc(l_["s"], 1)
                yield

            def ssd(step):
                n, o = step.n, step.once
                S = ssd_prompt if step.prompt else ssd_sample
                w = SSD_HEADS * n
                dve.wait_ge(s_["bc"], value(dve, o + 1))
                dve.wait_ge(s_["ea"], further(dve, o + 1))
                for h in range(SSD_HEADS):
                    last = dve.tensor_scalar(S["dd"][0:n, h * n:(h + 1) * n], ps[0:n, 6 + h // 4, h % 4 * n:(h % 4 + 1) * n],
                                             gc[0:n, ROW_DT + h:ROW_DT + h + 1], 0.0, SUB, MIN)
                last.then_inc(s_["d"], 1)
                yield
                dve.wait_ge(s_["st"], value(dve, o + 1))
                for g in range(2):
                    c = slice(4 * g * n, 4 * (g + 1) * n)
                    last = dve.tensor_tensor(view(S["ce"][:, c], 4), view(S["ea"][:, c], 4), over(S["xbc"][:, (6 + g) * n:(7 + g) * n], 4), MULT)
                last.then_inc(s_["ce"], 1)
                yield
                dve.wait_ge(s_["tr"], value(dve, o + 1))
                dve.tensor_tensor(view(S["xd"][0:n, :], 8), view(ps[0:n, 6, :], 8), each(tm[0:n, 96:104], 64), MULT).then_inc(s_["xd"], 1)
                dve.wait_ge(s_["dx"], value(dve, o + 1))
                dve.tensor_tensor(view(S["dd"][0:n, 0:w], 8), view(S["dd"][0:n, 0:w], 8), over(tri_of(step), 8), MULT).then_inc(s_["dm"], 1)
                dve.wait_ge(s_["xd"], value(dve, o + 1))
                dve.wait_ge(both["rg"], further(dve, o + 1))
                dve.tensor_tensor(view(S["xe"][0:n, :], 8), view(S["xd"][0:n, :], 8), each(rg[0:n, ROW_DT:ROW_DT + 8], 64), MULT).then_inc(s_["xe"], 1)
                dve.wait_ge(s_["dm"], value(dve, o + 1))
                dve.wait_ge(s_["bt"], further(dve, o + 1))
                for g in range(2):
                    c = slice(4 * g * n, 4 * (g + 1) * n)
                    last = dve.tensor_tensor(view(S["dd"][0:n, c], 4), view(S["dd"][0:n, c], 4), over(ps[0:n, 7, g * n:(g + 1) * n], 4), MULT)
                last.then_inc(s_["att"], 1)
                yield
                dve.wait_ge(s_["y"], value(dve, o + 1))
                for t in range(4):
                    last = dve.scalar_tensor_tensor(out=proj[:, SX + t, step.cols], in0=S["xbc"][:, t * n:(t + 1) * n],
                                                    scalar=prm[:, SSDD + t:SSDD + t + 1],
                                                    in1=ps[:, 6, t * n:(t + 1) * n], op0=MULT, op1=ADD)
                last.then_inc(s_["yc"], 1)
                yield
                if step.prompt:
                    dve.tensor_tensor(view(ss_[:, :], 8), view(ss_[:, :], 8), each(S["ea"][:, n - 1:w:n], 64), MULT).then_inc(s_["sm"], 1)
                    dve.wait_ge(s_["su"], value(dve, step.update2 + 1))
                    dve.wait_ge(s_["sm"], further(dve, step.update2 + 1))
                    dve.tensor_tensor(ss_[:, :], ss_[:, :], ps[:, 7, :], ADD).then_inc(s_["s"], 1)
                else:
                    for g in range(2):
                        dve.tensor_tensor(view(xexp[0:n, :], 8), over(S["xe"][0:n, g * 256:(g + 1) * 256], 8),
                                          each(cst[0:n, BMASK:BMASK + 8], 256), MULT).then_inc(s_["xe2"], 1)
                        dve.wait_ge(s_["su"], value(dve, step.update2 + g + 1))
                        for h in range(4 * g, 4 * g + 4):
                            s = states[:, :, h * 64:(h + 1) * 64]
                            last = dve.tensor_tensor(s, s, each(S["ea"][:, h * n + 3:(h + 1) * n:4], 64), MULT)
                        last.then_inc(s_["sm"], 1)
                        dve.wait_ge(s_["sm"], value(dve, step.update2 + g + 1))
                        s = states[:, :, g * 256:(g + 1) * 256]
                        last = dve.tensor_tensor(s, s, ps[:, 0:4, :].rearrange("p a (b m) -> p (a b) m", m=256), ADD)
                    last.then_inc(s_["s"], 1)
                yield
                yield

            def branch_norm(layer, b):
                if b == 2:
                    dve.wait_ge(s_["yc"], value(dve, layer * STEPS + (STEPS + 1)))
                    y = proj[:, SX:SX + 4, :]
                    dve.tensor_tensor(y, y, proj[:, SZ:SZ + 4, :], MULT).then_inc(n_["yz"], 1)
                    dve.wait_ge(n_["yz"], value(dve, layer + 1))
                dve.wait_ge(n_["rs"], further(dve, layer * 3 + b + 1))
                o = layer * 3 + b
                if b < 2:
                    c = (GDNN, GLAN)[b]
                    v = (GV, LV)[b]
                    for t in range(4):
                        last = dve.scalar_tensor_tensor(out=nt[:, t, :], in0=proj[:, v + t, :], scalar=prm[:, c:c + 1],
                                                        in1=nrs[:, t, :], op0=MULT, op1=MULT)
                    last.then_inc(n_["t"], 1)
                    dve.wait_ge(n_["t"], value(dve, layer * 2 + b + 1))
                    z = (GZ, LG)[b]
                    dve.tensor_tensor(nt[:, :, :], nt[:, :, :], proj[:, z:z + 4, :], MULT).then_inc(n_["tz"], 1)
                else:
                    for t in range(4):
                        last = dve.scalar_tensor_tensor(out=nt[:, t, :], in0=proj[:, SX + t, :],
                                                        scalar=prm[:, SSDN + t:SSDN + t + 1],
                                                        in1=nrs[:, t // 2, :], op0=MULT, op1=MULT)
                    last.then_inc(n_["tz"], 1)
                dve.wait_ge(n_["hi"], value(dve, o + 1))
                dve.wait_ge(n_["tz"], further(dve, o + 1))
                dve.tensor_tensor(ol[b][:, :, :], nt[:, :, :], oh[b][:, :, :].bitcast(F32), SUB).then_inc(n_["lo"], 1)
                dve.wait_ge(n_["lo"], value(dve, o + 1))

            with dve.Fori(0, DEPTH) as layer:
                dve.wait_ge(prm_in, value(dve, layer * 16 + 16))
                ffn(layer, 0, B_FFN1, F1PRE, F1POST)
                pre_norm(layer, 2, 1, MPRE)
                project(layer)
                dve.wait_ge(evict_done, value(dve, layer * 40 + 44))
                narrow_columns(layer)
                dve.wait_ge(cs_saved, value(dve, layer * 32 + 32))
                for state in (gs, ls, ss_):
                    dve.memset(state[:, :], 0.0).then_inc(zeroed, 1)
                with dve.Fori(0, CHUNKS) as c:
                    step = prompt_step(layer, c)
                    together(common(step), gdn(step), gla(step), ssd(step))
                step = sample_step(layer)
                for b, stages in enumerate(((common(step), gdn(step)), (gla(step),), (ssd(step),))):
                    alone(*stages)
                    branch_norm(layer, b)
                dve.wait_ge(st_out, value(dve, layer * 96 + 96))
                split_in(layer, 2, MPRE)
                with dve.Fori(0, KD // 2) as i:
                    dve.wait_ge(sg_done, value(dve, layer * 24 + i * 6 + 2))
                    dve.tensor_copy(bm[:, :].rearrange("p (r k) -> p r k", k=2),
                                    prm[:, BMERGE:BMERGE + 24].rearrange("p (r m) -> p r m", m=8)
                                    [:, :, bass.ds(i * 2, 2)]).then_inc(bm_ready, 1)
                    for u in range(6):
                        r, k = u % 3, u // 3
                        dve.wait_ge(blk_done, value(dve, layer * BLOCKS + i * 12 + (B_MERGE + 2 * u + 2 + SPLIT)))
                        dve.wait_ge(sg_done, further(dve, layer * 24 + i * 6 + (u + 3)))
                        dve.wait_ge(mac_done, further(dve, layer * 24 + i * 6 + (u + 2)))
                        dst = mac[:, k, :] if r == 0 else mt_[:, 0, :]
                        last = dve.tensor_tensor(halves(dst), halves(sg[:, u % 2, :]), pair((2 * u + 1) % 4), MULT)
                        if r:
                            last.then_inc(mac_tmp, 1)
                            dve.wait_ge(mac_tmp, value(dve, layer * 16 + i * 4 + (2 * k + r)))
                            last = dve.tensor_tensor(mac[:, k, :], mac[:, k, :], mt_[:, 0, :], ADD)
                        last.then_inc(mac_done, 1)
                        if r == 2:
                            dve.wait_ge(mac_done, value(dve, layer * 24 + i * 6 + (u + 3)))
                            dve.wait_ge(mh_done, further(dve, layer * KD + i * 2 + (k + 1)))
                            m = bass.ds(i * 2 + k, 1)
                            dve.tensor_tensor(ml[:, m, :].rearrange("p k t -> p (k t)"), mac[:, k, :],
                                              mh[:, m, :].rearrange("p k t -> p (k t)").bitcast(F32), SUB).then_inc(ml_done, 1)
                post_norm(layer, 3, MPOST, 1.0)
                ffn(layer, 1, B_FFN2, F2PRE, F2POST)


COLS = dict(qkv=0, z=1536, a=2048, b=2052, q=2056, r=3592, sz=3608, dt=5144, gate=5152)


def tiles(w):
    w = np.asarray(w)
    n, k, m = w.shape
    return np.ascontiguousarray(w.reshape(n, k // P, P, m // P, P).transpose(0, 3, 2, 1, 4).reshape(n * m // P, P, k))


def pack(a):
    a = {k: np.asarray(v) for k, v in a.items()}
    out = {}
    tokens = np.concatenate([a["x_prompt"].reshape(SEQ, D_MODEL), a["x_sample"].reshape(SAMPLE, D_MODEL)])
    out["x"] = tokens.T.reshape(KD, P, T).transpose(1, 0, 2).reshape(P, KD * T)

    ups, downs = [], []
    for l in range(DEPTH):
        for f in ("ffn1", "ffn2"):
            g, u = tiles(a[f + "_w_gate"][l:l + 1]), tiles(a[f + "_w_up"][l:l + 1])
            ups.append(np.stack([g, u], 1).reshape(UPS, P, D_MODEL))
            downs.append(tiles(a[f + "_w_down"][l:l + 1]))
    out["up"], out["down"] = np.concatenate(ups), np.concatenate(downs)
    w = a["w_in"]
    wide = np.concatenate([w[:, :, COLS["qkv"]:COLS["a"]], w[:, :, COLS["q"]:COLS["r"]], w[:, :, COLS["sz"]:COLS["dt"]]], 2)
    out["win"] = tiles(wide)
    small = np.zeros((DEPTH, D_MODEL, P), w.dtype)
    small[:, :, ROW_A:ROW_A + 4] = w[:, :, COLS["a"]:COLS["a"] + 4]
    small[:, :, ROW_B:ROW_B + 4] = w[:, :, COLS["b"]:COLS["b"] + 4]
    small[:, :, ROW_DT:ROW_DT + 8] = w[:, :, COLS["dt"]:COLS["dt"] + 8]
    small[:, :, ROW_R:ROW_R + 16] = w[:, :, COLS["r"]:COLS["r"] + 16]
    out["narrow"] = tiles(small)
    gate = tiles(w[:, :, COLS["gate"]:]).reshape(DEPTH, 3, KD, P, D_MODEL)
    out["gate"] = gate.transpose(0, 2, 1, 3, 4).reshape(DEPTH * 24, P, D_MODEL)
    br = np.stack([tiles(a["w_br_" + s]).reshape(DEPTH, KD, P, 512) for s in ("gdn", "gla", "ssd")], 2)
    out["branch"] = br.reshape(DEPTH * 24, P, 512)
    out["wout"] = tiles(a["w_out"])

    prm = np.zeros((DEPTH, P, NPRM), np.float32)

    def cols(c, v):
        v = v.reshape(DEPTH, -1, P)
        prm[:, :, c:c + v.shape[1]] = v.transpose(0, 2, 1)

    for c, s in ((F1PRE, "ffn1_norm_pre"), (F1POST, "ffn1_norm_post"), (MPRE, "mix_norm_pre"), (MPOST, "mix_norm_post"),
                 (F2PRE, "ffn2_norm_pre"), (F2POST, "ffn2_norm_post"), (BMERGE, "b_merge"), (GDNN, "gdn_norm"),
                 (GLAN, "gla_norm"), (SSDN, "ssd_norm")):
        cols(c, a[s])
    conv = np.concatenate([a["gdn_conv_w"], a["ssd_conv_w"]], 1).reshape(DEPTH, CONV_TILES, P, CONV)
    prm[:, :, CONVW:CONVW + 80] = conv.transpose(0, 2, 1, 3).reshape(DEPTH, P, 80)
    cols(CONVB + 12, a["ssd_conv_b"])
    cols(SSDD, np.repeat(a["ssd_D"], 64, axis=1))
    prm[:, ROW_A:ROW_A + 4, SBIAS] = a["gdn_dt_bias"]
    prm[:, ROW_DT:ROW_DT + 8, SBIAS] = a["ssd_dt_bias"]
    prm[:, ROW_A:ROW_A + 4, ALOG] = a["gdn_A_log"]
    prm[:, ROW_DT:ROW_DT + 8, ALOG] = a["ssd_A_log"]
    prm[:, :, SIGN] = 1.0
    prm[:, ROW_B:ROW_B + 32, SIGN] = -1.0
    prm[:, :, GLAB:GLAB + 256] = a["gla_gate_bias"][:, None, :]
    prm[:, ROW_R:ROW_R + 16, GUP:GUP + 256] = a["gla_gate_up"]
    out["prm"] = prm

    cst = np.zeros((P, NCONST), np.float32)
    j, i = np.meshgrid(np.arange(P), np.arange(P), indexing="ij")
    cst[:, IDENT:IDENT + P] = j == i
    cst[:, TRI:TRI + P] = i >= j
    cst[:, REV:REV + P] = j > i
    for l in range(LEVELS):
        m = 1 << l
        cst[:, MASK + l * P:MASK + (l + 1) * P] = (j // (2 * m) == i // (2 * m)) & (j % (2 * m) < m) & (i % (2 * m) >= m)
    cst[:, ONES:ONES + P] = 1.0
    n = SAMPLE
    same = (j // DEC_SEQ == i // DEC_SEQ)[:n, :n]
    cst[:n, TRI_S:TRI_S + n] = same & (i >= j)[:n, :n]
    cst[:n, REV_S:REV_S + n] = same & (j > i)[:n, :n]
    cst[:n, BMASK:BMASK + 8] = np.arange(n)[:, None] // DEC_SEQ == np.arange(8)[None, :]
    cst[:, EPSC] = EPS
    cst[:, EPSROW] = EPS * D_MODEL / P
    out["cst"] = cst

    cs = np.concatenate([a["state_gdn_conv"], a["state_ssd_conv"]], 3)
    cs = cs.reshape(DEPTH, DEC_BATCH, 3, CONV_TILES, P).transpose(0, 4, 3, 1, 2)
    out["in_conv"] = cs.reshape(DEPTH, P, CONV_TILES * DEC_BATCH * 3)
    out["in_gdn"] = a["state_gdn"].transpose(0, 3, 1, 2, 4).reshape(DEPTH, P, DEC_BATCH, 512)
    gla = a["state_gla"].reshape(DEPTH, DEC_BATCH, 2, 2, 64, P)
    out["in_gla"] = gla.transpose(0, 3, 4, 1, 2, 5).reshape(DEPTH, P, DEC_BATCH, 256)
    out["in_ssd"] = a["state_ssd"].transpose(0, 4, 1, 2, 3).reshape(DEPTH, P, DEC_BATCH, 512)
    return {k: np.ascontiguousarray(v) for k, v in out.items()}


OUTS = {
    "y": (P, KD * T),
    "out_p_conv": (DEPTH, P, CONV_TILES, 3), "out_s_conv": (DEPTH, P, CONV_TILES, DEC_BATCH * 3),
    "out_p_gdn": (DEPTH, P, 512), "out_p_gla": (DEPTH, P, 256), "out_p_ssd": (DEPTH, P, 512),
    "out_s_gdn": (DEPTH, P, DEC_BATCH, 512), "out_s_gla": (DEPTH, P, DEC_BATCH, 256), "out_s_ssd": (DEPTH, P, DEC_BATCH, 512),
}


def unpack(r):
    y = r["y"].reshape(P, KD, T).transpose(2, 1, 0).reshape(T, D_MODEL)
    outs = [y[:SEQ].reshape(1, SEQ, D_MODEL), y[SEQ:].reshape(DEC_BATCH, DEC_SEQ, D_MODEL)]
    for k, nb in (("p", 1), ("s", DEC_BATCH)):
        conv = r[f"out_{k}_conv"].reshape(DEPTH, P, CONV_TILES, nb, 3).transpose(0, 3, 4, 2, 1).reshape(DEPTH, nb, 3, CONV_TILES * P)
        gdn = r[f"out_{k}_gdn"].reshape(DEPTH, P, nb, HEADS, P).transpose(0, 2, 3, 1, 4)
        gla = r[f"out_{k}_gla"].reshape(DEPTH, 2, 64, nb, 2, P).transpose(0, 3, 4, 1, 2, 5).reshape(DEPTH, nb, HEADS, 64, P)
        ssd = r[f"out_{k}_ssd"].reshape(DEPTH, P, nb, SSD_HEADS, 64).transpose(0, 2, 3, 4, 1)
        outs += [conv[..., :12 * P], gdn, gla, conv[..., 12 * P:], ssd]
    return tuple(np.ascontiguousarray(o) for o in outs)


def kernel(**inputs):
    import concourse.bacc as bacc
    from concourse.bass_utils import run_bass_kernel_spmd

    arrays = pack(inputs)
    nc = bacc.Bacc("TRN2", target_bir_lowering=False, num_devices=1)
    io = {k: nc.dram_tensor("in_" + k, v.shape, mybir.dt.from_np(v.dtype), kind="ExternalInput").ap() for k, v in arrays.items()}
    for k, shape in OUTS.items():
        io[k] = nc.dram_tensor("res_" + k, shape, F32, kind="ExternalOutput").ap()
    trunk(nc, io)
    r = run_bass_kernel_spmd(nc, [{"in_" + k: v for k, v in arrays.items()}], core_ids=[0])
    return unpack({k: r.results[0]["res_" + k] for k in OUTS})
```

```python
from contextlib import ExitStack

import concourse.bass as bass
import numpy as np
from concourse import mybir

P = 128
D_MODEL, DEPTH, D_FF = 1024, 2, 2816
SEQ, DEC_BATCH, DEC_SEQ = 512, 8, 4
SAMPLE = DEC_BATCH * DEC_SEQ
T = SEQ + SAMPLE
HALF = T // 2
KD = D_MODEL // P
KF = D_FF // P
EPS = 1e-6
C = 128
CHUNKS = SEQ // C
STEPS = CHUNKS + 1
HEADS = 4
SSD_HEADS = 8
GDN_SCALE, GLA_SCALE = 128 ** -0.5, 64 ** -0.5
GLA_NORMALIZER = 16.0
CONV = 4
LEVELS, SAMPLE_LEVELS = 7, 2

GQ, GK, GV, GZ = 0, 4, 8, 12
LQ, LK, LV, LG = 16, 18, 20, 24
SZ, SX, SB, SC = 28, 32, 36, 38
SMALL = 40
TILES = 41
CONV_TILES = 20
ROW_A, ROW_B, ROW_DT, ROW_R = 0, 32, 64, 96

(F1PRE, F1POST, MPRE, MPOST, F2PRE, F2POST) = range(0, 48, 8)
BMERGE, CONVW, CONVB = 48, 72, 152
GDNN, GLAN, SSDN, SSDD = 172, 173, 174, 178
SBIAS, ALOG, SIGN = 182, 183, 184
GLAB, GUP, NPRM = 192, 448, 704

IDENT, TRI, REV, MASK = 0, 128, 256, 384
ONES = MASK + LEVELS * 128
TRI_S, REV_S, BMASK, EPSC, EPSROW = ONES + 128, ONES + 160, ONES + 192, ONES + 200, ONES + 201
NCONST = ONES + 204

UPS, DOWNS = 2 * KF, 3 * KD
FFN_BLOCKS = UPS + DOWNS
B_FFN1, B_PROJ = 0, FFN_BLOCKS
B_MERGE = B_PROJ + 4 + 40
B_OUT = B_MERGE + 6 * KD
B_FFN2 = B_OUT + KD
BLOCKS = B_FFN2 + FFN_BLOCKS
RAW, SPLIT = 4, 2
DOWN_K = (8, 8, 6)
assert all(b % RAW == 0 for b in (B_PROJ, B_MERGE, B_OUT, B_FFN2, BLOCKS))

F32, F32R, U32 = mybir.dt.float32, mybir.dt.float32r, mybir.dt.uint32
ACT, ALU = mybir.ActivationFunctionType, mybir.AluOpType
MULT, ADD, SUB, MIN, MAX = ALU.mult, ALU.add, ALU.subtract, ALU.min, ALU.max
LN_EXP = "natural_log_exp_and_others"


SOLVES = CHUNKS * (LEVELS - 1) + SAMPLE_LEVELS - 1
SCORES = CHUNKS * (LEVELS + 1) + SAMPLE_LEVELS + 1
SUMS = (1, 3, 4, 6, 7, 9)


class Step:

    def __init__(self, layer, n, states, levels, cols, c):
        self.c = c
        self.layer, self.n, self.states, self.levels = layer, n, states, levels
        self.cols = cols
        self.prompt = states == 1
        self.once = layer * STEPS + c
        self.solve = layer * SOLVES + c * (LEVELS - 1)
        self.inner = (layer * CHUNKS + c) * (LEVELS - 2)
        self.level = layer * (CHUNKS * LEVELS + SAMPLE_LEVELS) + c * LEVELS
        self.score = layer * SCORES + c * (LEVELS + 1)
        self.update = layer * (CHUNKS + HEADS) + c
        self.update2 = layer * (CHUNKS + 4) + c


def prompt_step(layer, c):
    return Step(layer, C, 1, LEVELS, bass.ds(c * C, C), c)


def sample_step(layer):
    return Step(layer, SAMPLE, DEC_BATCH, SAMPLE_LEVELS, slice(SEQ, T), CHUNKS)


ORDER = "clclcllggllgslggslgsglgslgslgslglglglgggg"
SAMPLE_ORDER = "clclclglsgsglsglglglllllsllslslsgsgsgsggggggggg"
NORM_ORDER = (2, 0, 1)
FIRST = 0


def together(order, common, gdn, gla, ssd):
    branch = dict(c=common, g=gdn, l=gla, s=ssd)
    for name in order:
        next(branch[name])
    for stages in branch.values():
        assert next(stages, "through") == "through"


def trunk(nc, io):
    ctx = ExitStack()
    with ctx:
        base = -(-nc.sbuf_base // 64) * 64

        def at(name, offset, shape, dt=F32):
            return nc.alloc_sbuf_tensor_at(name, shape, dt, offset=base + offset)

        def sem(name):
            return ctx.enter_context(nc.semaphore(name))

        TB = T * 4
        place = [0]

        def put(name, shape, dt=F32):
            size = 4 * int(np.prod(shape[1:]))
            t = at(name, place[0], shape, dt)
            place[0] += -(-size // 32) * 32
            return t

        x = put("x", [P, KD, T])
        RING = place[0]
        raw = put("raw", [P, RAW, KD, P])
        wh = put("wh", [P, SPLIT, KD, P], F32R)
        wl = put("wl", [P, SPLIT, KD, P], F32R)
        cst = put("cst", [P, NCONST])
        prm = put("prm", [P, NPRM])
        rstd = put("rstd", [P, T])
        RSTD_POST = place[0]
        rstd_post = put("rstd_post", [P, T])
        nega = put("nega", [P, 1])
        cw = put("cw", [P, 16])
        cb = put("cb", [P, 4])
        bm = put("bm", [P, 6])
        R = place[0]
        assert base + R + 68 * TB <= nc.sbuf_usable_end, (base + R + 68 * TB, nc.sbuf_usable_end)

        def row(name, r, shape, dt=F32, more=0):
            return at(name, R + r * TB + more, shape, dt)

        hh, hl = row("hh", 0, [P, KD, T], F32R), row("hl", 8, [P, KD, T], F32R)
        ah, al = row("ah", 16, [P, KF, T], F32R), row("al", 38, [P, KF, T], F32R)
        f = row("f", 60, [P, KD, T])
        hf = row("hf", 60, [P, KD, T])
        sq = row("sq", 0, [P, KD, T])
        sil, prod = row("sil", 60, [P, 2, T]), row("prod", 62, [P, 2, T])
        proj = row("proj", 16, [P, TILES, T])
        PADW = 3 + SEQ + DEC_BATCH * (3 + DEC_SEQ)
        CW = PADW - 3
        pad = row("pad", 60, [P, 4, PADW])
        cacc = row("cacc", 57, [P, 2, PADW])
        cs_in = row("cs_in", 65, [P, CONV_TILES, DEC_BATCH, 3])
        cs_p = row("cs_p", 66, [P, CONV_TILES, 3])
        cs_s = row("cs_s", 66, [P, CONV_TILES, DEC_BATCH, 3], more=256)
        assert 4 * 4 * PADW <= 5 * TB and 2 * 4 * PADW <= 3 * TB
        sp, se, sl = (row(s, 16 + SX + i, [P, T]) for i, s in enumerate(("sp", "se", "sl")))
        cm = at("cm", RSTD_POST, [P, T])
        cc, tm, gc = (row(s, 57, [P, P], more=512 * i) for i, s in enumerate(("cc", "tm", "gc")))
        br, rg = (row(s, 59, [P, P], more=512 * i) for i, s in enumerate(("br", "rg")))
        states = row("states", 60, [P, DEC_BATCH, 512])

        def work(name, k, units=1, dt=F32):
            return at(name, R + 2048 * k, [P, 512 * units], dt)

        (kn, qn, _, _, eg, dd, aa, att, al_, xx, xt, pp, rt, rr, uu, kd, gs) = (
            work(f"g{i}", i) for i in range(17))
        kqg = at("kqg", R + 2048 * 2, [P, 2, 512])
        kg, qg = kqg[:, 0, :], kqg[:, 1, :]
        sq8, rs8 = work("sq8", 0, 2), work("rs8", 5, 2)
        uexp = work("uexp", 9, 2)
        gla_sample = dict(
            {n: at(f"t_{n}", RING + 17408 + 1024 * i, [P, 256]) for i, n in enumerate("gk a kt".split())},
            vt=at("t_vt", RING + 26624, [P, 512]),
            **{n: at(f"t_{n}", RING + 28672 + 256 * i, [P, 2 * SAMPLE]) for i, n in enumerate("bt eb er qs qe kd ks".split())},
            dl=at("t_dl", RING + 30464, [P, SAMPLE_LEVELS, 2 * SAMPLE]),
            att=at("t_att", RING + 30976, [P, HEADS * SAMPLE]),
            rc=at("t_rc", R + 58 * TB, [P, SAMPLE]), vc=at("t_vc", R + 58 * TB + 128, [P, 4 * SAMPLE]),
            z=at("t_z", R + 58 * TB + 1024, [P, 256]))
        vexp = at("vexp", RING + 22528, [P, DEC_BATCH, P])
        F0, W0 = R + 60 * TB, RING + 24576
        gla_prompt = dict(
            dl=at("l_dl", F0, [P, LEVELS, 256]),
            **{n: at(f"l_{n}", F0 + 7168 + 2048 * i, [P, 512]) for i, n in enumerate(("att", "vc", "vt"))},
            **{n: at(f"l_{n}", F0 + 13312 + 1024 * i, [P, 256]) for i, n in enumerate("z a gk bt".split())},
            **{n: at(f"l_{n}", W0 + 1024 * i, [P, 256]) for i, n in enumerate("eb er qs qe kd ks kt s".split())},
            rc=at("l_rc", R + 58 * TB, [P, P]))
        ls = gla_prompt["s"]
        ssd_prompt = dict(
            {n: at(f"s_{n}", RING + 4096 * i, [P, 1024]) for i, n in enumerate("xbc ea dd ce".split())},
            **{n: at(f"s_{n}", RING + 16384 + 2048 * i, [P, 512]) for i, n in enumerate("xd xe s bt".split())})
        ssd_sample = dict(
            {n: at(f"u_{n}", RING + 1024 * i, [P, 256]) for i, n in enumerate("xbc ea dd ce bt".split())},
            **{n: at(f"u_{n}", RING + 5120 + 2048 * i, [P, 512]) for i, n in enumerate("xd xe".split())})
        ss_ = ssd_prompt["s"]
        xexp = at("xexp", RING + 9216, [P, 2048])
        gla_states = proj[:, LQ:LQ + 4, 0:512].rearrange("p t (e n) -> p t e n", e=2)
        ssd_states = proj[:, GQ:GQ + 8, 0:512]
        nsq = row("nsq", 0, [P, 4, T])
        nrs = [row(f"nrs{i}", r, [P, 4, T]) for i, r in enumerate((12, 4, 20))]
        nt = [row(f"nt{i}", r, [P, 4, T]) for i, r in enumerate((8, 8, 16))]
        oh = [row(f"oh{i}", 16 + r, [P, 4, T], F32R) for i, r in enumerate((GV, LG, SX))]
        ol = [row(f"ol{i}", 16 + r, [P, 4, T], F32R) for i, r in enumerate((GZ, SB, SZ))]
        mh, ml = row("mh", 16 + GQ, [P, KD, T], F32R), row("ml", 16 + LQ, [P, KD, T], F32R)
        sg, mt_, mac = row("sg", 60, [P, 2, T]), row("mt", 62, [P, 1, T]), row("mac", 63, [P, 2, T])

        ps = ctx.enter_context(nc.psum_tensor("ps", [P, 8, 512], F32))

        ident, tri, rev = (cst[:, a:a + P] for a in (IDENT, TRI, REV))
        ones = cst[:, ONES:ONES + P]
        epsc = cst[:, EPSC:EPSC + 1]

        def pair(slot):
            return ps[:, 2 * slot:2 * slot + 2, 0:HALF]

        def halves(ap):
            return ap.rearrange("p (a t) -> p a t", a=2)

        started = sem("started")
        loaded = sem("loaded")
        prm_in = sem("prm_in")
        raw_full = [sem(f"raw_full{i}") for i in range(RAW)]
        hi_done, lo_done = sem("hi_done"), sem("lo_done")
        blk_done = sem("blk_done")
        sq_ready, sum_ready, ln_ready, rstd_ready = (sem(s) for s in ("sq_ready", "sum_ready", "ln_ready", "rstd_ready"))
        x_tmp, x_done = sem("x_tmp"), sem("x_done")
        hf_ready, hh_ready, hl_ready = sem("hf_ready"), sem("hh_ready"), sem("hl_ready")
        sil_done, prod_done = sem("sil_done"), sem("prod_done")
        ah_done, al_done = sem("ah_done"), sem("al_done")
        out_done = sem("out_done")
        evict_done, small_done = sem("evict_done"), sem("small_done")
        pad_zero, tap, conv_done, csil_done = (sem(s) for s in ("pad_zero", "tap", "conv_done", "csil_done"))
        cs_loaded, cs_saved, cw_ready = sem("cs_loaded"), sem("cs_saved"), sem("cw_ready")
        narrow = {s: sem("n_" + s) for s in ("alog", "z", "abs", "exp", "ln", "sp", "beta", "dt")}
        both = {s: sem("r_" + s) for s in "cc tmp tm cum gc rg br".split()}
        g_ = {s: sem("g_" + s) for s in (
            "xx qx xtt bc d dx dm brb sq ss ln rs qk kk kt eg kg at atb xi kd al p pc q x "
            "tb sk rt rtt r up u o oc su sm s ue").split()}
        l_ = {s: sem("l_" + s) for s in (
            "rc z zt a1 a2 a3 g1 gk b bt qk qe dl d1 d2 ml at cp vc vtp vt kdp kt o oc ve su sm s").split()}
        s_ = {s: sem("s_" + s) for s in (
            "bc d dx dm sa st tr ea ce att xd xe bt y yc xe2 su sm s").split()}
        zeroed = sem("zeroed")
        st_in = [sem(f"st_in{b}") for b in range(3)]
        st_prompt, st_out = sem("st_prompt"), sem("st_out")
        n_ = {s: sem("o_" + s) for s in ("yz", "sq", "ss", "ln", "rs", "t", "tz", "hi", "lo")}
        sg_done, mac_tmp, mac_done, mh_done, ml_done, bm_ready = (
            sem(s) for s in ("sg_done", "mac_tmp", "mac_done", "mh_done", "ml_done", "bm_ready"))
        saved = sem("saved")

        def value(eng, v):
            eng.compute_val(v)
            eng.wait_ge(started, 1)
            return v

        def further(eng, v):
            eng.compute_val(v)
            eng.wait_ge(loaded, 32)
            return v

        block = ctx.enter_context(nc.Block())

        @block.sync
        def _(sp_):
            sp_.dma_start(cst[:], io["cst"]).then_inc(loaded, 16)
            sp_.dma_start(x[:], io["x"].rearrange("p (k t) -> p k t", k=KD)).then_inc(loaded, 16)

            def blocks(layer, first, i, nks, source):
                for j, nk in enumerate(nks):
                    sp_.wait_ge(lo_done, value(sp_, layer * BLOCKS + i * len(nks) + (first + j + 1)))
                    sp_.dma_start(raw[:, j % RAW, 0:nk, :], source(j)).then_inc(raw_full[j % RAW], 16)

            def tiles(name, index):
                return io[name][bass.ds(index, 1)].rearrange("a p (k m) -> p (a k) m", m=P)

            def ffn(layer, which, first):
                with sp_.Fori(0, KF // 2) as i:
                    blocks(layer, first, i, (KD,) * 4,
                           lambda j: tiles("up", layer * (2 * UPS) + i * 4 + (which * UPS + j)))
                k0 = np.cumsum((0,) + DOWN_K)
                with sp_.Fori(0, 2) as i:
                    blocks(layer, first + UPS, i, DOWN_K * 4,
                           lambda j: tiles("down", layer * (2 * KD) + i * 4 + (which * KD + j // 3))
                           [:, k0[j % 3]:k0[j % 3 + 1], :])

            with sp_.Fori(0, DEPTH) as layer:
                sp_.wait_ge(x_done, value(sp_, layer * (3 * KD) + 1))
                sp_.dma_start(prm[:], io["prm"][bass.ds(layer, 1)].rearrange("a p n -> (a p) n")).then_inc(prm_in, 16)
                ffn(layer, 0, B_FFN1)
                blocks(layer, B_PROJ, 0, (2,) * 4,
                       lambda j: tiles("narrow", layer)[:, 2 * j:2 * j + 2, :])
                with sp_.Fori(0, 10) as i:
                    blocks(layer, B_PROJ + 4, i, (KD,) * 4, lambda j: tiles("win", layer * 40 + i * 4 + j))
                sp_.wait_ge(l_["s"], value(sp_, layer * STEPS + (STEPS + 1)))
                sp_.wait_ge(s_["s"], value(sp_, layer * STEPS + (STEPS + 1)))
                sp_.wait_ge(st_prompt, value(sp_, layer * 48 + 48))
                with sp_.Fori(0, KD // 2) as i:
                    blocks(layer, B_MERGE, i, (6, 6) * 6, lambda j: tiles("merge", layer * 48 + i * 12 + j))
                with sp_.Fori(0, 2) as i:
                    blocks(layer, B_OUT, i, (KD,) * 4, lambda j: tiles("wout", layer * KD + i * 4 + j))
                ffn(layer, 1, B_FFN2)
            sp_.wait_ge(x_done, DEPTH * 3 * KD + 1)
            sp_.dma_start(io["y"].rearrange("p (k t) -> p k t", k=KD), x[:]).then_inc(saved, 16)
            sp_.wait_ge(saved, 16)
            sp_.wait_ge(cs_saved, DEPTH * 32)
            sp_.wait_ge(st_prompt, DEPTH * 48)
            sp_.wait_ge(st_out, DEPTH * 48)

        @block.gpsimd
        def _(pool):
            def blocks(layer, first, i, nks):
                for j, nk in enumerate(nks):
                    src = raw[:, j % RAW, 0:nk, :].rearrange("p k m -> p (k m)")
                    hi = wh[:, j % SPLIT, 0:nk, :].rearrange("p k m -> p (k m)")
                    lo = wl[:, j % SPLIT, 0:nk, :].rearrange("p k m -> p (k m)")
                    turns = len(nks) // RAW
                    pool.wait_ge(raw_full[j % RAW], value(pool, layer * (BLOCKS // RAW * 16) + i * (turns * 16) + 16 * ((first + j) // RAW + 1)))
                    pool.wait_ge(blk_done, further(pool, layer * BLOCKS + i * len(nks) + (first + j + 1)))
                    pool.tensor_scalar(hi, src, 1.0, 1.0, MULT, MULT).then_inc(hi_done, 1)
                    pool.wait_ge(hi_done, value(pool, layer * BLOCKS + i * len(nks) + (first + j + 1)))
                    pool.tensor_tensor(lo, src, hi.bitcast(F32), SUB).then_inc(lo_done, 1)

            def ffn(layer, first):
                with pool.Fori(0, KF // 2) as i:
                    blocks(layer, first, i, (KD,) * 4)
                with pool.Fori(0, 2) as i:
                    blocks(layer, first + UPS, i, DOWN_K * 4)

            with pool.Fori(0, DEPTH) as layer:
                ffn(layer, B_FFN1)
                blocks(layer, B_PROJ, 0, (2,) * 4)
                with pool.Fori(0, 10) as i:
                    blocks(layer, B_PROJ + 4, i, (KD,) * 4)
                with pool.Fori(0, KD // 2) as i:
                    blocks(layer, B_MERGE, i, (6, 6) * 6)
                with pool.Fori(0, 2) as i:
                    blocks(layer, B_OUT, i, (KD,) * 4)
                ffn(layer, B_FFN2)

        @block.tensor
        def _(pe):
            pe.wait_ge(loaded, 32)

            def products(j, slot, ks, moving, start, stop, ready=None):
                for n, k in enumerate(ks):
                    if ready:
                        ready(n)
                    mh_, ml_ = moving(n)
                    for h in range(2):
                        out = ps[:, 2 * slot + h, 0:HALF]
                        c = slice(h * HALF, (h + 1) * HALF)
                        a, b = start and n == 0, stop and n == len(ks) - 1
                        pe.matmul(out, wh[:, j % SPLIT, k, :], mh_[:, c], start=a, stop=False)
                        pe.matmul(out, wh[:, j % SPLIT, k, :], ml_[:, c], start=False, stop=False)
                        last = pe.matmul(out, wl[:, j % SPLIT, k, :], mh_[:, c], start=False, stop=b)
                return last

            def product(layer, first, i, j, per, slot, nk, moving, start=True, stop=True, ready=None):
                pe.wait_ge(lo_done, value(pe, layer * BLOCKS + i * per + (first + j + 1 + RAW)))
                products(j, slot, range(nk), moving, start, stop, ready).then_inc(blk_done, 1)

            def h_split(layer, number):
                def ready(k):
                    pe.wait_ge(hl_ready, value(pe, layer * (4 * KD) + (number * KD + k + 1)))
                return ready

            def h_tiles(k):
                return hh[:, k, :], hl[:, k, :]

            def add_squares(src, start=False, stop=False):
                for h in range(2):
                    last = pe.matmul(ps[:, 6 + h, 0:HALF], ones, src[:, h * HALF:(h + 1) * HALF],
                                     start=start, stop=stop, skip_group_check=True)
                return last

            def eps_first():
                for h in range(2):
                    pe.matmul(ps[:, 6 + h, 0:HALF], ones, cst[:, EPSROW:EPSROW + 1].to_broadcast([P, HALF]),
                              start=True, stop=False, skip_group_check=True)

            def pre_stats(layer, stage):
                for k in range(KD):
                    pe.wait_ge(sq_ready, value(pe, layer * (6 * KD) + (stage * KD + k + 1)))
                    if k == 0:
                        eps_first()
                    last = add_squares(sq[:, k, :], stop=(k == KD - 1))
                last.then_inc(sum_ready, 1)

            def reduce_out(layer, stage, first, nks, moving, ready):
                per = len(nks)
                k0 = np.cumsum((0,) + tuple(nks))

                def turn(i):
                    for m in range(4):
                        pe.wait_ge(out_done, value(pe, layer * (3 * KD) + i * 4 + (stage // 2 * KD + m + 1)))
                        for b, nk in enumerate(nks):
                            product(layer, first, i, per * m + b, 4 * per, m % 2, nk,
                                    lambda k, b=b: moving(k0[b] + k), b == 0, b == per - 1,
                                    ready=(lambda k, b=b: ready(k0[b] + k)) if i is FIRST and m == 0 else None)
                        if i is FIRST and m == 0:
                            eps_first()
                        if m:
                            pe.wait_ge(sq_ready, value(pe, layer * (6 * KD) + i * 4 + (stage * KD + m)))
                            add_squares(sq[:, m - 1, :])
                    pe.wait_ge(sq_ready, value(pe, layer * (6 * KD) + i * 4 + (stage * KD + 4)))
                    add_squares(sq[:, 3, :], stop=True).then_inc(sum_ready, 1)

                turn(FIRST)
                with pe.Fori(1, 2) as i:
                    turn(i)

            def ffn(layer, which, first):
                pre_stats(layer, 4 * which)

                def up(i):
                    for j in range(4):
                        pe.wait_ge(prod_done if j % 2 else sil_done, value(pe, layer * (2 * KF) + i * 2 + (which * KF + j // 2 + 1)))
                        product(layer, first, i, j, 4, j, KD, h_tiles,
                                ready=h_split(layer, 3 * which) if i is FIRST and j == 0 else None)

                up(FIRST)
                with pe.Fori(1, KF // 2) as i:
                    up(i)

                def ready(k):
                    if k in (0, KF - 2):
                        pe.wait_ge(al_done, value(pe, layer * (2 * KF) + (which * KF + KF - (0 if k else 2))))
                    if k == 0:
                        pe.wait_ge(sil_done, further(pe, layer * (2 * KF) + (which * KF + KF - 1 + 2)))

                reduce_out(layer, 4 * which + 1, first + UPS, DOWN_K, lambda k: (ah[:, k, :], al[:, k, :]), ready)

            def common(step):
                n = step.n
                tri_n, rev_n = (tri, rev) if step.prompt else (
                    cst[:, TRI_S:TRI_S + 32], cst[:, REV_S:REV_S + 32])
                pe.wait_ge(both["cc"], value(pe, step.once + 1))
                pe.transpose(ps[0:n, 2, 0:P], cc[:, 0:n], ident).then_inc(both["tmp"], 1)
                yield
                pe.wait_ge(both["tm"], value(pe, step.once + 1))
                pe.matmul(ps[0:n, 3, 0:P], tri_n[0:n, 0:n], tm[0:n, :], start=True, stop=True)
                pe.matmul(ps[0:n, 3, P:2 * P], rev_n[0:n, 0:n], tm[0:n, :], start=True, stop=True)
                pe.matmul(ps[:, 3, 2 * P:2 * P + n], tm[0:n, :], tri_n[0:n, 0:n], start=True, stop=True).then_inc(both["cum"], 1)
                pe.wait_ge(g_["sq"], value(pe, step.once + 1))
                w = 8 * n
                for b in range(-(-w // 512)):
                    c = min(512, w)
                    last = pe.matmul(ps[:, b, 0:c], ones, sq8[:, b * 512:b * 512 + c], start=True, stop=True)
                last.then_inc(g_["ss"], 1)
                yield
                yield

            def spread(bank, off, rowi, n):
                return pe.matmul(ps[:, bank, off:off + n], cst[:, IDENT + rowi:IDENT + rowi + 1].to_broadcast([P, P]),
                                 br[:, 0:n], start=True, stop=True)

            def gdn(step):
                n, o = step.n, step.once
                pe.wait_ge(g_["brb"], value(pe, o + 1))
                pe.wait_ge(both["rg"], further(pe, o + 1))
                for h in range(HEADS):
                    spread(2, h * n, ROW_A + h, n)
                for h in range(HEADS):
                    last = spread(3, h * n, ROW_B + h, n)
                last.then_inc(g_["bc"], 1)
                yield
                pe.wait_ge(g_["qk"], value(pe, o + 1))
                for h in range(HEADS):
                    k_, q_ = kn[:, h * n:(h + 1) * n], qn[:, h * n:(h + 1) * n]
                    pe.matmul(ps[0:n, 0, h * n:(h + 1) * n], k_, k_, start=True, stop=True)
                    last = pe.matmul(ps[0:n, 1, h * n:(h + 1) * n], k_, q_, start=True, stop=True)
                last.then_inc(g_["kk"], 1)
                pe.wait_ge(g_["d"], value(pe, o + 1))
                for h in range(HEADS):
                    last = pe.transpose(ps[0:n, 2, h * P:(h + 1) * P], kn[:, h * n:(h + 1) * n], ident)
                last.then_inc(g_["kt"], 1)
                yield
                yield

                def s_of(h, b):
                    return gs[:, h * P:(h + 1) * P] if step.prompt else states[:, b, h * P:(h + 1) * P]

                def through_state(bank, h, src):
                    c = slice(h * n, (h + 1) * n)
                    return pe.matmul(ps[:, bank, c], s_of(h, 0), src[:, c], start=(h == 0), stop=(bank == 3),
                                     skip_group_check=True)

                def through_states(h):
                    for b in range(step.states):
                        c = slice(h * n + b * DEC_SEQ, h * n + (b + 1) * DEC_SEQ)
                        last = pe.matmul(ps[:, 3, 0:2 * HEADS * n].rearrange("p (e c) -> p e c", e=2)[:, :, c], s_of(h, b),
                                         kqg[:, :, c], start=(h == 0 and b == 0), stop=False, skip_group_check=True)
                    return last

                def value_of_keys():
                    if step.prompt:
                        pe.wait_ge(g_["s"], value(pe, o + 1))
                        pe.wait_ge(zeroed, further(pe, step.layer * 3 + 1))
                    else:
                        pe.wait_ge(st_in[0], further(pe, step.layer * 16 + 16))
                    pe.wait_ge(g_["kg"], further(pe, o + 1))
                    for h in range(HEADS):
                        last = through_state(3, h, kg) if step.prompt else through_states(h)
                        if h < HEADS - 1 and not step.prompt:
                            yield
                    last.then_inc(g_["sk"], 1)

                def turned():
                    pe.wait_ge(g_["rt"], value(pe, o + 1))
                    for h in range(HEADS):
                        last = pe.transpose(ps[0:n, 3 if step.prompt else 2, h * P:(h + 1) * P], rt[:, h * n:(h + 1) * n], ident)
                    last.then_inc(g_["rtt"], 1)

                pe.wait_ge(g_["x"], value(pe, step.level + 1))
                for h in range(HEADS):
                    c = slice(h * n, (h + 1) * n)
                    last = pe.transpose(ps[0:n, 0, c], xt[0:n, c], ident[0:n, 0:n])
                last.then_inc(g_["xtt"], 1)
                if step.prompt:
                    yield from value_of_keys()
                yield
                for l in range(step.levels - 1):
                    final = l == step.levels - 2
                    pe.wait_ge(g_["al"], value(pe, step.level + l + 2))
                    if l == 0:
                        pe.wait_ge(g_["xi"], further(pe, o + 1))
                        pe.wait_ge(g_["kd"], further(pe, o + 1))
                    else:
                        pe.wait_ge(g_["xx"], further(pe, step.inner + l))
                    for h in range(HEADS):
                        c = slice(h * n, (h + 1) * n)
                        last = pe.matmul(ps[0:n, 0, c], al_[0:n, c], xx[0:n, c], start=True, stop=True)
                    last.then_inc(g_["p"], 1)
                    if l == 0 and step.prompt:
                        turned()
                    yield
                    pe.wait_ge(g_["pc"], value(pe, step.solve + l + 1))
                    pe.wait_ge(g_["x"], further(pe, step.level + l + 1))
                    if not final:
                        for h in range(HEADS):
                            c = slice(h * n, (h + 1) * n)
                            last = pe.matmul(ps[0:n, 1, c], xt[0:n, c], pp[0:n, c], start=True, stop=True)
                        last.then_inc(g_["qx"], 1)
                    for h in range(HEADS):
                        c = slice(h * n, (h + 1) * n)
                        last = pe.matmul(ps[0:n, 2, c], pp[0:n, c], xt[0:n, c], start=True, stop=True)
                    last.then_inc(g_["q"], 1)
                    yield
                if not step.prompt:
                    yield from value_of_keys()
                    yield
                    turned()
                    yield
                pe.wait_ge(g_["r"], value(pe, o + 1))
                pe.wait_ge(g_["tb"], further(pe, o + 1))
                for h in range(HEADS):
                    last = pe.matmul(ps[0:n, 1, h * P:(h + 1) * P], xt[0:n, h * n:(h + 1) * n],
                                     rr[0:n, h * P:(h + 1) * P], start=True, stop=True)
                last.then_inc(g_["up"], 1)
                if step.prompt:
                    for h in range(HEADS):
                        through_state(2, h, qg)
                else:
                    yield
                    yield
                out = ps[:, 2, 0:HEADS * n] if step.prompt else ps[:, 3, HEADS * n:2 * HEADS * n]
                pe.wait_ge(g_["u"], value(pe, o + 1))
                for h in range(HEADS):
                    last = pe.matmul(out[:, h * n:(h + 1) * n], uu[0:n, h * P:(h + 1) * P],
                                     att[0:n, h * n:(h + 1) * n], start=False, stop=True, skip_group_check=True)
                last.then_inc(g_["o"], 1)
                if not step.prompt:
                    yield
                if step.prompt:
                    for h in range(HEADS):
                        last = pe.matmul(ps[:, 3, h * P:(h + 1) * P], kd[0:n, h * P:(h + 1) * P],
                                         uu[0:n, h * P:(h + 1) * P], start=True, stop=True)
                    last.then_inc(g_["su"], 1)
                else:
                    for h in range(HEADS):
                        pe.wait_ge(g_["ue"], value(pe, step.layer * HEADS + h + 1))
                        for b in range(2):
                            last = pe.matmul(ps[:, b, :], kd[0:n, h * P:(h + 1) * P], uexp[0:n, b * 512:(b + 1) * 512],
                                             start=True, stop=True)
                        last.then_inc(g_["su"], 1)
                        yield
                if step.prompt:
                    yield

            def gla(step):
                n, o = step.n, step.once
                L = gla_prompt if step.prompt else gla_sample
                tri_n, rev_n = (tri, rev) if step.prompt else (
                    cst[:, TRI_S:TRI_S + 32], cst[:, REV_S:REV_S + 32])
                pe.wait_ge(l_["rc"], value(pe, o + 1))
                pe.matmul(ps[0:n, 4, 0:256], L["rc"][96:112, 0:n], prm[96:112, GUP:GUP + 256],
                          start=True, stop=True).then_inc(l_["z"], 1)
                yield
                pe.wait_ge(l_["gk"], value(pe, o + 1))
                for g in range(2):
                    pe.matmul(ps[:, 5, g * n:(g + 1) * n], L["gk"][0:n, g * P:(g + 1) * P], tri_n[0:n, 0:n], start=True, stop=True)
                for g in range(2):
                    last = pe.matmul(ps[:, 5, (2 + g) * n:(3 + g) * n], L["gk"][0:n, g * P:(g + 1) * P], rev_n[0:n, 0:n],
                                     start=True, stop=True)
                last.then_inc(l_["b"], 1)
                pe.wait_ge(l_["vc"], value(pe, o + 1))
                for h in range(HEADS):
                    last = pe.transpose(ps[0:n, 4, h * P:(h + 1) * P], L["vc"][:, h * n:(h + 1) * n], ident)
                last.then_inc(l_["vtp"], 1)
                yield
                pe.wait_ge(l_["qe"], value(pe, o + 1))
                for g in range(2):
                    last = pe.transpose(ps[0:n, 5, g * P:(g + 1) * P], L["kd"][:, g * n:(g + 1) * n], ident)
                last.then_inc(l_["kdp"], 1)
                yield
                yield
                yield
                for l in range(step.levels + 1):
                    if l == 0:
                        pe.wait_ge(l_["ml"], value(pe, o + 1))
                        pe.wait_ge(l_["vt"], further(pe, o + 1))
                        pe.wait_ge(l_["kt"], further(pe, o + 1))
                    else:
                        pe.wait_ge(l_["cp"], value(pe, step.score + l))
                    for h in range(HEADS):
                        r = slice(64 * (h % 2), 64 * (h % 2) + 64)
                        c = slice(h // 2 * n, (h // 2 + 1) * n)
                        a, b = (L["dl"][r, l, c], L["dl"][r, l, c]) if l < step.levels else (L["ks"][r, c], L["qs"][r, c])
                        last = pe.matmul(ps[0:n, 4 + h % 2, c], a, b, start=True, stop=True)
                    last.then_inc(l_["at"], 1)
                    yield
                if step.prompt:
                    pe.wait_ge(l_["s"], value(pe, o + 1))
                    pe.wait_ge(zeroed, further(pe, step.layer * 3 + 2))
                else:
                    pe.wait_ge(st_in[1], further(pe, step.layer * 16 + 16))
                pe.wait_ge(l_["cp"], further(pe, step.score + step.levels + 1))
                w_ = n // step.states
                for h in range(HEADS):
                    r = slice(64 * (h % 2), 64 * (h % 2) + 64)
                    g = h // 2
                    for b in range(step.states):
                        s_b = ls[r, g * P:(g + 1) * P] if step.prompt else gla_states[r, b // 2, b % 2, g * P:(g + 1) * P]
                        pe.matmul(ps[:, 4 + h % 2, g * n + b * w_:g * n + (b + 1) * w_], s_b,
                                  L["qe"][r, g * n + b * w_:g * n + (b + 1) * w_], start=(b == 0), stop=False,
                                  skip_group_check=True)
                    a = (h % 2 * 2 + g) * n
                    last = pe.matmul(ps[:, 4 + h % 2, g * n:(g + 1) * n], L["vt"][0:n, h * P:(h + 1) * P],
                                     L["att"][0:n, a:a + n], start=False, stop=True, skip_group_check=True)
                    if h < HEADS - 1 and not step.prompt:
                        yield
                last.then_inc(l_["o"], 1)
                yield
                pe.wait_ge(l_["oc"], value(pe, o + 2))
                if step.prompt:
                    for h in range(HEADS):
                        r = slice(64 * (h % 2), 64 * (h % 2) + 64)
                        last = pe.matmul(ps[r, 4, h // 2 * P:(h // 2 + 1) * P], L["kt"][0:n, h * 64:(h + 1) * 64],
                                         L["vt"][0:n, h * P:(h + 1) * P], start=True, stop=True)
                    last.then_inc(l_["su"], 1)
                    yield
                else:
                    for h in range(HEADS):
                        r = slice(64 * (h % 2), 64 * (h % 2) + 64)
                        pe.wait_ge(l_["ve"], value(pe, step.layer * HEADS + h + 1))
                        for b in range(2):
                            last = pe.matmul(ps[r, 4 + b, :], L["kt"][0:n, h * 64:(h + 1) * 64],
                                             vexp[0:n, 4 * b:4 * b + 4, :].rearrange("p a b -> p (a b)"),
                                             start=True, stop=True)
                        last.then_inc(l_["su"], 1)
                        yield

            def ssd(step):
                n, o = step.n, step.once
                S = ssd_prompt if step.prompt else ssd_sample
                pe.wait_ge(both["br"], value(pe, o + 1))
                pe.wait_ge(g_["brb"], further(pe, o + 1))
                for h in range(SSD_HEADS):
                    last = spread(6 + h // 4, h % 4 * n, ROW_DT + h, n)
                last.then_inc(s_["bc"], 1)
                yield
                pe.wait_ge(s_["st"], value(pe, o + 1))
                pe.wait_ge(s_["d"], further(pe, o + 1))
                for g in range(2):
                    pe.matmul(ps[0:n, 7, g * n:(g + 1) * n], S["xbc"][:, (4 + g) * n:(5 + g) * n],
                              S["xbc"][:, (6 + g) * n:(7 + g) * n], start=True, stop=True)
                for t in range(4):
                    pe.transpose(ps[0:n, 6, t * P:(t + 1) * P], S["xbc"][:, t * n:(t + 1) * n], ident)
                for g in range(2):
                    last = pe.transpose(ps[0:n, 7, 256 + g * P:256 + (g + 1) * P], S["xbc"][:, (4 + g) * n:(5 + g) * n], ident)
                last.then_inc(s_["tr"], 1)
                yield
                yield
                if step.prompt:
                    pe.wait_ge(s_["s"], value(pe, o + 1))
                    pe.wait_ge(zeroed, further(pe, step.layer * 3 + 3))
                else:
                    pe.wait_ge(st_in[2], further(pe, step.layer * 16 + 16))
                pe.wait_ge(s_["att"], further(pe, o + 1))
                pe.wait_ge(s_["xe"], further(pe, o + 1))
                pe.wait_ge(s_["ce"], further(pe, o + 1))
                w_ = n // step.states
                for h in range(SSD_HEADS):
                    r = slice(64 * (h % 2), 64 * (h % 2) + 64)
                    t = h // 2
                    for b in range(step.states):
                        s_b = ss_[:, h * 64:(h + 1) * 64] if step.prompt else ssd_states[:, b, h * 64:(h + 1) * 64]
                        pe.matmul(ps[r, 6, t * n + b * w_:t * n + (b + 1) * w_], s_b,
                                  S["ce"][:, h * n + b * w_:h * n + (b + 1) * w_], start=(b == 0), stop=False,
                                  skip_group_check=True)
                    last = pe.matmul(ps[r, 6, t * n:(t + 1) * n], S["xd"][0:n, h * 64:(h + 1) * 64],
                                     S["dd"][0:n, h * n:(h + 1) * n], start=False, stop=True, skip_group_check=True)
                    if h in (1, 3, 5) and not step.prompt:
                        yield
                last.then_inc(s_["y"], 1)
                yield
                pe.wait_ge(s_["bt"], value(pe, o + 1))
                if step.prompt:
                    for g in range(2):
                        last = pe.matmul(ps[:, 7, g * 256:(g + 1) * 256], S["bt"][0:n, g * P:(g + 1) * P],
                                         S["xe"][0:n, g * 256:(g + 1) * 256], start=True, stop=True)
                    last.then_inc(s_["su"], 1)
                else:
                    for g in range(2):
                        pe.wait_ge(s_["xe2"], value(pe, step.layer * 2 + g + 1))
                        for half in range(2):
                            if 2 * g + half:
                                pe.wait_ge(s_["sa"], value(pe, step.layer * 3 + (2 * g + half)))
                            for b in range(2):
                                last = pe.matmul(ps[:, 6 + b, :], S["bt"][0:n, g * P:(g + 1) * P],
                                                 xexp[0:n, (2 * half + b) * 512:(2 * half + b + 1) * 512], start=True, stop=True)
                            last.then_inc(s_["su"], 1)
                        if g == 0:
                            yield
                yield
                yield

            def branch_stats(layer, branch):
                pe.wait_ge(n_["sq"], value(pe, layer * 3 + (NORM_ORDER.index(branch) + 1)))
                if branch != NORM_ORDER[0]:
                    pe.wait_ge(n_["ln"], value(pe, layer * 3 + NORM_ORDER.index(branch)))
                if branch < 2:
                    for t in range(4):
                        for h in range(2):
                            last = pe.matmul(ps[:, 2 * t + h, 0:HALF], ones, nsq[:, t, h * HALF:(h + 1) * HALF],
                                             start=True, stop=True)
                else:
                    for g in range(2):
                        for t in range(2):
                            for h in range(2):
                                last = pe.matmul(ps[:, 2 * g + h, 0:HALF], ones,
                                                 nsq[:, 2 * g + t, h * HALF:(h + 1) * HALF],
                                                 start=(t == 0), stop=(t == 1))
                last.then_inc(n_["ss"], 1)

            with pe.Fori(0, DEPTH) as layer:
                ffn(layer, 0, B_FFN1)
                pre_stats(layer, 2)
                for j in range(4):
                    product(layer, B_PROJ, 0, j, 4, 0, 2, lambda k: h_tiles(2 * j + k), j == 0, j == 3,
                            ready=lambda k: h_split(layer, 1)(2 * j + k))
                pe.wait_ge(small_done, value(pe, layer + 1))
                with pe.Fori(0, 10) as i:
                    for j in range(4):
                        pe.wait_ge(evict_done, value(pe, layer * 40 + i * 4 + (j + 1)))
                        product(layer, B_PROJ + 4, i, j, 4, j, KD, h_tiles)
                pe.wait_ge(evict_done, value(pe, layer * 40 + 44))
                with pe.Fori(0, CHUNKS) as c:
                    step = prompt_step(layer, c)
                    together(ORDER, common(step), gdn(step), gla(step), ssd(step))
                step = sample_step(layer)
                together(SAMPLE_ORDER, common(step), gdn(step), gla(step), ssd(step))
                for branch in NORM_ORDER:
                    branch_stats(layer, branch)

                pe.wait_ge(n_["ln"], value(pe, layer * 3 + 3))

                def merge(i):
                    for u in range(6):
                        pe.wait_ge(sg_done, value(pe, layer * 24 + i * 6 + (u + 1)))
                        product(layer, B_MERGE, i, 2 * u, 12, 2 * u % 4, 6, h_tiles, True, False,
                                ready=h_split(layer, 2) if i is FIRST and u == 0 else None)
                        pe.wait_ge(mac_done, value(pe, layer * 24 + i * 6 + (u + 1)))
                        pe.wait_ge(lo_done, value(pe, layer * BLOCKS + i * 12 + (B_MERGE + 2 * u + 2 + RAW)))
                        if i is FIRST and u == 0:
                            h_split(layer, 2)(KD - 1)
                        if i is FIRST and u < 2:
                            pe.wait_ge(n_["lo"], value(pe, layer * 3 + (u + 2)))
                        products(2 * u + 1, 2 * u % 4, (0, 1), lambda n: h_tiles(6 + n), False, True)
                        products(2 * u + 1, (2 * u + 1) % 4, range(2, 6), lambda k, u=u: (oh[u % 3][:, k, :], ol[u % 3][:, k, :]),
                                 True, True).then_inc(blk_done, 1)
                merge(FIRST)
                with pe.Fori(1, KD // 2) as i:
                    merge(i)

                def ready(k):
                    if k in (0, KD - 1):
                        pe.wait_ge(ml_done, value(pe, layer * KD + (KD if k else KD - 1)))
                    if k == 0:
                        pe.wait_ge(sg_done, further(pe, layer * 24 + 25))

                reduce_out(layer, 3, B_OUT, (KD,), lambda k: (mh[:, k, :], ml[:, k, :]), ready)
                ffn(layer, 1, B_FFN2)

        @block.scalar
        def _(act):
            act.wait_ge(loaded, 32)

            def rsqrt_stats(layer, stage, out):
                act.preload_act_table_set(LN_EXP)
                act.wait_ge(sum_ready, value(act, layer * SUMS[-1] + SUMS[stage]))
                act.activation(halves(out[:, :]), ps[:, 6:8, 0:HALF], ACT.Ln, scale=1.0 / D_MODEL).then_inc(ln_ready, 1)
                act.wait_ge(ln_ready, value(act, layer * 6 + (stage + 1)))
                act.activation(out[:, :], out[:, :], ACT.Exp, scale=-0.5).then_inc(rstd_ready, 1)

            def split_h(layer, number):
                for k in range(KD):
                    act.wait_ge(hf_ready, value(act, layer * (4 * KD) + (number * KD + k + 1)))
                    act.activation(hh[:, k, :], hf[:, k, :], ACT.Copy).then_inc(hh_ready, 1)

            def pre_norm(layer, stage, number):
                for k in range(KD):
                    act.wait_ge(x_done, value(act, layer * (3 * KD) + ((stage // 2 - 1) * KD + k + 2 if stage else 1)))
                    act.activation(sq[:, k, :], x[:, k, :], ACT.Square).then_inc(sq_ready, 1)
                rsqrt_stats(layer, stage, rstd)
                split_h(layer, number)

            def reduce_out(layer, stage, first, per):
                with act.Fori(0, 2) as i:
                    for m in range(4):
                        act.wait_ge(blk_done, value(act, layer * BLOCKS + i * (4 * per) + (first + per * m + per + SPLIT)))
                        act.activation(sq[:, m, :].rearrange("p (a t) -> p a t", a=2), pair(m % 2), ACT.Square).then_inc(sq_ready, 1)
                        act.activation(f[:, bass.ds(i * 4 + m, 1), :].rearrange("p k (a t) -> p (k a) t", a=2),
                                       pair(m % 2), ACT.Copy).then_inc(out_done, 1)
                rsqrt_stats(layer, stage, rstd_post)

            def ffn(layer, which, first):
                pre_norm(layer, 4 * which, 3 * which)
                with act.Fori(0, KF // 2) as i:
                    for j in range(2):
                        n = layer * (2 * KF) + i * 2 + (which * KF + j)
                        act.wait_ge(blk_done, value(act, layer * BLOCKS + i * 4 + (first + 2 * j + 1 + SPLIT)))
                        act.wait_ge(prod_done, further(act, n + 1))
                        act.activation(halves(sil[:, j, :]), pair(2 * j), ACT.Silu).then_inc(sil_done, 1)
                        act.wait_ge(prod_done, value(act, n + 3))
                        act.activation(ah[:, bass.ds(i * 2 + j, 1), :].rearrange("p k t -> p (k t)"), prod[:, j, :],
                                       ACT.Copy).then_inc(ah_done, 1)
                reduce_out(layer, 4 * which + 1, first + UPS, 3)

            def view(a, k, n):
                return a[:, 0:k * n].rearrange("p (k t) -> p k t", k=k)

            def common(step):
                n, o = step.n, step.once
                act.wait_ge(g_["oc"], value(act, o + 1))
                act.activation(view(sq8, 8, n), proj[:, GQ:GQ + 8, step.cols], ACT.Square).then_inc(g_["sq"], 1)
                act.wait_ge(both["tmp"], value(act, o + 1))
                act.activation(tm[0:n, :], ps[0:n, 2, 0:P], ACT.Copy).then_inc(both["tm"], 1)
                yield
                act.wait_ge(both["cum"], value(act, o + 1))
                act.activation(br[:, 0:n], ps[:, 3, 2 * P:2 * P + n], ACT.Copy).then_inc(both["br"], 1)
                act.activation(gc[0:n, :], ps[0:n, 3, 0:P], ACT.Copy).then_inc(both["gc"], 1)
                act.activation(rg[0:n, ROW_A:ROW_A + 4], ps[0:n, 3, P + ROW_A:P + ROW_A + 4], ACT.Exp)
                act.activation(rg[0:n, ROW_DT:ROW_DT + 8], ps[0:n, 3, P + ROW_DT:P + ROW_DT + 8], ACT.Exp).then_inc(both["rg"], 1)
                yield
                act.wait_ge(g_["ss"], value(act, o + 1))
                w = min(512, 8 * n)
                act.activation(rs8[:, 0:8 * n].rearrange("p (b c) -> p b c", c=w), ps[:, 0:8 * n // w, 0:w], ACT.Ln,
                               bias=epsc).then_inc(g_["ln"], 1)
                act.wait_ge(g_["ln"], value(act, o + 1))
                act.activation(rs8[:, 0:8 * n], rs8[:, 0:8 * n], ACT.Exp, scale=-0.5).then_inc(g_["rs"], 1)
                yield

            def gdn(step):
                n, o = step.n, step.once
                act.wait_ge(g_["bc"], value(act, o + 1))
                act.activation(eg[:, 0:4 * n], ps[:, 2, 0:4 * n], ACT.Exp).then_inc(g_["eg"], 1)
                yield
                act.wait_ge(g_["d"], value(act, o + 1))
                act.activation(dd[0:n, 0:4 * n], dd[0:n, 0:4 * n], ACT.Exp).then_inc(g_["dx"], 1)
                yield
                yield
                def turned():
                    act.wait_ge(g_["rtt"], value(act, o + 1))
                    act.activation(rr[0:n, :], ps[0:n, 3 if step.prompt else 2, :], ACT.Copy).then_inc(g_["r"], 1)

                act.wait_ge(g_["xtt"], value(act, o + 1))
                act.activation(xx[0:n, 0:4 * n], ps[0:n, 0, 0:4 * n], ACT.Copy).then_inc(g_["xi"], 1)
                yield
                for l in range(step.levels - 1):
                    act.wait_ge(g_["p"], value(act, step.solve + l + 1))
                    act.activation(pp[0:n, 0:4 * n], ps[0:n, 0, 0:4 * n], ACT.Copy).then_inc(g_["pc"], 1)
                    if l == 0 and step.prompt:
                        turned()
                    yield
                    yield
                if not step.prompt:
                    for h in range(HEADS):
                        yield
                    turned()
                    yield
                act.wait_ge(g_["up"], value(act, o + 1))
                act.activation(uu[0:n, :], ps[0:n, 1, :], ACT.Copy).then_inc(g_["u"], 1)
                if not step.prompt:
                    yield
                    yield
                act.wait_ge(g_["o"], value(act, o + 1))
                out = ps[:, 2, :] if step.prompt else ps[:, 3, HEADS * n:2 * HEADS * n]
                act.activation(proj[:, GV:GV + 4, step.cols], view(out, 4, n), ACT.Copy).then_inc(g_["oc"], 1)
                yield
                if not step.prompt:
                    for h in range(HEADS):
                        yield

            def gla(step):
                n, o = step.n, step.once
                L = gla_prompt if step.prompt else gla_sample
                for a, (want, done, func, scale, bias) in enumerate((
                        ("zt", "a1", ACT.Abs, 1.0, 0.0), ("a1", "a2", ACT.Exp, -1.0, 0.0), ("a2", "a3", ACT.Ln, 1.0, 1.0))):
                    act.wait_ge(l_[want], value(act, o + 1))
                    act.activation(L["a"][0:n, :], L["z" if a == 0 else "a"][0:n, :], func, scale=scale, bias=bias).then_inc(l_[done], 1)
                yield
                act.wait_ge(l_["b"], value(act, o + 1))
                act.activation(L["bt"][:, 0:2 * n], ps[:, 5, 0:2 * n], ACT.Copy)
                act.activation(L["eb"][:, 0:2 * n], ps[:, 5, 0:2 * n], ACT.Exp)
                act.activation(L["er"][:, 0:2 * n], ps[:, 5, 2 * n:4 * n], ACT.Exp).then_inc(l_["bt"], 1)
                yield
                act.wait_ge(l_["vtp"], value(act, o + 1))
                act.activation(L["vt"][0:n, :], ps[0:n, 4, :], ACT.Copy).then_inc(l_["vt"], 1)
                yield
                act.wait_ge(l_["kdp"], value(act, o + 1))
                act.activation(L["kt"][0:n, :], ps[0:n, 5, 0:256], ACT.Copy).then_inc(l_["kt"], 1)
                act.wait_ge(l_["dl"], value(act, o + 1))
                d = L["dl"][:, 0:step.levels, 0:2 * n]
                act.activation(d, d, ACT.Abs).then_inc(l_["d1"], 1)
                yield
                act.wait_ge(l_["d1"], value(act, o + 1))
                act.activation(d, d, ACT.Exp, scale=-1.0).then_inc(l_["d2"], 1)
                yield
                for l in range(step.levels + 1):
                    yield
                for h in range(0 if step.prompt else HEADS - 1):
                    yield
                act.wait_ge(l_["o"], value(act, o + 1))
                for e in range(2):
                    last = act.activation(proj[:, LV + e:LV + 4:2, step.cols], view(ps[:, 4 + e, :], 2, n), ACT.Copy)
                last.then_inc(l_["oc"], 1)
                yield
                for h in range(1 if step.prompt else HEADS):
                    yield

            def ssd(step):
                n, o = step.n, step.once
                S = ssd_prompt if step.prompt else ssd_sample
                act.wait_ge(s_["s"], value(act, o + 1))
                act.wait_ge(s_["yc"], further(act, o + 1))
                act.activation(view(S["xbc"], 8, n), proj[:, SX:SX + 8, step.cols], ACT.Copy).then_inc(s_["st"], 1)
                act.wait_ge(s_["bc"], value(act, o + 1))
                act.activation(S["ea"][:, 0:8 * n].rearrange("p (b c) -> p b c", b=2), ps[:, 6:8, 0:4 * n], ACT.Exp).then_inc(s_["ea"], 1)
                yield
                act.wait_ge(s_["d"], value(act, o + 1))
                act.activation(S["dd"][0:n, 0:8 * n], S["dd"][0:n, 0:8 * n], ACT.Exp).then_inc(s_["dx"], 1)
                act.wait_ge(s_["tr"], value(act, o + 1))
                act.activation(S["bt"][0:n, 0:256], ps[0:n, 7, 256:512], ACT.Copy).then_inc(s_["bt"], 1)
                yield
                for h in range(4 if step.prompt else 8):
                    yield

            def branch_norms(layer):
                def squares(number, b):
                    if b < 2:
                        act.wait_ge((g_, l_)[b]["oc"], value(act, layer * STEPS + (STEPS + 1)))
                    else:
                        act.wait_ge(n_["yz"], value(act, layer + 1))
                    src = proj[:, (GV, LV, SX)[b]:(GV, LV, SX)[b] + 4, :]
                    act.activation(nsq[:, :, :], src, ACT.Square).then_inc(n_["sq"], 1)

                def log(number, b):
                    act.wait_ge(n_["ss"], value(act, layer * 3 + (number + 1)))
                    if number == 2:
                        act.wait_ge(st_out, further(act, layer * 48 + 48))
                    k = 4 if b < 2 else 2
                    o = nrs[number][:, 0:k, :].rearrange("p k (a t) -> p (k a) t", a=2)
                    act.activation(o, ps[:, 0:2 * k, 0:HALF], ACT.Ln, scale=1.0 / (128 if b < 2 else 256), bias=epsc).then_inc(n_["ln"], 1)

                def exp(number, b):
                    act.wait_ge(n_["ln"], value(act, layer * 3 + (number + 1)))
                    o = nrs[number][:, 0:4 if b < 2 else 2, :]
                    act.activation(o, o, ACT.Exp, scale=-0.5).then_inc(n_["rs"], 1)

                def high(number, b):
                    act.wait_ge(n_["tz"], value(act, layer * 3 + (number + 1)))
                    act.activation(oh[b][:, :, :], nt[number][:, :, :], ACT.Copy).then_inc(n_["hi"], 1)

                act.wait_ge(g_["s"], value(act, layer * STEPS + (STEPS + 1)))
                act.wait_ge(st_prompt, value(act, layer * 48 + 48))
                for number, b in enumerate(NORM_ORDER):
                    squares(number, b)
                    if number:
                        high(number - 1, NORM_ORDER[number - 1])
                    log(number, b)
                    if number == 2:
                        act.wait_ge(n_["lo"], value(act, layer * 3 + 2))
                        split_h(layer, 2)
                    exp(number, b)
                high(2, NORM_ORDER[2])

            def save_prompt_states(layer):
                for name, cols, live in (("gdn", 512, gs), ("gla", 256, ls), ("ssd", 512, ss_)):
                    act.dma_start(io["out_p_" + name][bass.ds(layer, 1)].rearrange("a p n -> (a p) n"), live[:, 0:cols]).then_inc(st_prompt, 16)

            def sample_states(kind, layer):
                return ((io[kind + "gdn"][bass.ds(layer, 1)].rearrange("a p b n -> (a p) b n"), states[:, :, :]),
                        (io[kind + "gla"][bass.ds(layer, 1)].rearrange("a p (t e) n -> (a p) t (e n)", e=2), proj[:, LQ:LQ + 4, 0:512]),
                        (io[kind + "ssd"][bass.ds(layer, 1)].rearrange("a p b n -> (a p) b n"), ssd_states))

            def load_states(layer):
                for b in range(3):
                    act.wait_ge((g_, l_, s_)[b]["s"], value(act, layer * STEPS + (CHUNKS + 1)))
                for b, (outside, inside) in enumerate(sample_states("in_", layer)):
                    act.dma_start(inside, outside).then_inc(st_in[b], 16)

            def save_states(layer):
                for b, (outside, inside) in enumerate(sample_states("out_s_", layer)):
                    act.wait_ge((g_, l_, s_)[b]["s"], value(act, layer * STEPS + (STEPS + 1)))
                    act.dma_start(outside, inside).then_inc(st_out, 16)

            def save_conv(layer):
                act.wait_ge(conv_done, value(act, layer * CONV_TILES + CONV_TILES))
                act.dma_start(io["out_p_conv"][bass.ds(layer, 1)].rearrange("a p t c -> (a p) t c"), cs_p[:, :, :]).then_inc(cs_saved, 16)
                act.dma_start(io["out_s_conv"][bass.ds(layer, 1)].rearrange("a p t n -> (a p) t n"),
                              cs_s[:, :, :, :].rearrange("p t b c -> p t (b c)")).then_inc(cs_saved, 16)

            def project(layer):
                def block_in(i, first, j):
                    act.wait_ge(blk_done, value(act, layer * BLOCKS + i * 4 + (B_PROJ + 4 + 4 * first + j + 1 + SPLIT)))

                def by_batch(a):
                    return a.rearrange("p (b s) -> p b s", s=3 + DEC_SEQ)

                def conv_group(i, first, tile, number):
                    def silu(j):
                        act.wait_ge(conv_done, value(act, layer * CONV_TILES + i * 4 + (number + j + 1)))
                        t = bass.ds(i * 4 + (tile + j), 1)
                        act.activation(proj[:, t, 0:SEQ].rearrange("p k t -> p (k t)"), cacc[:, j % 2, 0:SEQ],
                                       ACT.Silu, bias=cb[:, j:j + 1])
                        act.activation(proj[:, t, SEQ:T].rearrange("p k (b s) -> p (k b) s", s=DEC_SEQ),
                                       by_batch(cacc[:, j % 2, 3 + SEQ:PADW])[:, :, 0:DEC_SEQ],
                                       ACT.Silu, bias=cb[:, j:j + 1]).then_inc(csil_done, 1)

                    for j in range(4):
                        block_in(i, first, j)
                        a, b = ps[:, 2 * j, :], ps[:, 2 * j + 1, :]
                        s = by_batch(pad[:, j, 3 + SEQ:PADW])
                        act.activation(pad[:, j, 3:3 + HALF], a[:, 0:HALF], ACT.Copy)
                        act.activation(pad[:, j, 3 + HALF:3 + SEQ], b[:, 0:SEQ - HALF], ACT.Copy)
                        act.activation(s[:, :, 0:3], cs_in[:, bass.ds(i * 4 + (number + j), 1), :, :].rearrange(
                            "p k b c -> p (k b) c"), ACT.Copy)
                        act.activation(s[:, :, 3:], b[:, SEQ - HALF:HALF].rearrange("p (b s) -> p b s", s=DEC_SEQ),
                                       ACT.Copy).then_inc(evict_done, 1)
                        if j:
                            silu(j - 1)
                    silu(3)

                def direct_group(i, first, tile, func):
                    for j in range(4):
                        block_in(i, first, j)
                        act.activation(proj[:, bass.ds(i * 4 + (tile + j), 1), :].rearrange("p k (a t) -> p (k a) t", a=2),
                                       pair(j), func).then_inc(evict_done, 1)

                act.wait_ge(blk_done, value(act, layer * BLOCKS + (B_PROJ + 4 + SPLIT)))
                act.activation(halves(proj[:, SMALL, :]), pair(0), ACT.Copy).then_inc(small_done, 1)
                act.wait_ge(cs_loaded, value(act, layer * 16 + 16))
                act.wait_ge(pad_zero, further(act, layer + 1))
                with act.Fori(0, 3) as i:
                    conv_group(i, 0, GQ, 0)
                with act.Fori(0, 2) as i:
                    direct_group(i, 3, LQ, ACT.Copy)
                narrow_columns(layer)
                with act.Fori(0, 2) as i:
                    conv_group(i, 5, SX, 12)
                save_conv(layer)
                for group, tile in ((7, GZ), (8, LG), (9, SZ)):
                    direct_group(0, group, tile, ACT.Silu)

            def narrow_columns(layer):
                act.preload_act_table_set(LN_EXP)
                act.activation(nega[:, :], prm[:, ALOG:ALOG + 1], ACT.Exp).then_inc(narrow["alog"], 1)
                for want, done, src, dst, func, scale, bias in (
                        ("z", "abs", sp, se, ACT.Abs, 1.0, 0.0), ("abs", "exp", se, se, ACT.Exp, -1.0, 0.0),
                        ("exp", "ln", se, sl, ACT.Ln, 1.0, 1.0)):
                    act.wait_ge(narrow[want], value(act, layer + 1))
                    act.activation(dst[:, :], src[:, :], func, scale=scale, bias=bias).then_inc(narrow[done], 1)
                act.wait_ge(narrow["sp"], value(act, layer * 2 + 2))
                act.activation(cm[32:64, :], sp[32:64, :], ACT.Exp, scale=-1.0).then_inc(narrow["beta"], 1)

            with act.Fori(0, DEPTH) as layer:
                ffn(layer, 0, B_FFN1)
                act.wait_ge(prm_in, value(act, layer * 16 + 16))
                pre_norm(layer, 2, 1)
                act.wait_ge(hl_ready, value(act, layer * (4 * KD) + 2 * KD))
                act.dma_start(cs_in[:, :, :, :].rearrange("p t b c -> p (t b c)"),
                              io["in_conv"][bass.ds(layer, 1)].rearrange("a p n -> (a p) n")).then_inc(cs_loaded, 16)
                project(layer)
                act.preload_act_table_set(LN_EXP)
                with act.Fori(0, CHUNKS) as c:
                    step = prompt_step(layer, c)
                    together(ORDER, common(step), gdn(step), gla(step), ssd(step))
                load_states(layer)
                save_prompt_states(layer)
                step = sample_step(layer)
                together(SAMPLE_ORDER, common(step), gdn(step), gla(step), ssd(step))
                save_states(layer)
                branch_norms(layer)
                with act.Fori(0, KD // 2) as i:
                    for u in range(6):
                        if u == 0:
                            act.wait_ge(bm_ready, value(act, layer * 4 + i + 1))
                        act.wait_ge(blk_done, further(act, layer * BLOCKS + i * 12 + (B_MERGE + 2 * u + 2 + SPLIT)))
                        act.wait_ge(mac_done, further(act, layer * 24 + i * 6 + (u + 1)))
                        act.activation(halves(sg[:, u % 2, :]), pair(2 * u % 4), ACT.Sigmoid,
                                       bias=bm[:, u % 3 * 2 + u // 3:u % 3 * 2 + u // 3 + 1]).then_inc(sg_done, 1)
                        if u % 3 == 2:
                            act.wait_ge(mac_done, value(act, layer * 24 + i * 6 + (u + 3)))
                            act.activation(mh[:, bass.ds(i * 2 + u // 3, 1), :].rearrange("p k t -> p (k t)"),
                                           mac[:, u // 3, :], ACT.Copy).then_inc(mh_done, 1)
                reduce_out(layer, 3, B_OUT, 1)
                ffn(layer, 1, B_FFN2)

        @block.vector
        def _(dve):
            for n, (s, free) in enumerate(((blk_done, SPLIT), (sil_done, 2), (prod_done, 2), (out_done, 2),
                                           (evict_done, 4), (csil_done, 2), (sg_done, 2), (mac_done, 2),
                                           (lo_done, RAW), (x_done, 1), (g_["s"], 1), (l_["s"], 1),
                                           (s_["s"], 1), (g_["oc"], 1), (l_["oc"], 1))):
                dve.memset(cw[:, n:n + 1], 0.0).then_inc(s, free)
            dve.memset(cb[:, 0:1], 0.0).then_inc(s_["yc"], 1)
            dve.memset(cb[:, 1:2], 0.0).then_inc(started, 1)
            dve.wait_ge(loaded, 32)

            def scale(k, wcol):
                return dve.scalar_tensor_tensor(out=hf[:, k, :], in0=x[:, k, :], scalar=prm[:, wcol + k:wcol + k + 1],
                                                in1=rstd[:, :], op0=MULT, op1=MULT)

            def low(layer, number, k):
                dve.wait_ge(hh_ready, value(dve, layer * (4 * KD) + (number * KD + k + 1)))
                dve.tensor_tensor(hl[:, k, :], hf[:, k, :], hh[:, k, :].bitcast(F32), SUB).then_inc(hl_ready, 1)

            def split_in(layer, number, wcol):
                for k in range(KD):
                    scale(k, wcol).then_inc(hf_ready, 1)
                    if k:
                        low(layer, number, k - 1)
                low(layer, number, KD - 1)

            def pre_norm(layer, stage, number, wcol):
                dve.wait_ge(rstd_ready, value(dve, layer * 6 + (stage + 1)))
                dve.wait_ge(x_done, further(dve, layer * (3 * KD) + (stage // 2 * KD + 1)))
                split_in(layer, number, wcol)

            def post_norm(layer, stage, wcol, scale):
                q = stage // 2
                dve.wait_ge(rstd_ready, value(dve, layer * 6 + (stage + 1)))
                for k in range(KD):
                    dve.scalar_tensor_tensor(out=f[:, k, :], in0=f[:, k, :], scalar=prm[:, wcol + k:wcol + k + 1],
                                             in1=rstd_post[:, :], op0=MULT, op1=MULT).then_inc(x_tmp, 1)
                for k in range(KD):
                    dve.wait_ge(x_tmp, value(dve, layer * (3 * KD) + (q * KD + k + 1)))
                    dve.scalar_tensor_tensor(out=x[:, k, :], in0=f[:, k, :], scalar=scale, in1=x[:, k, :],
                                             op0=MULT, op1=ADD).then_inc(x_done, 1)

            def ffn(layer, which, first, wpre, wpost):
                pre_norm(layer, 4 * which, 3 * which, wpre)
                with dve.Fori(0, KF // 2) as i:
                    for j in range(2):
                        n = layer * (2 * KF) + i * 2 + (which * KF + j)
                        dve.wait_ge(blk_done, value(dve, layer * BLOCKS + i * 4 + (first + 2 * j + 2 + SPLIT)))
                        dve.wait_ge(sil_done, further(dve, n + 3))
                        dve.tensor_tensor(halves(prod[:, j, :]), halves(sil[:, j, :]), pair(2 * j + 1), MULT).then_inc(prod_done, 1)
                        dve.wait_ge(prod_done, value(dve, n + 3))
                        dve.wait_ge(ah_done, further(dve, n + 1))
                        m = bass.ds(i * 2 + j, 1)
                        dve.tensor_tensor(al[:, m, :].rearrange("p k t -> p (k t)"), prod[:, j, :],
                                          ah[:, m, :].rearrange("p k t -> p (k t)").bitcast(F32), SUB).then_inc(al_done, 1)
                post_norm(layer, 4 * which + 1, wpost, 0.5)

            def project(layer):
                def conv_group(i, first, number):
                    c0 = layer * CONV_TILES + i * 4 + number
                    dve.wait_ge(csil_done, value(dve, c0 + 2))
                    dve.tensor_copy(cw[:, :], prm[:, bass.ds(i * 16 + (CONVW + 4 * number), 16)])
                    dve.tensor_copy(cb[:, :], prm[:, bass.ds(i * 4 + (CONVB + number), 4)]).then_inc(cw_ready, 1)
                    dve.wait_ge(cw_ready, value(dve, layer * 5 + i + (number // 4 + 1)))
                    for j in range(4):
                        dve.wait_ge(evict_done, value(dve, layer * 40 + i * 4 + (4 * first + j + 5)))
                        dve.wait_ge(csil_done, further(dve, c0 + j + 1))
                        a = cacc[:, j % 2, 0:CW]
                        dve.tensor_scalar(a, pad[:, j, 0:CW], cw[:, 4 * j:4 * j + 1], None, MULT).then_inc(tap, 1)
                        for t in range(1, CONV):
                            dve.wait_ge(tap, value(dve, c0 * 3 + 3 * j + t))
                            last = dve.scalar_tensor_tensor(out=a, in0=pad[:, j, t:t + CW],
                                                            scalar=cw[:, 4 * j + t:4 * j + t + 1], in1=a,
                                                            op0=MULT, op1=ADD)
                            if t < CONV - 1:
                                last.then_inc(tap, 1)
                        tile = bass.ds(i * 4 + (number + j), 1)
                        dve.tensor_copy(cs_p[:, tile, :].rearrange("p k c -> p (k c)"), pad[:, j, SEQ:SEQ + 3])
                        dve.tensor_copy(cs_s[:, tile, :, :].rearrange("p k b c -> p (k b) c"),
                                        pad[:, j, 3 + SEQ:PADW].rearrange("p (b s) -> p b s", s=3 + DEC_SEQ)
                                        [:, :, DEC_SEQ:]).then_inc(conv_done, 1)

                dve.memset(pad[:, :, 0:3], 0.0).then_inc(pad_zero, 1)
                with dve.Fori(0, 3) as i:
                    conv_group(i, 0, 0)
                narrow_columns(layer)
                with dve.Fori(0, 2) as i:
                    conv_group(i, 5, 12)

            def narrow_columns(layer):
                dve.wait_ge(small_done, value(dve, layer + 1))
                dve.wait_ge(narrow["alog"], further(dve, layer + 1))
                dve.tensor_scalar(nega[:, :], nega[:, :], -1.0, None, MULT)
                dve.tensor_scalar(sp[:, :], proj[:, SMALL, :], prm[:, SIGN:SIGN + 1], prm[:, SBIAS:SBIAS + 1],
                                  MULT, ADD).then_inc(narrow["z"], 1)
                dve.wait_ge(narrow["ln"], value(dve, layer + 1))
                dve.scalar_tensor_tensor(out=sp[:, :], in0=sp[:, :], scalar=0.0, in1=sl[:, :], op0=MAX, op1=ADD).then_inc(narrow["sp"], 1)
                dve.wait_ge(narrow["sp"], value(dve, layer * 2 + 1))
                dve.tensor_scalar(cm[:, :], sp[:, :], nega[:, 0:1], None, MULT).then_inc(narrow["sp"], 1)
                dve.wait_ge(narrow["sp"], value(dve, layer * 2 + 2))
                dve.tensor_copy(cm[96:128, :], sp[64:96, :]).then_inc(narrow["dt"], 1)
                dve.wait_ge(narrow["beta"], value(dve, layer + 1))
                dve.wait_ge(narrow["dt"], further(dve, layer + 1))

            def view(a, k):
                return a.rearrange("p (k t) -> p k t", k=k)

            def over(a, k):
                n, m = a.shape
                return a.rearrange("p (k t) -> p k t", k=1).to_broadcast([n, k, m])

            def each(a, m):
                n, k = a.shape
                return a.rearrange("p (k t) -> p k t", t=1).to_broadcast([n, k, m])

            def tri_of(step):
                return tri if step.prompt else cst[0:SAMPLE, TRI_S:TRI_S + SAMPLE]

            def common(step):
                n, o = step.n, step.once
                dve.wait_ge(g_["oc"], value(dve, o + 1))
                dve.wait_ge(g_["s"], further(dve, o + 1))
                if step.prompt:
                    dve.wait_ge(s_["s"], further(dve, o + 1))
                    dve.wait_ge(s_["yc"], further(dve, o + 1))
                dve.tensor_copy(cc[:, 0:n], cm[:, step.cols]).then_inc(both["cc"], 1)
                yield
                yield
                dve.wait_ge(both["br"], value(dve, o + 1))
                dve.wait_ge(both["cc"], further(dve, o + 1))
                dve.tensor_copy(br[32:64, 0:n], cc[32:64, 0:n]).then_inc(g_["brb"], 1)
                yield

            def gdn(step):
                n, o = step.n, step.once
                w = HEADS * n
                dve.wait_ge(g_["rs"], value(dve, o + 1))
                dve.tensor_tensor(view(kn[:, 0:w], 4), proj[:, GK:GK + 4, step.cols], view(rs8[:, w:2 * w], 4), MULT)
                dve.scalar_tensor_tensor(out=view(qn[:, 0:w], 4), in0=proj[:, GQ:GQ + 4, step.cols], scalar=GDN_SCALE,
                                         in1=view(rs8[:, 0:w], 4), op0=MULT, op1=MULT).then_inc(g_["qk"], 1)
                dve.wait_ge(g_["bc"], value(dve, o + 1))
                dve.wait_ge(g_["eg"], further(dve, o + 1))
                dve.wait_ge(g_["qk"], further(dve, o + 1))
                for h in range(HEADS):
                    last = dve.tensor_scalar(dd[0:n, h * n:(h + 1) * n], ps[0:n, 2, h * n:(h + 1) * n],
                                             gc[0:n, ROW_A + h:ROW_A + h + 1], 0.0, SUB, MIN)
                last.then_inc(g_["d"], 1)
                yield
                dve.wait_ge(g_["qk"], value(dve, o + 1))
                dve.tensor_tensor(kg[:, 0:w], kn[:, 0:w], eg[:, 0:w], MULT)
                dve.tensor_tensor(qg[:, 0:w], qn[:, 0:w], eg[:, 0:w], MULT).then_inc(g_["kg"], 1)
                dve.wait_ge(g_["kt"], value(dve, o + 1))
                dve.tensor_tensor(view(kd[0:n, :], 4), view(ps[0:n, 2, :], 4), each(rg[0:n, ROW_A:ROW_A + 4], P), MULT).then_inc(g_["kd"], 1)
                dve.wait_ge(g_["dx"], value(dve, o + 1))
                dve.tensor_tensor(view(dd[0:n, 0:w], 4), view(dd[0:n, 0:w], 4), over(tri_of(step), 4), MULT).then_inc(g_["dm"], 1)
                yield
                dve.wait_ge(g_["kk"], value(dve, o + 1))
                dve.wait_ge(g_["dm"], further(dve, o + 1))
                dve.tensor_tensor(aa[0:n, 0:w], ps[0:n, 0, 0:w], dd[0:n, 0:w], MULT)
                dve.tensor_tensor(att[0:n, 0:w], ps[0:n, 1, 0:w], dd[0:n, 0:w], MULT).then_inc(g_["at"], 1)
                dve.wait_ge(g_["at"], value(dve, o + 1))
                dve.tensor_tensor(aa[0:n, 0:w], ps[0:n, 3, 0:w], aa[0:n, 0:w], MULT).then_inc(g_["atb"], 1)
                dve.wait_ge(g_["atb"], value(dve, o + 1))

                def level(l):
                    m = cst[0:n, MASK + l * P:MASK + l * P + n]
                    return dve.tensor_tensor(view(al_[0:n, 0:w], 4), view(aa[0:n, 0:w], 4), over(m, 4), MULT)

                def rest():
                    dve.wait_ge(g_["sk"], value(dve, o + 1))
                    dve.tensor_tensor(view(rt[:, 0:w], 4), proj[:, GV:GV + 4, step.cols], view(ps[:, 3, 0:w], 4), SUB).then_inc(g_["rt"], 1)

                level(0).then_inc(g_["al"], 1)
                dve.wait_ge(g_["al"], value(dve, step.level + 1))
                dve.tensor_tensor(view(xt[0:n, 0:w], 4), over(ident[0:n, 0:n], 4), view(al_[0:n, 0:w], 4), SUB).then_inc(g_["x"], 1)
                dve.wait_ge(g_["x"], value(dve, step.level + 1))
                level(1).then_inc(g_["al"], 1)
                yield
                if step.prompt:
                    rest()
                yield
                for l in range(step.levels - 1):
                    dve.wait_ge(g_["p"], value(dve, step.solve + l + 1))
                    if l < step.levels - 2:
                        level(l + 2).then_inc(g_["al"], 1)
                    yield
                    if l < step.levels - 2:
                        dve.wait_ge(g_["qx"], value(dve, step.inner + l + 1))
                        if l:
                            dve.wait_ge(g_["xx"], further(dve, step.inner + l))
                        else:
                            dve.wait_ge(g_["xi"], further(dve, o + 1))
                        dve.tensor_tensor(xx[0:n, 0:w], xx[0:n, 0:w], ps[0:n, 1, 0:w], SUB).then_inc(g_["xx"], 1)
                    dve.wait_ge(g_["q"], value(dve, step.solve + l + 1))
                    dve.wait_ge(g_["x"], further(dve, step.level + l + 1))
                    dve.tensor_tensor(xt[0:n, 0:w], xt[0:n, 0:w], ps[0:n, 2, 0:w], SUB).then_inc(g_["x"], 1)
                    if l == step.levels - 2:
                        dve.wait_ge(g_["x"], value(dve, step.level + step.levels))
                        dve.tensor_tensor(view(xt[0:n, 0:w], 4), view(xt[0:n, 0:w], 4), each(tm[0:n, ROW_B:ROW_B + 4], n), MULT).then_inc(g_["tb"], 1)
                    yield
                if step.prompt:
                    dve.wait_ge(g_["su"], value(dve, step.update + 1))
                    for h in range(HEADS):
                        s = gs[:, h * P:(h + 1) * P]
                        last = dve.scalar_tensor_tensor(out=s, in0=s, scalar=eg[:, h * n + n - 1:h * n + n],
                                                        in1=ps[:, 3, h * P:(h + 1) * P], op0=MULT, op1=ADD)
                    last.then_inc(g_["s"], 1)
                    yield
                else:
                    for h in range(HEADS):
                        yield
                    rest()
                    yield
                    yield
                    yield
                    yield

                    def add(h):
                        dve.wait_ge(g_["su"], value(dve, step.update + h + 1))
                        dve.wait_ge(g_["sm"], further(dve, step.layer * HEADS + h + 1))
                        s = states[:, :, h * P:(h + 1) * P]
                        return dve.tensor_tensor(s, s, ps[:, 0:2, :].rearrange("p a (b m) -> p (a b) m", m=P), ADD)

                    dve.wait_ge(g_["u"], value(dve, o + 1))
                    dve.wait_ge(g_["o"], further(dve, o + 1))
                    for h in range(HEADS):
                        if h:
                            add(h - 1)
                        dve.tensor_tensor(view(uexp[0:n, :], 8), over(uu[0:n, h * P:(h + 1) * P], 8),
                                          each(cst[0:n, BMASK:BMASK + 8], P), MULT).then_inc(g_["ue"], 1)
                        s = states[:, :, h * P:(h + 1) * P]
                        dve.tensor_tensor(s, s, each(eg[:, h * n + 3:(h + 1) * n:4], P), MULT).then_inc(g_["sm"], 1)
                        if h == HEADS - 1:
                            add(h).then_inc(g_["s"], 1)
                        yield

            def gla(step):
                n, o = step.n, step.once
                L = gla_prompt if step.prompt else gla_sample
                w = 2 * n
                dve.wait_ge(l_["oc"], value(dve, o + 1))
                dve.wait_ge(l_["s"], further(dve, o + 1))
                if not step.prompt:
                    dve.wait_ge(s_["s"], further(dve, o + 1))
                dve.tensor_copy(L["rc"][96:128, 0:n], proj[96:128, SMALL, step.cols]).then_inc(l_["rc"], 1)
                dve.tensor_copy(view(L["vc"][:, 0:4 * n], 4), proj[:, LV:LV + 4, step.cols]).then_inc(l_["vc"], 1)
                dve.memset(L["att"][0:n, 0:4 * n], 0.0)
                dve.wait_ge(l_["z"], value(dve, o + 1))
                dve.tensor_tensor(L["z"][0:n, :], ps[0:n, 4, 0:256], prm[0:n, GLAB:GLAB + 256], ADD).then_inc(l_["zt"], 1)
                dve.tensor_scalar(view(L["qs"][:, 0:w], 2), proj[:, LQ:LQ + 2, step.cols], GLA_SCALE, None, MULT)
                dve.tensor_copy(view(L["ks"][:, 0:w], 2), proj[:, LK:LK + 2, step.cols]).then_inc(l_["qk"], 1)
                yield
                dve.wait_ge(l_["a3"], value(dve, o + 1))
                dve.wait_ge(l_["zt"], further(dve, o + 1))
                dve.scalar_tensor_tensor(out=L["gk"][0:n, :], in0=L["z"][0:n, :], scalar=0.0, in1=L["a"][0:n, :], op0=MIN, op1=SUB).then_inc(l_["g1"], 1)
                dve.wait_ge(l_["g1"], value(dve, o + 1))
                dve.tensor_scalar(L["gk"][0:n, :], L["gk"][0:n, :], 1.0 / GLA_NORMALIZER, None, MULT).then_inc(l_["gk"], 1)
                yield
                dve.wait_ge(l_["bt"], value(dve, o + 1))
                dve.wait_ge(l_["qk"], further(dve, o + 1))
                dve.tensor_tensor(L["qe"][:, 0:w], L["qs"][:, 0:w], L["eb"][:, 0:w], MULT)
                dve.tensor_tensor(L["kd"][:, 0:w], L["ks"][:, 0:w], L["er"][:, 0:w], MULT).then_inc(l_["qe"], 1)
                yield

                def by_block(a, m):
                    return a.rearrange("p (b s) -> p b s", s=2 * m)

                for l in range(step.levels):
                    m = 1 << l
                    b = by_block(L["bt"][:, 0:w], m)
                    last = dve.tensor_tensor(by_block(L["dl"][:, l, 0:w], m), b,
                                             b[:, :, m:m + 1].to_broadcast([P, w // (2 * m), 2 * m]), SUB)
                last.then_inc(l_["dl"], 1)
                yield
                dve.wait_ge(l_["d2"], value(dve, o + 1))
                for l in range(step.levels):
                    m = 1 << l
                    d = by_block(L["dl"][:, l, 0:w], m)
                    dve.tensor_tensor(d[:, :, 0:m], by_block(L["ks"][:, 0:w], m)[:, :, 0:m], d[:, :, 0:m], MULT)
                    last = dve.tensor_tensor(d[:, :, m:], by_block(L["qs"][:, 0:w], m)[:, :, m:], d[:, :, m:], MULT)
                last.then_inc(l_["ml"], 1)
                yield
                for l in range(step.levels + 1):
                    dve.wait_ge(l_["at"], value(dve, step.score + l + 1))
                    if l:
                        dve.wait_ge(l_["cp"], further(dve, step.score + l))
                    c = MASK + l * P if l < step.levels else IDENT
                    for e in range(2):
                        last = dve.copy_predicated(view(L["att"][0:n, e * w:(e + 1) * w], 2), over(cst[0:n, c:c + n], 2).bitcast(U32),
                                                   view(ps[0:n, 4 + e, 0:w], 2))
                    last.then_inc(l_["cp"], 1)
                    yield
                for h in range(1 if step.prompt else HEADS):
                    yield
                if step.prompt:
                    dve.wait_ge(l_["su"], value(dve, step.update + 1))
                    for g in range(2):
                        s = ls[:, g * P:(g + 1) * P]
                        last = dve.scalar_tensor_tensor(out=s, in0=s, scalar=L["eb"][:, g * n + n - 1:g * n + n],
                                                        in1=ps[:, 4, g * P:(g + 1) * P], op0=MULT, op1=ADD)
                    last.then_inc(l_["s"], 1)
                    yield
                else:
                    def heads_states(h):
                        r, g = slice(64 * (h % 2), 64 * (h % 2) + 64), h // 2
                        return gla_states[r, :, :, g * P:(g + 1) * P]

                    def add(h):
                        dve.wait_ge(l_["su"], value(dve, step.update + h + 1))
                        dve.wait_ge(l_["sm"], further(dve, step.layer * HEADS + h + 1))
                        s, r = heads_states(h), slice(64 * (h % 2), 64 * (h % 2) + 64)
                        return dve.tensor_tensor(s, s, ps[r, 4:6, :].rearrange("p a (t e m) -> p (a t) e m", e=2, m=P), ADD)

                    dve.wait_ge(l_["vt"], value(dve, o + 1))
                    dve.wait_ge(l_["o"], further(dve, o + 1))
                    for h in range(HEADS):
                        if h:
                            add(h - 1)
                        r, g = slice(64 * (h % 2), 64 * (h % 2) + 64), h // 2
                        dve.tensor_tensor(vexp[0:n, :, :], over(L["vt"][0:n, h * P:(h + 1) * P], 8),
                                          each(cst[0:n, BMASK:BMASK + 8], P), MULT).then_inc(l_["ve"], 1)
                        s = heads_states(h)
                        decay = L["eb"][r, g * n + 3:(g + 1) * n:4].rearrange("p (t e o) -> p t e o", e=2, o=1)
                        dve.tensor_tensor(s, s, decay.to_broadcast([64, 4, 2, P]), MULT).then_inc(l_["sm"], 1)
                        if h == HEADS - 1:
                            add(h).then_inc(l_["s"], 1)
                        yield

            def ssd(step):
                n, o = step.n, step.once
                S = ssd_prompt if step.prompt else ssd_sample
                w = SSD_HEADS * n
                dve.wait_ge(s_["bc"], value(dve, o + 1))
                dve.wait_ge(s_["ea"], further(dve, o + 1))
                for h in range(SSD_HEADS):
                    last = dve.tensor_scalar(S["dd"][0:n, h * n:(h + 1) * n], ps[0:n, 6 + h // 4, h % 4 * n:(h % 4 + 1) * n],
                                             gc[0:n, ROW_DT + h:ROW_DT + h + 1], 0.0, SUB, MIN)
                last.then_inc(s_["d"], 1)
                yield
                dve.wait_ge(s_["st"], value(dve, o + 1))
                for g in range(2):
                    c = slice(4 * g * n, 4 * (g + 1) * n)
                    last = dve.tensor_tensor(view(S["ce"][:, c], 4), view(S["ea"][:, c], 4), over(S["xbc"][:, (6 + g) * n:(7 + g) * n], 4), MULT)
                last.then_inc(s_["ce"], 1)
                yield
                dve.wait_ge(s_["tr"], value(dve, o + 1))
                dve.tensor_tensor(view(S["xd"][0:n, :], 8), view(ps[0:n, 6, :], 8), each(tm[0:n, 96:104], 64), MULT).then_inc(s_["xd"], 1)
                dve.wait_ge(s_["dx"], value(dve, o + 1))
                dve.tensor_tensor(view(S["dd"][0:n, 0:w], 8), view(S["dd"][0:n, 0:w], 8), over(tri_of(step), 8), MULT).then_inc(s_["dm"], 1)
                dve.wait_ge(s_["xd"], value(dve, o + 1))
                dve.wait_ge(both["rg"], further(dve, o + 1))
                dve.tensor_tensor(view(S["xe"][0:n, :], 8), view(S["xd"][0:n, :], 8), each(rg[0:n, ROW_DT:ROW_DT + 8], 64), MULT).then_inc(s_["xe"], 1)
                dve.wait_ge(s_["dm"], value(dve, o + 1))
                dve.wait_ge(s_["bt"], further(dve, o + 1))
                for g in range(2):
                    c = slice(4 * g * n, 4 * (g + 1) * n)
                    last = dve.tensor_tensor(view(S["dd"][0:n, c], 4), view(S["dd"][0:n, c], 4), over(ps[0:n, 7, g * n:(g + 1) * n], 4), MULT)
                last.then_inc(s_["att"], 1)
                yield
                for h in range(0 if step.prompt else 3):
                    yield
                dve.wait_ge(s_["y"], value(dve, o + 1))
                for t in range(4):
                    last = dve.scalar_tensor_tensor(out=proj[:, SX + t, step.cols], in0=S["xbc"][:, t * n:(t + 1) * n],
                                                    scalar=prm[:, SSDD + t:SSDD + t + 1],
                                                    in1=ps[:, 6, t * n:(t + 1) * n], op0=MULT, op1=ADD)
                last.then_inc(s_["yc"], 1)
                yield
                if step.prompt:
                    dve.tensor_tensor(view(ss_[:, :], 8), view(ss_[:, :], 8), each(S["ea"][:, n - 1:w:n], 64), MULT).then_inc(s_["sm"], 1)
                    dve.wait_ge(s_["su"], value(dve, step.update2 + 1))
                    dve.wait_ge(s_["sm"], further(dve, step.layer * (CHUNKS + 2) + step.c + 1))
                    dve.tensor_tensor(ss_[:, :], ss_[:, :], ps[:, 7, :], ADD).then_inc(s_["s"], 1)
                else:
                    for g in range(2):
                        dve.tensor_tensor(view(xexp[0:n, :], 8), over(S["xe"][0:n, g * 256:(g + 1) * 256], 8),
                                          each(cst[0:n, BMASK:BMASK + 8], 256), MULT).then_inc(s_["xe2"], 1)
                        for h in range(4 * g, 4 * g + 4):
                            s = ssd_states[:, :, h * 64:(h + 1) * 64]
                            last = dve.tensor_tensor(s, s, each(S["ea"][:, h * n + 3:(h + 1) * n:4], 64), MULT)
                        last.then_inc(s_["sm"], 1)
                        dve.wait_ge(s_["sm"], value(dve, step.layer * (CHUNKS + 2) + (CHUNKS + g + 1)))
                        for half in range(2):
                            dve.wait_ge(s_["su"], value(dve, step.update2 + 2 * g + half + 1))
                            s = ssd_states[:, 4 * half:4 * half + 4, g * 256:(g + 1) * 256]
                            dve.tensor_tensor(s, s, ps[:, 6:8, :].rearrange("p a (b m) -> p (a b) m", m=256), ADD).then_inc(
                                s_["s"] if g and half else s_["sa"], 1)
                        if g == 0:
                            yield
                yield
                yield

            def branch_norm(layer, b):
                if b == 2:
                    dve.wait_ge(s_["yc"], value(dve, layer * STEPS + (STEPS + 1)))
                    y = proj[:, SX:SX + 4, :]
                    dve.tensor_tensor(y, y, proj[:, SZ:SZ + 4, :], MULT).then_inc(n_["yz"], 1)
                    dve.wait_ge(n_["yz"], value(dve, layer + 1))
                number = NORM_ORDER.index(b)
                o, rs = layer * 3 + number, nrs[number]
                dve.wait_ge(n_["rs"], further(dve, o + 1))
                if b < 2:
                    c = (GDNN, GLAN)[b]
                    v = (GV, LV)[b]
                    for t in range(4):
                        last = dve.scalar_tensor_tensor(out=nt[number][:, t, :], in0=proj[:, v + t, :], scalar=prm[:, c:c + 1],
                                                        in1=rs[:, t, :], op0=MULT, op1=MULT)
                    last.then_inc(n_["t"], 1)
                    dve.wait_ge(n_["t"], value(dve, layer * 2 + b + 1))
                    z = (GZ, LG)[b]
                    dve.tensor_tensor(nt[number][:, :, :], nt[number][:, :, :], proj[:, z:z + 4, :], MULT).then_inc(n_["tz"], 1)
                else:
                    for t in range(4):
                        last = dve.scalar_tensor_tensor(out=nt[number][:, t, :], in0=proj[:, SX + t, :],
                                                        scalar=prm[:, SSDN + t:SSDN + t + 1],
                                                        in1=rs[:, t // 2, :], op0=MULT, op1=MULT)
                    last.then_inc(n_["tz"], 1)
                dve.wait_ge(n_["hi"], value(dve, o + 1))
                dve.wait_ge(n_["tz"], further(dve, o + 1))
                dve.tensor_tensor(ol[b][:, :, :], nt[number][:, :, :], oh[b][:, :, :].bitcast(F32), SUB).then_inc(n_["lo"], 1)
                dve.wait_ge(n_["lo"], value(dve, o + 1))

            with dve.Fori(0, DEPTH) as layer:
                dve.wait_ge(prm_in, value(dve, layer * 16 + 16))
                ffn(layer, 0, B_FFN1, F1PRE, F1POST)
                pre_norm(layer, 2, 1, MPRE)
                project(layer)
                dve.wait_ge(evict_done, value(dve, layer * 40 + 44))
                dve.wait_ge(cs_saved, value(dve, layer * 32 + 32))
                for state in (gs, ls, ss_):
                    dve.memset(state[:, :], 0.0).then_inc(zeroed, 1)
                with dve.Fori(0, CHUNKS) as c:
                    step = prompt_step(layer, c)
                    together(ORDER, common(step), gdn(step), gla(step), ssd(step))
                step = sample_step(layer)
                together(SAMPLE_ORDER, common(step), gdn(step), gla(step), ssd(step))
                for branch in NORM_ORDER[:2]:
                    branch_norm(layer, branch)
                dve.wait_ge(st_out, value(dve, layer * 48 + 48))
                split_in(layer, 2, MPRE)
                branch_norm(layer, NORM_ORDER[2])
                with dve.Fori(0, KD // 2) as i:
                    dve.wait_ge(sg_done, value(dve, layer * 24 + i * 6 + 2))
                    dve.tensor_copy(bm[:, :].rearrange("p (r k) -> p r k", k=2),
                                    prm[:, BMERGE:BMERGE + 24].rearrange("p (r m) -> p r m", m=8)
                                    [:, :, bass.ds(i * 2, 2)]).then_inc(bm_ready, 1)
                    for u in range(6):
                        r, k = u % 3, u // 3
                        dve.wait_ge(blk_done, value(dve, layer * BLOCKS + i * 12 + (B_MERGE + 2 * u + 2 + SPLIT)))
                        dve.wait_ge(sg_done, further(dve, layer * 24 + i * 6 + (u + 3)))
                        dve.wait_ge(mac_done, further(dve, layer * 24 + i * 6 + (u + 2)))
                        dst = mac[:, k, :] if r == 0 else mt_[:, 0, :]
                        last = dve.tensor_tensor(halves(dst), halves(sg[:, u % 2, :]), pair((2 * u + 1) % 4), MULT)
                        if r:
                            last.then_inc(mac_tmp, 1)
                            dve.wait_ge(mac_tmp, value(dve, layer * 16 + i * 4 + (2 * k + r)))
                            last = dve.tensor_tensor(mac[:, k, :], mac[:, k, :], mt_[:, 0, :], ADD)
                        last.then_inc(mac_done, 1)
                        if r == 2:
                            dve.wait_ge(mac_done, value(dve, layer * 24 + i * 6 + (u + 3)))
                            dve.wait_ge(mh_done, further(dve, layer * KD + i * 2 + (k + 1)))
                            m = bass.ds(i * 2 + k, 1)
                            dve.tensor_tensor(ml[:, m, :].rearrange("p k t -> p (k t)"), mac[:, k, :],
                                              mh[:, m, :].rearrange("p k t -> p (k t)").bitcast(F32), SUB).then_inc(ml_done, 1)
                post_norm(layer, 3, MPOST, 1.0)
                ffn(layer, 1, B_FFN2, F2PRE, F2POST)


COLS = dict(qkv=0, z=1536, a=2048, b=2052, q=2056, r=3592, sz=3608, dt=5144, gate=5152)


def tiles(w):
    w = np.asarray(w)
    n, k, m = w.shape
    return np.ascontiguousarray(w.reshape(n, k // P, P, m // P, P).transpose(0, 3, 2, 1, 4).reshape(n * m // P, P, k))


def pack(a):
    a = {k: np.asarray(v) for k, v in a.items()}
    out = {}
    tokens = np.concatenate([a["x_prompt"].reshape(SEQ, D_MODEL), a["x_sample"].reshape(SAMPLE, D_MODEL)])
    out["x"] = tokens.T.reshape(KD, P, T).transpose(1, 0, 2).reshape(P, KD * T)

    ups, downs = [], []
    for l in range(DEPTH):
        for f in ("ffn1", "ffn2"):
            g, u = tiles(a[f + "_w_gate"][l:l + 1]), tiles(a[f + "_w_up"][l:l + 1])
            ups.append(np.stack([g, u], 1).reshape(UPS, P, D_MODEL))
            downs.append(tiles(a[f + "_w_down"][l:l + 1]))
    out["up"], out["down"] = np.concatenate(ups), np.concatenate(downs)
    w = a["w_in"]
    wide = np.concatenate([w[:, :, COLS["qkv"]:COLS["a"]], w[:, :, COLS["q"]:COLS["r"]], w[:, :, COLS["sz"]:COLS["dt"]]], 2)
    order = [*range(GQ, GZ), *range(LQ, LG), *range(SX, SMALL), *range(GZ, LQ), *range(LG, SX)]
    out["win"] = tiles(wide).reshape(DEPTH, 40, P, D_MODEL)[:, order].reshape(DEPTH * 40, P, D_MODEL)
    small = np.zeros((DEPTH, D_MODEL, P), w.dtype)
    small[:, :, ROW_A:ROW_A + 4] = w[:, :, COLS["a"]:COLS["a"] + 4]
    small[:, :, ROW_B:ROW_B + 4] = w[:, :, COLS["b"]:COLS["b"] + 4]
    small[:, :, ROW_DT:ROW_DT + 8] = w[:, :, COLS["dt"]:COLS["dt"] + 8]
    small[:, :, ROW_R:ROW_R + 16] = w[:, :, COLS["r"]:COLS["r"] + 16]
    out["narrow"] = tiles(small)
    gate = tiles(w[:, :, COLS["gate"]:]).reshape(DEPTH, 3, KD, P, D_MODEL)
    gate = gate.transpose(0, 2, 1, 3, 4).reshape(DEPTH * 24, P, D_MODEL)
    br = np.stack([tiles(a["w_br_" + s]).reshape(DEPTH, KD, P, 512) for s in ("gdn", "gla", "ssd")], 2)
    merge = np.concatenate([gate, br.reshape(DEPTH * 24, P, 512)], 2).reshape(DEPTH * 24, P, 2, 6 * P)
    out["merge"] = merge.transpose(0, 2, 1, 3).reshape(DEPTH * 48, P, 6 * P)
    out["wout"] = tiles(a["w_out"])

    prm = np.zeros((DEPTH, P, NPRM), np.float32)

    def cols(c, v):
        v = v.reshape(DEPTH, -1, P)
        prm[:, :, c:c + v.shape[1]] = v.transpose(0, 2, 1)

    for c, s in ((F1PRE, "ffn1_norm_pre"), (F1POST, "ffn1_norm_post"), (MPRE, "mix_norm_pre"), (MPOST, "mix_norm_post"),
                 (F2PRE, "ffn2_norm_pre"), (F2POST, "ffn2_norm_post"), (BMERGE, "b_merge"), (GDNN, "gdn_norm"),
                 (GLAN, "gla_norm"), (SSDN, "ssd_norm")):
        cols(c, a[s])
    conv = np.concatenate([a["gdn_conv_w"], a["ssd_conv_w"]], 1).reshape(DEPTH, CONV_TILES, P, CONV)
    prm[:, :, CONVW:CONVW + 80] = conv.transpose(0, 2, 1, 3).reshape(DEPTH, P, 80)
    cols(CONVB + 12, a["ssd_conv_b"])
    cols(SSDD, np.repeat(a["ssd_D"], 64, axis=1))
    prm[:, ROW_A:ROW_A + 4, SBIAS] = a["gdn_dt_bias"]
    prm[:, ROW_DT:ROW_DT + 8, SBIAS] = a["ssd_dt_bias"]
    prm[:, ROW_A:ROW_A + 4, ALOG] = a["gdn_A_log"]
    prm[:, ROW_DT:ROW_DT + 8, ALOG] = a["ssd_A_log"]
    prm[:, :, SIGN] = 1.0
    prm[:, ROW_B:ROW_B + 32, SIGN] = -1.0
    prm[:, :, GLAB:GLAB + 256] = a["gla_gate_bias"][:, None, :]
    prm[:, ROW_R:ROW_R + 16, GUP:GUP + 256] = a["gla_gate_up"]
    out["prm"] = prm

    cst = np.zeros((P, NCONST), np.float32)
    j, i = np.meshgrid(np.arange(P), np.arange(P), indexing="ij")
    cst[:, IDENT:IDENT + P] = j == i
    cst[:, TRI:TRI + P] = i >= j
    cst[:, REV:REV + P] = j > i
    for l in range(LEVELS):
        m = 1 << l
        cst[:, MASK + l * P:MASK + (l + 1) * P] = (j // (2 * m) == i // (2 * m)) & (j % (2 * m) < m) & (i % (2 * m) >= m)
    cst[:, ONES:ONES + P] = 1.0
    n = SAMPLE
    same = (j // DEC_SEQ == i // DEC_SEQ)[:n, :n]
    cst[:n, TRI_S:TRI_S + n] = same & (i >= j)[:n, :n]
    cst[:n, REV_S:REV_S + n] = same & (j > i)[:n, :n]
    cst[:n, BMASK:BMASK + 8] = np.arange(n)[:, None] // DEC_SEQ == np.arange(8)[None, :]
    cst[:, EPSC] = EPS
    cst[:, EPSROW] = EPS * D_MODEL / P
    out["cst"] = cst

    cs = np.concatenate([a["state_gdn_conv"], a["state_ssd_conv"]], 3)
    cs = cs.reshape(DEPTH, DEC_BATCH, 3, CONV_TILES, P).transpose(0, 4, 3, 1, 2)
    out["in_conv"] = cs.reshape(DEPTH, P, CONV_TILES * DEC_BATCH * 3)
    out["in_gdn"] = a["state_gdn"].transpose(0, 3, 1, 2, 4).reshape(DEPTH, P, DEC_BATCH, 512)
    gla = a["state_gla"].reshape(DEPTH, DEC_BATCH, 2, 2, 64, P)
    out["in_gla"] = gla.transpose(0, 3, 4, 1, 2, 5).reshape(DEPTH, P, DEC_BATCH, 256)
    out["in_ssd"] = a["state_ssd"].transpose(0, 4, 1, 2, 3).reshape(DEPTH, P, DEC_BATCH, 512)
    return {k: np.ascontiguousarray(v) for k, v in out.items()}


OUTS = {
    "y": (P, KD * T),
    "out_p_conv": (DEPTH, P, CONV_TILES, 3), "out_s_conv": (DEPTH, P, CONV_TILES, DEC_BATCH * 3),
    "out_p_gdn": (DEPTH, P, 512), "out_p_gla": (DEPTH, P, 256), "out_p_ssd": (DEPTH, P, 512),
    "out_s_gdn": (DEPTH, P, DEC_BATCH, 512), "out_s_gla": (DEPTH, P, DEC_BATCH, 256), "out_s_ssd": (DEPTH, P, DEC_BATCH, 512),
}


def unpack(r):
    y = r["y"].reshape(P, KD, T).transpose(2, 1, 0).reshape(T, D_MODEL)
    outs = [y[:SEQ].reshape(1, SEQ, D_MODEL), y[SEQ:].reshape(DEC_BATCH, DEC_SEQ, D_MODEL)]
    for k, nb in (("p", 1), ("s", DEC_BATCH)):
        conv = r[f"out_{k}_conv"].reshape(DEPTH, P, CONV_TILES, nb, 3).transpose(0, 3, 4, 2, 1).reshape(DEPTH, nb, 3, CONV_TILES * P)
        gdn = r[f"out_{k}_gdn"].reshape(DEPTH, P, nb, HEADS, P).transpose(0, 2, 3, 1, 4)
        gla = r[f"out_{k}_gla"].reshape(DEPTH, 2, 64, nb, 2, P).transpose(0, 3, 4, 1, 2, 5).reshape(DEPTH, nb, HEADS, 64, P)
        ssd = r[f"out_{k}_ssd"].reshape(DEPTH, P, nb, SSD_HEADS, 64).transpose(0, 2, 3, 4, 1)
        outs += [conv[..., :12 * P], gdn, gla, conv[..., 12 * P:], ssd]
    return tuple(np.ascontiguousarray(o) for o in outs)


def kernel(**inputs):
    import concourse.bacc as bacc
    from concourse.bass_utils import run_bass_kernel_spmd

    arrays = pack(inputs)
    nc = bacc.Bacc("TRN2", target_bir_lowering=False, num_devices=1)
    io = {k: nc.dram_tensor("in_" + k, v.shape, mybir.dt.from_np(v.dtype), kind="ExternalInput").ap() for k, v in arrays.items()}
    for k, shape in OUTS.items():
        io[k] = nc.dram_tensor("res_" + k, shape, F32, kind="ExternalOutput").ap()
    trunk(nc, io)
    r = run_bass_kernel_spmd(nc, [{"in_" + k: v for k, v in arrays.items()}], core_ids=[0])
    return unpack({k: r.results[0]["res_" + k] for k in OUTS})
```
